# Optimizing a Trainium2 kernel written in Bass

```python
import jax, jax.numpy as jnp
from jax import lax
import numpy as np

D_MODEL = 1024
BATCH = 1
SEQ = 512
DEPTH = 2
DEC_BATCH = 8
DEC_SEQ = 1
PAST_LEN = 1024
PAGE_SIZE = 128

N_HEADS = 16
HEAD_DIM = D_MODEL // N_HEADS
N_KV_HEADS = 4
GROUP = N_HEADS // N_KV_HEADS
ROPE_FRACTION = 4
ROPE_THETA = 500000.0
N_IDX_HEADS = 8
IDX_DIM = 64
TOPK_MAX = 256
D_FF = 2816
CONV_W = 3
Q_BLOCK = 128
N_MIXERS = 2
N_A_LAYERS = (DEPTH + 1) // 2
N_B_LAYERS = DEPTH // 2
EPS = 1e-6
FORGET_BIAS_MEAN = 4.0
QKV_COLS = (N_HEADS + 2 * N_KV_HEADS) * HEAD_DIM
IN_A_COLS = QKV_COLS + N_IDX_HEADS * IDX_DIM + IDX_DIM + N_IDX_HEADS
IN_B_COLS = QKV_COLS + N_HEADS
A_SPLITS = (N_HEADS * HEAD_DIM, (N_HEADS + N_KV_HEADS) * HEAD_DIM, QKV_COLS,
            QKV_COLS + N_IDX_HEADS * IDX_DIM, QKV_COLS + N_IDX_HEADS * IDX_DIM + IDX_DIM)
B_SPLITS = (N_HEADS * HEAD_DIM, (N_HEADS + N_KV_HEADS) * HEAD_DIM, QKV_COLS)

kernel_name = 'hybrid_dsa_fox_convffn_adaln_step'

def rmsnorm(x, g):
    xf = x.astype(jnp.float32)
    y = xf * lax.rsqrt(jnp.mean(xf * xf, axis=-1, keepdims=True) + EPS)
    return (y * g.astype(jnp.float32)).astype(x.dtype)

def adaln(c, w, b):
    m = jax.nn.silu(c) @ w + b
    return jnp.split(m[:, None, :], 6, axis=-1)

def modulate(h, shift, scale):
    return h * (1 + scale) + shift

def rope_partial(x, pos):
    rd = x.shape[-1] // ROPE_FRACTION
    half = rd // 2
    inv_freq = ROPE_THETA ** (-jnp.arange(half, dtype=jnp.float32) / half)
    ang = pos.astype(jnp.float32)[:, None] * inv_freq[None, :]
    cos = jnp.cos(ang)[:, None, :]
    sin = jnp.sin(ang)[:, None, :]
    xf = x.astype(jnp.float32)
    x1, x2 = xf[..., :half], xf[..., half:rd]
    rot = jnp.concatenate([x1 * cos - x2 * sin, x1 * sin + x2 * cos], axis=-1).astype(x.dtype)
    return jnp.concatenate([rot, x[..., rd:]], axis=-1)

def paged_past(cache, layer, page_table):
    g = cache[layer, page_table]
    return g.reshape((g.shape[0], g.shape[1] * g.shape[2]) + g.shape[3:])

def dsa_project(h, w_in, pos):
    B, T, _ = h.shape
    q, k, v, iq, ik, iw = jnp.split(h @ w_in, A_SPLITS, axis=-1)
    q = rope_partial(q.reshape(B, T, N_HEADS, HEAD_DIM), pos)
    k = rope_partial(k.reshape(B, T, N_KV_HEADS, HEAD_DIM), pos)
    v = v.reshape(B, T, N_KV_HEADS, HEAD_DIM)
    iq = rope_partial(iq.reshape(B, T, N_IDX_HEADS, IDX_DIM), pos)
    ik = rope_partial(ik.reshape(B, T, 1, IDX_DIM), pos)[:, :, 0]
    return q, k, v, iq, ik, iw

def dsa_attend(q, iq, iw, qpos, k, v, ik, kpos, n_sel):
    B, Tq = q.shape[:2]
    f32 = jnp.float32
    dots = jnp.einsum('bqhd,bsd->bqhs', iq.astype(f32), ik.astype(f32))
    score = jnp.einsum('bqhs,bqh->bqs', jax.nn.relu(dots), iw.astype(f32))
    causal = kpos[None, :] <= qpos[:, None]
    score = jnp.where(causal[None], score, -jnp.inf)
    top_score, idx = lax.top_k(score, n_sel)
    valid = jnp.isfinite(top_score)
    ks = jax.vmap(lambda a, i: a[i])(k, idx)
    vs = jax.vmap(lambda a, i: a[i])(v, idx)
    qg = q.reshape(B, Tq, N_KV_HEADS, GROUP, HEAD_DIM).astype(f32)
    logits = jnp.einsum('bqkgd,bqnkd->bqkgn', qg, ks.astype(f32)) * (HEAD_DIM ** -0.5)
    logits = jnp.where(valid[:, :, None, None, :], logits, -jnp.inf)
    p = jax.nn.softmax(logits, axis=-1)
    o = jnp.einsum('bqkgn,bqnkd->bqkgd', p.astype(vs.dtype), vs)
    return o.reshape(B, Tq, N_HEADS * HEAD_DIM)

def dsa_prompt(h, w_in, w_o):
    B, T, _ = h.shape
    pos = jnp.arange(T)
    q, k, v, iq, ik, iw = dsa_project(h, w_in, pos)
    n_sel = min(TOPK_MAX, T // 4)

    def block(start):
        sl = lambda a: lax.dynamic_slice_in_dim(a, start, Q_BLOCK, axis=1)
        qpos = start + jnp.arange(Q_BLOCK)
        return dsa_attend(sl(q), sl(iq), sl(iw), qpos, k, v, ik, pos, n_sel)

    o = lax.map(block, jnp.arange(0, T, Q_BLOCK))
    o = jnp.swapaxes(o, 0, 1).reshape(B, T, N_HEADS * HEAD_DIM)
    return o @ w_o, k, v, ik

def dsa_sample(h, w_in, w_o, k_past, v_past, ik_past):
    B, T, _ = h.shape
    qpos = PAST_LEN + jnp.arange(T)
    q, k, v, iq, ik, iw = dsa_project(h, w_in, qpos)
    k_all = jnp.concatenate([k_past.astype(k.dtype), k], axis=1)
    v_all = jnp.concatenate([v_past.astype(v.dtype), v], axis=1)
    ik_all = jnp.concatenate([ik_past.astype(ik.dtype), ik], axis=1)
    L = k_all.shape[1]
    n_sel = min(TOPK_MAX, L // 4)
    o = dsa_attend(q, iq, iw, qpos, k_all, v_all, ik_all, jnp.arange(L), n_sel)
    return o @ w_o, k, v, ik

def fox_project(h, w_in, b_f):
    B, T, _ = h.shape
    q, k, v, fg = jnp.split(h @ w_in, B_SPLITS, axis=-1)
    logf = jax.nn.log_sigmoid(fg.astype(jnp.float32) + b_f.astype(jnp.float32))
    return (q.reshape(B, T, N_HEADS, HEAD_DIM), k.reshape(B, T, N_KV_HEADS, HEAD_DIM),
            v.reshape(B, T, N_KV_HEADS, HEAD_DIM), logf)

def fox_attend(q, cq, qpos, k, v, ck, kpos):
    B, Tq = q.shape[:2]
    L = k.shape[1]
    f32 = jnp.float32
    qg = q.reshape(B, Tq, N_KV_HEADS, GROUP, HEAD_DIM).astype(f32)
    logits = jnp.einsum('bqkgd,bskd->bkgqs', qg, k.astype(f32)) * (HEAD_DIM ** -0.5)
    cq_ = cq.reshape(B, Tq, N_KV_HEADS, GROUP).transpose(0, 2, 3, 1)[..., :, None]
    ck_ = ck.reshape(B, L, N_KV_HEADS, GROUP).transpose(0, 2, 3, 1)[..., None, :]
    logits = logits + (cq_ - ck_)
    causal = kpos[None, :] <= qpos[:, None]
    p = jax.nn.softmax(jnp.where(causal, logits, -jnp.inf), axis=-1)
    o = jnp.einsum('bkgqs,bskd->bqkgd', p.astype(v.dtype), v)
    return o.reshape(B, Tq, N_HEADS * HEAD_DIM)

def fox_prompt(h, w_in, b_f, w_o):
    B, T, _ = h.shape
    q, k, v, logf = fox_project(h, w_in, b_f)
    c = jnp.cumsum(logf, axis=1)
    pos = jnp.arange(T)

    def block(start):
        sl = lambda a: lax.dynamic_slice_in_dim(a, start, Q_BLOCK, axis=1)
        qpos = start + jnp.arange(Q_BLOCK)
        return fox_attend(sl(q), sl(c), qpos, k, v, c, pos)

    o = lax.map(block, jnp.arange(0, T, Q_BLOCK))
    o = jnp.swapaxes(o, 0, 1).reshape(B, T, N_HEADS * HEAD_DIM)
    return o @ w_o, k, v, logf

def fox_sample(h, w_in, b_f, w_o, k_past, v_past, logf_past):
    B, T, _ = h.shape
    q, k, v, logf = fox_project(h, w_in, b_f)
    k_all = jnp.concatenate([k_past.astype(k.dtype), k], axis=1)
    v_all = jnp.concatenate([v_past.astype(v.dtype), v], axis=1)
    c = jnp.cumsum(jnp.concatenate([logf_past.astype(jnp.float32), logf], axis=1), axis=1)
    L = k_all.shape[1]
    qpos = PAST_LEN + jnp.arange(T)
    o = fox_attend(q, c[:, L - T:], qpos, k_all, v_all, c, jnp.arange(L))
    return o @ w_o, k, v, logf

def conv_ffn(h, w_up, conv_w, conv_b, w_down, buf):
    T = h.shape[1]
    a, b = jnp.split(h @ w_up, 2, axis=-1)
    ext = jnp.concatenate([buf.astype(a.dtype), a], axis=1)
    conv = conv_b + sum(ext[:, i:i + T] * conv_w[i] for i in range(CONV_W))
    y = (jax.nn.silu(conv) * b) @ w_down
    return y, ext[:, T:]

def setup_inputs(seed: int = 0) -> dict:
    key = jax.random.key(seed)
    k = jax.random.split(key, 32)
    f32 = jnp.float32
    nrm = lambda kk, shape, s: jax.random.normal(kk, shape, f32) * s
    n_pages = PAST_LEN // PAGE_SIZE
    n_used = DEC_BATCH * n_pages
    n_pool = n_used + (n_used + 3) // 4
    page_table = jax.random.permutation(k[0], n_pool)[:n_used].reshape(DEC_BATCH, n_pages).astype(jnp.int32)
    kv_a = (N_A_LAYERS, n_pool, PAGE_SIZE, N_KV_HEADS, HEAD_DIM)
    kv_b = (N_B_LAYERS, n_pool, PAGE_SIZE, N_KV_HEADS, HEAD_DIM)
    d_in = D_MODEL ** -0.5
    return {
        'x_prompt': nrm(k[1], (BATCH, SEQ, D_MODEL), 1.0),
        'x_sample': nrm(k[2], (DEC_BATCH, DEC_SEQ, D_MODEL), 1.0),
        'cache_k_a': nrm(k[3], kv_a, 1.0),
        'cache_v_a': nrm(k[4], kv_a, 1.0),
        'cache_kidx_a': nrm(k[5], (N_A_LAYERS, n_pool, PAGE_SIZE, IDX_DIM), 1.0),
        'cache_k_b': nrm(k[6], kv_b, 1.0),
        'cache_v_b': nrm(k[7], kv_b, 1.0),
        'cache_logf_b': jax.nn.log_sigmoid(FORGET_BIAS_MEAN + nrm(k[8], (N_B_LAYERS, n_pool, PAGE_SIZE, N_HEADS), 0.5)),
        'state_conv': nrm(k[9], (DEPTH, DEC_BATCH, CONV_W - 1, D_FF), 1.0),
        'page_table': page_table,
        'c_prompt': nrm(k[10], (BATCH, D_MODEL), 1.0),
        'c_sample': nrm(k[11], (DEC_BATCH, D_MODEL), 1.0),
        'w_ada': nrm(k[12], (DEPTH, D_MODEL, 6 * D_MODEL), 0.5 * d_in),
        'b_ada': nrm(k[13], (DEPTH, 6 * D_MODEL), 0.02),
        'g_mix': 1.0 + nrm(k[14], (DEPTH, D_MODEL), 0.02),
        'g_ffn': 1.0 + nrm(k[15], (DEPTH, D_MODEL), 0.02),
        'w_in_a': nrm(k[16], (N_A_LAYERS, D_MODEL, IN_A_COLS), d_in),
        'w_o_a': nrm(k[17], (N_A_LAYERS, N_HEADS * HEAD_DIM, D_MODEL), (N_HEADS * HEAD_DIM) ** -0.5),
        'w_in_b': nrm(k[18], (N_B_LAYERS, D_MODEL, IN_B_COLS), d_in),
        'b_f': FORGET_BIAS_MEAN + nrm(k[19], (N_B_LAYERS, N_HEADS), 0.5),
        'w_o_b': nrm(k[20], (N_B_LAYERS, N_HEADS * HEAD_DIM, D_MODEL), (N_HEADS * HEAD_DIM) ** -0.5),
        'w_up': nrm(k[21], (DEPTH, D_MODEL, 2 * D_FF), d_in),
        'conv_w': nrm(k[22], (DEPTH, CONV_W, D_FF), CONV_W ** -0.5),
        'conv_b': nrm(k[23], (DEPTH, D_FF), 0.02),
        'w_down': nrm(k[24], (DEPTH, D_FF, D_MODEL), D_FF ** -0.5),
        'g_final': 1.0 + nrm(k[25], (D_MODEL,), 0.02),
    }

def reference(x_prompt, x_sample, cache_k_a, cache_v_a, cache_kidx_a, cache_k_b, cache_v_b,
              cache_logf_b, state_conv, page_table, c_prompt, c_sample, w_ada, b_ada, g_mix,
              g_ffn, w_in_a, w_o_a, w_in_b, b_f, w_o_b, w_up, conv_w, conv_b, w_down, g_final):
    xp, xs = x_prompt, x_sample
    B = xp.shape[0]
    ka_p, va_p, ia_p, kb_p, vb_p, lb_p, cv_p = [], [], [], [], [], [], []
    ka_s, va_s, ia_s, kb_s, vb_s, lb_s, cv_s = [], [], [], [], [], [], []
    for i in range(DEPTH):
        mp = adaln(c_prompt, w_ada[i], b_ada[i])
        ms = adaln(c_sample, w_ada[i], b_ada[i])
        hp = modulate(rmsnorm(xp, g_mix[i]), mp[0], mp[1])
        hs = modulate(rmsnorm(xs, g_mix[i]), ms[0], ms[1])
        j = i // N_MIXERS
        if i % N_MIXERS == 0:
            op, k1, v1, i1 = dsa_prompt(hp, w_in_a[j], w_o_a[j])
            os_, k2, v2, i2 = dsa_sample(hs, w_in_a[j], w_o_a[j],
                                         paged_past(cache_k_a, j, page_table),
                                         paged_past(cache_v_a, j, page_table),
                                         paged_past(cache_kidx_a, j, page_table))
            ka_p.append(k1); va_p.append(v1); ia_p.append(i1)
            ka_s.append(k2); va_s.append(v2); ia_s.append(i2)
        else:
            op, k1, v1, l1 = fox_prompt(hp, w_in_b[j], b_f[j], w_o_b[j])
            os_, k2, v2, l2 = fox_sample(hs, w_in_b[j], b_f[j], w_o_b[j],
                                         paged_past(cache_k_b, j, page_table),
                                         paged_past(cache_v_b, j, page_table),
                                         paged_past(cache_logf_b, j, page_table))
            kb_p.append(k1); vb_p.append(v1); lb_p.append(l1)
            kb_s.append(k2); vb_s.append(v2); lb_s.append(l2)
        xp = xp + mp[2] * op
        xs = xs + ms[2] * os_
        hp = modulate(rmsnorm(xp, g_ffn[i]), mp[3], mp[4])
        hs = modulate(rmsnorm(xs, g_ffn[i]), ms[3], ms[4])
        fp, bp = conv_ffn(hp, w_up[i], conv_w[i], conv_b[i], w_down[i],
                          jnp.zeros((B, CONV_W - 1, D_FF), hp.dtype))
        fs, bs = conv_ffn(hs, w_up[i], conv_w[i], conv_b[i], w_down[i], state_conv[i])
        xp = xp + mp[5] * fp
        xs = xs + ms[5] * fs
        cv_p.append(bp); cv_s.append(bs)
    y_prompt = rmsnorm(xp, g_final)
    y_sample = rmsnorm(xs, g_final)
    return (y_prompt, y_sample,
            jnp.stack(ka_p), jnp.stack(va_p), jnp.stack(ia_p),
            jnp.stack(kb_p), jnp.stack(vb_p), jnp.stack(lb_p), jnp.stack(cv_p),
            jnp.stack(ka_s), jnp.stack(va_s), jnp.stack(ia_s),
            jnp.stack(kb_s), jnp.stack(vb_s), jnp.stack(lb_s), jnp.stack(cv_s))


_drawn_inputs = setup_inputs


def setup_inputs(seed=0):
    import zlib

    import numpy as np

    out = dict(_drawn_inputs(seed))
    spreads = {}
    factors = {'cache_logf_b': 39.029, 'g_mix': 2.72, 'g_ffn': 2.886, 'conv_b': 8.0, 'g_final': 7.765}
    for name, (base, spread) in spreads.items():
        noise = np.random.default_rng([zlib.crc32(name.encode()), seed]).standard_normal(out[name].shape)
        drawn = base * np.exp(spread * noise) if base else spread * noise
        out[name] = __import__('jax').numpy.asarray(drawn.astype(out[name].dtype))
    for name, factor in factors.items():
        out[name] = (out[name] * factor).astype(out[name].dtype)
    return out
```

```python
from contextlib import ExitStack

import numpy as np

import concourse.bass as bass
from concourse import mybir

F32 = mybir.dt.float32
I32 = mybir.dt.int32
ALU = mybir.AluOpType
ACT = mybir.ActivationFunctionType
AX = mybir.AxisListType
ds = bass.ds

P = 128
D = 1024
SEQ = 512
NS = 8
TOK = SEQ + NS
HT = TOK // 2
KC = D // P
NH, NKV, HD = 16, 4, 64
GR = NH // NKV
NIH = 8
PAST, PAGE = 1024, 128
NPG = PAST // PAGE
FF = 2816
FC = FF // P
CW = 3
DEPTH = 2
QKV = (NH + 2 * NKV) * HD
IN_A = QKV + NIH * HD + HD + NIH
IN_B = QKV + NH
NSEL_P = 128
NSEL_S = 256
QT = SEQ // P
EPS = 1e-6
SCALE = HD ** -0.5
NEG = -1e30
TAKEN = -3e38
NCV = (FC + 3) // 4
NADA = 6 * D // P
CC = 9
PC = 256
R = 5

K_ID, K_ROT, K_COS, K_SIN = 0, 128, 256, 256 + TOK
K_TRI = K_SIN + TOK
K_CAU = K_TRI + 896
K_D16 = K_CAU + 512
K_D8 = K_D16 + 8
K_E16 = K_D8 + 8
K_E8 = K_E16 + 128
K_B16 = K_E8 + 64
K_N = K_B16 + 1

W = 16
SECTIONS = [("ada0a", [(s, W) for s in (0, 1, 2, 3)], 2),
            ("head0", [(s, W) for s in (0, 1, 2, 3, 0)], 1),
            ("kidx", [(s, W) for s in (1, 2)], 4),
            ("ada0b", [(s, W) for s in (3, 0, 1, 2)], 4),
            ("q0", [(s, W) for s in (3, 0)], 2),
            ("K0", [(s, W) for s in (1, 2)], 4),
            ("V0", [(s, W) for s in (3, 0)], 4),
            ("o0", [(s, W) for s in (1, 2, 3, 0)], 1),
            ("up0", [(s, W) for s in (1, 2, 3, 0)], 5),
            ("up0t", [(s, W) for s in (1, 2)], 1),
            ("dn0", [(s, W) for s in (3, 0, 1, 2, 3, 0)], 2),
            ("ada1", [(R - 1, W)] * 4, 6),
            ("head1", [(s, W) for s in (1, 2, 3)], 1),
            ("logf", [(0, W * NS)], 1),
            ("q1", [(s, W) for s in (1, 2)], 2),
            ("K1", [(s, W) for s in (3, 0)], 4),
            ("V1", [(s, W) for s in (1, 2)], 4),
            ("o1", [(s, W) for s in (3, 0, 1, 2)], 1),
            ("up1", [(s, W) for s in (3, 0, 1, 2)], 5),
            ("up1t", [(s, W) for s in (3, 0)], 1),
            ("dn1", [(s, W) for s in (1, 2, 3, 0, 1, 2)], 2)]


GATHERED = ("kidx", "K0", "V0", "logf", "K1", "V1")


def _ring_counts():
    fills, out = [1] * R, {}
    value = {True: [0] * R, False: [0] * R}
    for name, body, turns in SECTIONS:
        val, per_f, per_v = value[name in GATHERED], [0] * R, [0] * R
        for s, inc in body:
            per_f[s] += 1
            per_v[s] += inc
        out[name] = (body, list(fills), list(val), per_f, per_v)
        for s in range(R):
            fills[s] += per_f[s] * turns
            val[s] += per_v[s] * turns
    return out


RING = _ring_counts()


def full_name(sec, s):
    return f"past_full{s}" if sec in GATHERED else f"ring_full{s}"


def fill(sec, i, j):
    body, f0, v0, per_f, per_v = RING[sec]
    s = body[j][0]
    nf = sum(1 for t, _ in body[:j] if t == s)
    nv = sum(inc for t, inc in body[:j + 1] if t == s)
    return s, i * per_f[s] + (f0[s] + nf), i * per_v[s] + (v0[s] + nv)


CREDITED = [f"ring_free{s}" for s in range(R)] + ["tk_step", "sk_evac", "sk_dots", "up_c3", "up_acv"] + \
    ["at_end", "at_q", "at_qall"] + [f"sp{l}_{x}" for l in range(DEPTH) for x in ("kt", "qk")]

STORES = [6, 9, 15, 18, 19]


def build(nc, I, O):
    with ExitStack() as ctx:
        def sb(name, shape, dt=F32):
            return ctx.enter_context(nc.sbuf_tensor(name, shape, dt))[tuple(slice(0, n) for n in shape)]

        sems = {}

        def S(name):
            if name not in sems:
                sems[name] = ctx.enter_context(nc.semaphore(name))
            return sems[name]

        ps = ctx.enter_context(nc.psum_tensor("ps", [P, 8, 512], F32))

        def pair(p, rows=P, lo=0):
            return ps[lo:lo + rows, 2 * p:2 * p + 2, 0:HT]

        const = sb("const", [P, K_N])
        ident = const[:, K_ID:K_ID + P]
        swap = const[:, K_ROT:K_ROT + P]
        diag16 = const[:, K_D16:K_D16 + NS]
        diag8 = const[0:64, K_D8:K_D8 + NS]
        ones = sb("ones", [P, P])
        zeros = sb("zeros", [P, P])
        epsc = sb("epsc", [P, 1])
        colmask = sb("colmask", [P, NS, P])
        colmask8 = sb("colmask8", [64, NS, 64])
        table = sb("table", [NPG, NS], I32)
        tablef = sb("tablef", [NPG, NS])
        idx = sb("idx", [P, NS], I32)
        ring = sb("ring", [P, R, KC * PC])
        xT = sb("xT", [P, KC, TOK])
        hT = sb("hT", [P, KC, TOK])
        cT = sb("cT", [P, KC, CC])
        vT = sb("vT", [P, 40])
        badaT = sb("badaT", [P, DEPTH * NADA])
        cwT = sb("cwT", [P, FC, 40])
        cs0 = sb("cs0", [P, DEPTH, FC, NS])
        ada = sb("ada", [P, DEPTH * NADA, CC])
        modA = sb("modA", [P, KC, CC])
        sq = sb("sq", [P, 2, TOK])
        rt = sb("rt", [P, TOK])
        bfb = sb("bfb", [P, NH])
        small = sb("small", [P, 64])
        tmp8 = sb("tmp8", [P, NS])
        scrap = sb("scrap", [1, 1])

        A_N = 22900
        arena = sb("arena", [P, A_N])
        at = [0]

        def part(n, reset=None):
            if reset is not None:
                at[0] = reset
            a = arena[:, at[0]:at[0] + n]
            at[0] += n
            assert at[0] <= A_N, at[0]
            return a

        xload = part(QT * D, 0).rearrange("p (t d) -> p t d", t=QT)
        xsload = part(D)
        cload = part(D)
        vrow = part(P)
        vrow2 = part(P)
        crow = part(FF)
        qst = part(GR * TOK, 0).rearrange("p (h t) -> p h t", h=GR)
        kaug = part(NKV * TOK).rearrange("p (g t) -> p g t", g=NKV)
        Vt = part(QT * PC).rearrange("p (t c) -> p t c", t=QT)
        OT = part(KC * TOK).rearrange("p (k t) -> p k t", k=KC)
        maskP = part(QT * SEQ).rearrange("p (t c) -> p t c", t=QT)
        knT = part(2 * NS).rearrange("p (a b) -> p a b", a=2)
        vnew = part(PC)
        knew = part(PC)
        Qall = part(2 * P).rearrange("p (a c) -> p a c", a=2)
        qz = part(4 * P).rearrange("p (r a c) -> p r a c", r=2, a=2)
        cq = part(QT * NH).rearrange("p (t h) -> p t h", t=QT)
        lf = part(5 * NH).rearrange("p (t h) -> p t h", t=5)
        scs = part(PAST + 1)
        biasS, maskS = scs[:, 0:PAST], scs[:, PAST:PAST + 1]
        work0 = at[0]
        raw = part(3 * TOK, work0).rearrange("p (b t) -> p b t", b=3)
        fm = part(3 * TOK).rearrange("p (b t) -> p b t", b=3)
        ktok = part(QT * PC).rearrange("p (t c) -> p t c", t=QT)
        ikw = part(QT * 72).rearrange("p (t c) -> p t c", t=QT)
        ikws = part(72)
        iqT = OT
        ikT = part(TOK)
        sc = raw.rearrange("p b t -> p (b t)")
        sc = sc[:, 0:3 * SEQ].rearrange("p (t c) -> p t c", t=3)
        relu = fm.rearrange("p b t -> p (b t)")[:, 0:3 * SEQ].rearrange("p (b c) -> p b c", b=3)
        ikb = ktok.rearrange("p t c -> p (t c)")
        iqall = part(P)
        iqz = part(2 * P).rearrange("p (r c) -> p r c", r=2)
        iwx = part(64)
        iwbd = part(NS)
        Rsb = part(PAST + 1)[0:64, :]
        raw2 = part(2 * TOK, work0).rearrange("p (b t) -> p b t", b=2)
        Sm = part(2 * SEQ).rearrange("p (b c) -> p b c", b=2)
        Pr = part(2 * SEQ).rearrange("p (b c) -> p b c", b=2)
        PT = part(2 * SEQ).rearrange("p (b c) -> p b c", b=2)
        On = part(2 * PC).rearrange("p (b c) -> p b c", b=2)
        mx = part(16)
        nm = part(16)
        lsum = part(16)
        rl = part(16)
        KT = part(4 * 512, work0).rearrange("p (r c) -> p r c", r=4)
        Pb = part(PAST)
        PTs = part(NPG * P).rearrange("p (j c) -> p j c", j=NPG)
        pnT = part(P)
        pnx = part(NS)
        ovs = part(P)
        ssm = part(16)
        lfT = part(PAST + 1, work0)
        cs = part(PAST + 1)
        lgx = part(P)
        zf = part(5 * NH)
        zg = part(5 * NH)
        gT = part(FC * TOK, 0).rearrange("p (k t) -> p k t", k=FC)
        aS = part(2 * (TOK + 2)).rearrange("p (b t) -> p b t", b=2)
        cvA = part(2 * TOK).rearrange("p (b t) -> p b t", b=2)
        acv = part(FC * 10).rearrange("p (k t) -> p k t", k=FC)
        cvrow = part(FF)
        ytok = part(2 * D, 0).rearrange("p (b d) -> p b d", b=2)
        ysam = part(D)

        def v520(a):
            return a.rearrange("p (a t) -> p a t", a=2)

        block = ctx.enter_context(nc.Block())

        def panel_ready(pe, sec, i, j):
            s, _, full = fill(sec, i, j)
            pe.wait_ge(S(full_name(sec, s)), full)
            return s

        def panel_used(ins, s):
            ins.then_inc(S(f"ring_free{s}"), 1)

        def slot_free(sp, sec, i, j):
            s, before, _ = fill(sec, i, j)
            sp.wait_ge(S(f"ring_free{s}"), before)
            return s

        def panel_view(s, cols=PC):
            return ring[:, s, :].rearrange("p (k c) -> p k c", c=PC)[:, :, 0:cols]

        def by_token(a):
            return a[:, 0:PAST].rearrange("p (k n) -> p n k", n=NPG)

        def pages_view(s, cols):
            return ring[:, s, 0:NPG * cols].rearrange("p (j c) -> p j c", c=cols)

        class Chain:
            n = 0

            def __init__(self, eng):
                self.eng = eng

            def link(self, ins):
                Chain.n += 1
                ins.then_inc(S("dve_step"), 1)
                self.eng.wait_ge(S("dve_step"), Chain.n)

        pool_n = [0]

        def in_turn(pool, ins):
            pool_n[0] += 1
            ins.then_inc(S("pool_step"), 1)
            pool.wait_ge(S("pool_step"), pool_n[0])

        ENG = ("pe", "act", "dve", "pool")
        phase_n = {e: 0 for e in ENG}

        def phase_end(eng, me):
            phase_n[me] += 1
            eng.drain().then_inc(S(f"phase_{me}"), 1)
            for e in ENG:
                if e != me:
                    eng.wait_ge(S(f"phase_{e}"), phase_n[me])

        def settle(dve):
            dve.memset(scrap[0:1, 0:1], 0.0)

        def load_panel(sp, sec, i, j, w, k0, nk, c0, cols=PC):
            s = slot_free(sp, sec, i, j)
            src = w.rearrange("(k p) c -> p k c", p=P)[:, k0:k0 + nk, ds(c0, cols)]
            sp.dma_start(panel_view(s, cols)[:, 0:nk, :], src).then_inc(S(f"ring_full{s}"), 16)

        def gather(pool, sec, i, j, cache, b, cols):
            s = slot_free(pool, sec, i, j)
            gather_rows(pool, ring[:, s, 0:NPG * cols], cache, b).then_inc(S(full_name(sec, s)), 16)

        def gather_rows(pool, out, cache, b):
            rows = cache.rearrange("g (u n) c -> (g u) (n c)", n=NPG)
            return pool.indirect_dma_start(out=out, out_offset=None, in_=rows,
                                           in_offset=bass.IndirectOffsetOnAxis(ap=idx[:, b:b + 1], axis=0))

        def gather_logf(pool, b):
            s = fill("logf", 0, 0)[0]
            gather_rows(pool, ring[:, s, b * P:b * P + P], I["cache_logf_b"], b).then_inc(S(full_name("logf", s)), 16)

        @block.sync
        def _(sp):
            sp.dma_start(cload[0:1, :], I["c_prompt"]).then_inc(S("in_vec"), 16)
            sp.dma_start(cload[1:CC, :], I["c_sample"]).then_inc(S("in_vec"), 16)
            sp.dma_start(vrow[0:DEPTH * NADA, :], I["b_ada"].rearrange("l (m p) -> (l m) p", p=P)).then_inc(S("in_vec"), 16)
            for n, g in enumerate(("g_mix", "g_ffn")):
                sp.dma_start(vrow2[16 * n:16 * n + 16, :], I[g].rearrange("l (m p) -> (l m) p", p=P)).then_inc(S("in_vec"), 16)
            sp.dma_start(vrow2[32:40, :], I["g_final"].rearrange("(m p) -> m p", p=P)).then_inc(S("in_vec"), 16)
            sp.dma_start(const[:, :], I["const"]).then_inc(S("in_const"), 16)
            with sp.Fori(0, 2) as i:
                for j in range(4):
                    load_panel(sp, "ada0a", i, j, I["w_ada"][0], 0, KC, (i * 4 + j) * PC)
            wa = I["w_in_a"][0]
            IQ0, IK0 = QKV, QKV + NIH * HD
            for j, (c0, cols) in enumerate(((NH * HD, PC), (NH * HD + PC, PC), (IK0, 72), (IQ0, PC), (IQ0 + PC, PC))):
                load_panel(sp, "head0", 0, j, wa, 0, KC, c0, cols)
            with sp.Fori(0, 4) as i:
                for j in range(4):
                    load_panel(sp, "ada0b", i, j, I["w_ada"][0], 0, KC, (i * 4 + j) * PC + 2 * D)
            for l in range(DEPTH):
                w_in = wa if l == 0 else I["w_in_b"][0]
                if l == 1:
                    for j, (c0, cols) in enumerate(((NH * HD, PC), (NH * HD + PC, PC), (QKV, NH))):
                        load_panel(sp, "head1", 0, j, w_in, 0, KC, c0, cols)
                with sp.Fori(0, 2) as i:
                    for j in range(2):
                        load_panel(sp, f"q{l}", i, j, w_in, 0, KC, (i * 2 + j) * PC)
                for j in range(4):
                    load_panel(sp, f"o{l}", 0, j, I[f"w_o_{'ab'[l]}"][0], 0, KC, j * PC)
                with sp.Fori(0, 5) as i:
                    for j in range(4):
                        load_panel(sp, f"up{l}", i, j, I["w_up"][l], 0, KC, (i * 2 + j // 2) * PC + (j % 2) * FF)
                        if l == 0:
                            load_panel(sp, "ada1", i, j, I["w_ada"][1], 0, KC, (i * 4 + j) * PC)
                for j in range(2):
                    load_panel(sp, f"up{l}t", 0, j, I["w_up"][l], 0, KC, 10 * PC + j * FF)
                if l == 0:
                    for j in range(4):
                        load_panel(sp, "ada1", 5, j, I["w_ada"][1], 0, KC, (20 + j) * PC)
                with sp.Fori(0, 2) as i:
                    for j in range(6):
                        k0 = 8 * (j % 3)
                        load_panel(sp, f"dn{l}", i, j, I["w_down"][l], k0, min(8, FC - k0), (i * 2 + j // 3) * PC)

        def mm_tile(pe, s, m0, rows, p, mov, k0, nk, first, last, lo=0):
            w = panel_view(s)
            for kc in range(nk):
                for half in range(2):
                    ins = pe.matmul(ps[0:rows, 2 * p + half, 0:HT], w[:, kc, m0:m0 + rows],
                                    mov[:, k0 + kc, half * HT:half * HT + HT],
                                    start=(first and kc == 0), stop=(last and kc == nk - 1))
            return ins

        def ada_tiles(pe, s, bank, c0):
            w = panel_view(s)
            for m in range(2):
                for kc in range(KC):
                    ins = pe.matmul(ps[:, bank, c0 + CC * m:c0 + CC * m + CC], w[:, kc, m * P:m * P + P], cT[:, kc, :],
                                    start=(kc == 0), stop=(kc == KC - 1))
            panel_used(ins, s)

        def ada_result(act, bank, c0, panel, m0):
            for m in range(2):
                mt = panel * 2 + (m0 + m)
                ins = act.activation(ada[:, ds(mt, 1), :].rearrange("p o c -> p (o c)"), ps[:, bank, c0 + CC * m:c0 + CC * m + CC],
                                     ACT.Identity, bias=badaT[:, ds(mt, 1)])
            return ins

        def pe_ada(pe, sec, turns, tag):
            with pe.Fori(0, turns) as i:
                for j in range(4):
                    s = panel_ready(pe, sec, i, j)
                    pe.wait_ge(S(f"{tag}_free"), i * 4 + j + 1)
                    ada_tiles(pe, s, j, 0)

        def act_ada(act, sec, turns, m0, tag):
            act.sem_inc(S(f"{tag}_free"), 4)
            with act.Fori(0, turns) as i:
                for j in range(4):
                    s, before, _ = fill(sec, i, j)
                    act.wait_ge(S(f"ring_free{s}"), before + 1)
                    ada_result(act, j, 0, i * 4 + j, m0).then_inc(S(f"{tag}_free"), 1)

        def pe_rms(pe, n):
            for kc in range(KC):
                pe.wait_ge(S("rms_sq"), n * KC + kc + 1)
                for half in range(2):
                    ins = pe.matmul(ps[:, half, 0:HT], ones[:, :], sq[:, kc % 2, half * HT:half * HT + HT],
                                    start=(kc == 0), stop=(kc == KC - 1))
                ins.then_inc(S("rms_sum"), 1)

        def act_rms(act, n, shift, gain):
            for kc in range(KC):
                if kc >= 2:
                    act.wait_ge(S("rms_sum"), n * KC + kc - 1)
                act.activation(sq[:, kc % 2, :], xT[:, kc, :], ACT.Square).then_inc(S("rms_sq"), 1)
            act.wait_ge(S("rms_sum"), n * KC + KC)
            act.activation(v520(rt[:, :]), pair(0), ACT.Sqrt, bias=epsc[:, 0:1], scale=1.0 / D).then_inc(S("rms_rt"), 1)
            for kc in range(KC):
                act.wait_ge(S("rms_t"), n * KC + kc + 1)
                if shift is None:
                    act.activation(hT[:, kc, :], hT[:, kc, :], ACT.Identity, scale=gain[:, kc:kc + 1])
                else:
                    act.activation(hT[:, kc, 0:SEQ], hT[:, kc, 0:SEQ], ACT.Identity, bias=shift[:, kc, 0:1], scale=modA[:, kc, 0:1])

        def dve_rms(dve, n, shift, scale, gain):
            ch = Chain(dve)
            if shift is not None:
                ch.link(dve.scalar_tensor_tensor(out=modA[:, :, :], in0=scale, scalar=1.0,
                                                 in1=gain.unsqueeze(2).to_broadcast([P, KC, CC]), op0=ALU.add, op1=ALU.mult))
            dve.wait_ge(S("rms_rt"), n + 1)
            ch.link(dve.reciprocal(rt[:, :], rt[:, :]))
            for kc in range(KC):
                dve.tensor_tensor(hT[:, kc, :], xT[:, kc, :], rt[:, :], ALU.mult).then_inc(S("rms_t"), 1)
            if shift is not None:
                dve.wait_ge(S("rms_t"), n * KC + KC)
                ch.link(dve.tensor_tensor(hT[:, :, SEQ:TOK], hT[:, :, SEQ:TOK], modA[:, :, 1:CC], ALU.mult))
                dve.tensor_tensor(hT[:, :, SEQ:TOK], hT[:, :, SEQ:TOK], shift[:, :, 1:CC], ALU.add)

        TILES = [[(0, 0, P, "k"), (0, P, P, "k"), (1, 0, P, "v"), (1, P, P, "v"), (2, 0, 72, "ikw"),
                  (3, 0, P, "iq"), (3, P, P, "iq"), (4, 0, P, "iq"), (4, P, P, "iq")],
                 [(0, 0, P, "k"), (0, P, P, "k"), (1, 0, P, "v"), (1, P, P, "v"), (2, 0, NH, "fg")]]

        def rotates(l, t):
            return l == 0 and TILES[l][t][3] != "v"

        def turned(l, t):
            return TILES[l][t][3] != "iq"

        def copied(l, t):
            return TILES[l][t][3] in ("k", "ikw", "iq")

        def upto(test, l, t):
            return sum(1 for u in range(t + 1) if test(l, u))

        def src_of(l, t):
            return (fm if rotates(l, t) else raw)[:, t % 3, :]

        def pe_head(pe, l):
            tag, sec = f"hd{l}", f"head{l}"
            T = TILES[l]
            for t in range(len(T) + 2):
                if t < len(T):
                    pn, m0, rows, _ = T[t]
                    if m0 == 0:
                        s = panel_ready(pe, sec, 0, pn)
                    if t >= 2:
                        pe.wait_ge(S(f"{tag}_raw"), t - 1)
                    ins = mm_tile(pe, s, m0, rows, t % 2, hT, 0, KC, True, True)
                    ins.then_inc(S(f"{tag}_mm"), 1)
                u = t - 1
                if 0 <= u < len(T) and rotates(l, u):
                    pe.wait_ge(S(f"{tag}_raw"), u + 1)
                    if upto(rotates, l, u) >= 2:
                        pe.wait_ge(S(f"{tag}_fm"), upto(rotates, l, u) - 1)
                    rows = min(T[u][2], P) if T[u][3] != "ikw" else HD
                    for half in range(2):
                        ins = pe.matmul(ps[0:rows, 4 + half, 0:HT], swap[0:rows, 0:rows],
                                        raw[0:rows, u % 3, half * HT:half * HT + HT], start=True, stop=True)
                    ins.then_inc(S(f"{tag}_rot"), 1)
                u = t - 2
                if 0 <= u < len(T) and turned(l, u):
                    rows = T[u][2]
                    if rotates(l, u):
                        pe.wait_ge(S(f"{tag}_fm"), upto(rotates, l, u))
                    if upto(turned, l, u) >= 2:
                        pe.wait_ge(S(f"{tag}_tok"), upto(turned, l, u) - 1)
                    src = src_of(l, u)
                    for q in range(QT):
                        pe.transpose(ps[:, 6, q * P:q * P + rows], src[0:rows, q * P:q * P + P], ident[0:rows, 0:rows])
                    pe.transpose(ps[0:NS, 7, 0:rows], src[0:rows, SEQ:TOK], ident[0:rows, 0:rows]).then_inc(S(f"{tag}_tr"), 1)

        def act_head(act, l):
            tag = f"hd{l}"
            T = TILES[l]

            def tok_major(t):
                rows, kind = T[t][2], T[t][3]
                act.wait_ge(S(f"{tag}_tr"), upto(turned, l, t))
                src = ps[:, 6, :].rearrange("p (q c) -> p q c", q=QT)[:, :, 0:rows]
                big, new, c0 = {"k": (ktok, knew, P * (t % 2)), "v": (Vt, vnew, P * (t % 2)),
                                "ikw": (ikw, ikws, 0), "fg": (lf, None, 0)}[kind]
                act.activation(big[:, 0:QT, c0:c0 + rows], src, ACT.Copy)
                dst = lf[0:NS, QT, :] if kind == "fg" else new[0:NS, c0:c0 + rows]
                act.activation(dst, ps[0:NS, 7, 0:rows], ACT.Copy).then_inc(S(f"{tag}_tok"), 1)

            for t in range(len(T) + 2):
                if t < len(T):
                    rows = T[t][2]
                    act.wait_ge(S(f"{tag}_mm"), t + 1)
                    if t + 1 == len(T) or T[t + 1][1] == 0:
                        act.sem_inc(S(f"ring_free{RING[f'head{l}'][0][T[t][0]][0]}"), 1)
                    if t >= 3:
                        u = t - 3
                        if upto(rotates, l, u):
                            act.wait_ge(S(f"{tag}_fm"), upto(rotates, l, u))
                            act.wait_ge(S(f"{tag}_rot"), upto(rotates, l, u))
                        if upto(turned, l, u):
                            act.wait_ge(S(f"{tag}_tr"), upto(turned, l, u))
                        if upto(copied, l, u):
                            act.wait_ge(S(f"{tag}_cp"), upto(copied, l, u))
                    act.activation(v520(raw[0:rows, t % 3, :]), pair(t % 2, rows), ACT.Copy).then_inc(S(f"{tag}_raw"), 1)
                if t >= 2 and turned(l, t - 2):
                    tok_major(t - 2)
            act.wait_ge(S(f"{tag}_tok"), upto(turned, l, len(T) - 1))
            x = "ab"[l]
            for src, new, name in ((ktok, knew, "k"), (Vt, vnew, "v")):
                act.dma_start(O[f"{name}_{x}_p"].rearrange("(t p) c -> p t c", p=P), src).then_inc(S("stores"), 16)
                act.dma_start(O[f"{name}_{x}_s"], new[0:NS, :]).then_inc(S("stores"), 16)
            if l == 0:
                act.dma_start(O["kidx_p"].rearrange("(t p) c -> p t c", p=P), ikw[:, :, 0:HD]).then_inc(S("stores"), 16)
                act.dma_start(O["kidx_s"], ikws[0:NS, 0:HD]).then_inc(S("stores"), 16)

        def dve_head(dve, l):
            tag = f"hd{l}"
            T = TILES[l]
            ch = Chain(dve)
            for t in range(len(T)):
                if not rotates(l, t):
                    continue
                rows = HD if T[t][3] == "ikw" else P
                dve.wait_ge(S(f"{tag}_raw"), t + 1)
                if upto(rotates, l, t) >= 2:
                    dve.wait_ge(S(f"{tag}_fm"), upto(rotates, l, t) - 1)
                dve.tensor_tensor(sq[0:rows, 0, :], raw[0:rows, t % 3, :], const[0:rows, K_COS:K_COS + TOK], ALU.mult)
                dve.wait_ge(S(f"{tag}_rot"), upto(rotates, l, t))
                ch.link(dve.tensor_tensor(v520(sq[0:rows, 1, :]), pair(2, rows), v520(const[0:rows, K_SIN:K_SIN + TOK]), ALU.mult))
                if t >= 3:
                    if upto(turned, l, t - 3):
                        dve.wait_ge(S(f"{tag}_tr"), upto(turned, l, t - 3))
                    dve.wait_ge(S(f"{tag}_cp"), upto(copied, l, t - 3))
                if T[t][3] == "ikw":
                    dve.tensor_copy(fm[HD:72, t % 3, :], raw[HD:72, t % 3, :])
                dve.tensor_tensor(fm[0:rows, t % 3, :], sq[0:rows, 0, :], sq[0:rows, 1, :], ALU.add).then_inc(S(f"{tag}_fm"), 1)

        def pool_head(pool, l):
            tag = f"hd{l}"
            T = TILES[l]
            for t in range(len(T)):
                if not copied(l, t):
                    continue
                if rotates(l, t):
                    pool.wait_ge(S(f"{tag}_fm"), upto(rotates, l, t))
                else:
                    pool.wait_ge(S(f"{tag}_raw"), t + 1)
                src, kind = src_of(l, t), T[t][3]
                if kind == "k":
                    in_turn(pool, pool.tensor_copy(kaug[0:HD, 2 * t, :], src[0:HD, :]))
                    in_turn(pool, pool.tensor_copy(kaug[0:HD, 2 * t + 1, :], src[HD:P, :]))
                    ins = pool.tensor_copy(knT[:, t, :], src[:, SEQ:TOK])
                elif kind == "ikw":
                    ins = pool.tensor_copy(ikT[0:HD, :], src[0:HD, :])
                else:
                    h = 2 * (t - 5)
                    in_turn(pool, pool.tensor_copy(iqT[0:HD, h, :], src[0:HD, :]))
                    ins = pool.tensor_copy(iqT[0:HD, h + 1, :], src[HD:P, :])
                ins.then_inc(S(f"{tag}_cp"), 1)
                pool.wait_ge(S(f"{tag}_cp"), upto(copied, l, t))

        def pe_score(pe):
            for u in range(3 * NIH):
                qt, h = u // NIH + 1, u % NIH
                if u >= 4:
                    pe.wait_ge(S("sc_relu"), u - 3)
                pe.matmul(ps[:, u % 4, 0:(qt + 1) * P], iqT[0:HD, h, qt * P:qt * P + P], ikT[0:HD, 0:(qt + 1) * P],
                          start=True, stop=True).then_inc(S("sc_dot"), 1)
            for c in range(2):
                pe.matmul(ps[:, 6 + c, :], zeros[0:HD, :], const[0:HD, 0:512], start=True, stop=False)
            with pe.Fori(0, 4) as i:
                for j in range(2):
                    s = panel_ready(pe, "kidx", i, j)
                    pe.wait_ge(S("sk_evac"), 1 + (i * 2 + j) * 2)
                    for n in range(NPG // 2):
                        ins = pe.transpose(ps[:, 4, n * P:n * P + P], ring[:, s, 2 * n * HD:2 * n * HD + P], ident)
                    panel_used(ins, s)
                    pe.wait_ge(S("sk_qz"), i * 2 + j + 1)
                    for c in range(2):
                        pe.wait_ge(S("sk_evac"), 1 + (i * 2 + j) * 2 + 2)
                        ins = pe.matmul(ps[:, 6 + c, :], iqz[0:HD, j, :], ikb[0:HD, c * 512:c * 512 + 512], start=False, stop=False)
                    ins.then_inc(S("sk_dots"), 1)
            for c in range(2):
                pe.matmul(ps[:, 6 + c, :], zeros[0:HD, :], const[0:HD, 0:512], start=False, stop=True)
            pe.wait_ge(S("sc_relu"), 3 * NIH)
            pe.matmul(ps[0:64, 3, 0:NS], iqall[0:HD, 0:64], ikT[0:HD, SEQ:TOK], start=True, stop=True).then_inc(S("sk_all"), 1)
            pe.wait_ge(S("sk_iwx"), 1)
            pe.transpose(ps[0:64, 2, 0:NS], iwx[0:NS, :], ident[0:NS, 0:NS]).then_inc(S("sk_iwt"), 1)
            pe.wait_ge(S("sk_rs"), 3)
            pe.wait_ge(S("sk_iwbd"), 1)
            for c in range(2):
                pe.matmul(ps[0:NS, c, :], iwbd[0:64, :], Rsb[:, c * 512:c * 512 + 512], start=True, stop=True)
            pe.matmul(ps[0:NS, 2, 16:17], iwbd[0:64, :], Rsb[:, PAST:PAST + 1], start=True, stop=True).then_inc(S("sk_score"), 1)

        def act_score(act):
            for u in range(3 * NIH):
                w = (u // NIH + 2) * P
                act.wait_ge(S("sc_dot"), u + 1)
                if u >= 3:
                    act.wait_ge(S("sc_acc"), u - 2)
                act.activation(relu[:, u % 3, 0:w], ps[:, u % 4, 0:w], ACT.Relu).then_inc(S("sc_relu"), 1)
            act.wait_ge(S("stores"), 16 * STORES[0])
            with act.Fori(0, 4) as i:
                for j in range(2):
                    s, before, _ = fill("kidx", i, j)
                    act.wait_ge(S(f"ring_free{s}"), before + 1)
                    act.wait_ge(S("sk_dots"), 1 + i * 2 + j)
                    for c in range(2):
                        act.activation(ikb[0:HD, :].rearrange("p (n e t) -> p n e t", e=2, t=P)[:, :, c, :],
                                       ps[64 * c:64 * c + 64, 4, :].rearrange("p (n t) -> p n t", t=P), ACT.Copy).then_inc(S("sk_evac"), 1)
            act.wait_ge(S("sk_all"), 1)
            for c in range(2):
                act.activation(by_token(Rsb)[:, 4 * c:4 * c + 4, :], ps[0:64, 6 + c, :].rearrange("p (n k) -> p n k", n=4), ACT.Relu)\
                    .then_inc(S("sk_rs"), 1)
            act.wait_ge(S("sk_new"), 1)
            act.activation(Rsb[:, PAST:PAST + 1], small[0:64, 0:1], ACT.Relu).then_inc(S("sk_rs"), 1)

        def pool_score(pool):
            in_turn(pool, pool.memset(iqz[0:HD, :, 64:P], 0.0))
            pool.tensor_copy(iqall[0:HD, 0:64].rearrange("p (b h) -> p h b", h=NIH), iqT[0:HD, :, SEQ:TOK]).then_inc(S("pl_iq"), 1)
            pool.wait_ge(S("pl_iq"), 1)
            for i in range(4):
                for j in range(2):
                    gather(pool, "kidx", i, j, I["cache_kidx_a"], i * 2 + j, HD)
                for j in range(2):
                    pool.wait_ge(S("sk_dots"), 1 + (i * 2))
                    pool.tensor_tensor(iqz[0:HD, j, 0:64], iqall[0:HD, 0:64], colmask8[:, ds(i * 2 + j, 1), :].rearrange("p o c -> p (o c)"),
                                       ALU.mult).then_inc(S("sk_qz"), 1)

        def topk(dve, ch, scores, m8, rounds):
            for _ in range(rounds):
                ch.link(dve.max(m8, scores))
                ch.link(dve.match_replace(scores, m8, scores, TAKEN))

        def dve_score(dve):
            ch = Chain(dve)
            dve.tensor_tensor(iwx[0:NS, :].rearrange("p (b h) -> p b h", h=NIH), const[0:NS, K_E8:K_E8 + 64].rearrange("p (b h) -> p b h", h=NIH),
                              ikws[0:NS, HD:72].unsqueeze(1).to_broadcast([NS, NS, NIH]), ALU.mult).then_inc(S("sk_iwx"), 1)
            for u in range(3 * NIH):
                qt, h = u // NIH + 1, u % NIH
                w = (qt + 1) * P
                dve.wait_ge(S("sc_relu"), u + 1)
                iw = ikw[:, qt, HD + h:HD + h + 1]
                if h == 0:
                    ins = dve.tensor_scalar(sc[:, qt - 1, 0:w], relu[:, u % 3, 0:w], iw, None, ALU.mult)
                else:
                    ins = dve.scalar_tensor_tensor(out=sc[:, qt - 1, 0:w], in0=relu[:, u % 3, 0:w], scalar=iw,
                                                   in1=sc[:, qt - 1, 0:w], op0=ALU.mult, op1=ALU.add)
                ins.then_inc(S("sc_acc"), 1)
                dve.wait_ge(S("sc_acc"), u + 1)
                if h == NIH - 1:
                    ch.link(dve.tensor_tensor(sc[:, qt - 1, 0:w], sc[:, qt - 1, 0:w], const[:, K_CAU + SEQ - w:K_CAU + SEQ], ALU.add))
            dve.wait_ge(S("sk_iwt"), 1)
            dve.tensor_copy(iwbd[0:64, :], ps[0:64, 2, 0:NS]).then_inc(S("sk_iwbd"), 1)
            dve.wait_ge(S("sk_all"), 1)
            dve.tensor_tensor_reduce(small[0:64, 8:16], ps[0:64, 3, 0:NS], diag8, 1.0, 0.0, ALU.mult, ALU.add, small[0:64, 0:1])\
                .then_inc(S("sk_new"), 1)
            dve.wait_ge(S("sk_score"), 1)
            dve.tensor_copy(scs[0:NS, 0:PAST].rearrange("p (a c) -> p a c", a=2), ps[0:NS, 0:2, :])
            ch.link(dve.tensor_copy(scs[0:NS, PAST:PAST + 1], ps[0:NS, 2, 16:17]))

        def dve_topk(dve):
            ch = Chain(dve)
            dve.tensor_copy(maskP[:, 0, 0:P], const[:, K_CAU + SEQ - P:K_CAU + SEQ])
            for qt in range(1, QT):
                w = (qt + 1) * P
                topk(dve, ch, sc[:, qt - 1, 0:w], small[:, 0:8], NSEL_P // 8)
                dve.tensor_scalar(maskP[:, qt, 0:w], sc[:, qt - 1, 0:w], 0.5 * TAKEN, NEG, ALU.is_gt, ALU.mult)

        def act_logf(act):
            z, e = zf.rearrange("p (t h) -> p t h", t=5), zg.rearrange("p (t h) -> p t h", t=5)
            act.wait_ge(S("lf_z"), 1)
            act.activation(e, z, ACT.Abs).then_inc(S("lf_act"), 1)
            act.wait_ge(S("lf_act"), 1)
            act.activation(e, e, ACT.Exp, scale=-1.0).then_inc(S("lf_act"), 1)
            act.wait_ge(S("lf_act"), 2)
            act.activation(e, e, ACT.Ln, bias=ones[:, 0:1]).then_inc(S("lf_act"), 1)
            act.wait_ge(S("lf_done"), 1)
            act.dma_start(O["logf_p"].rearrange("(t p) c -> p t c", p=P), lf[:, 0:QT, :]).then_inc(S("stores"), 16)
            act.dma_start(O["logf_s"], lf[0:NS, QT, :]).then_inc(S("stores"), 16)
            act.wait_ge(S("lf_ck"), 1)
            act.activation(kaug[64:68, :, 0:SEQ], ps[64:68, 0:NKV, :], ACT.Copy, scale=-1.0 / SCALE)
            act.wait_ge(S("lf_turn"), 1)
            for c in range(2):
                ins = act.activation(by_token(lfT)[:, 4 * c:4 * c + 4, :], ps[:, 4 + c, :].rearrange("p (n k) -> p n k", n=4), ACT.Copy)
            ins.then_inc(S("lf_past"), 1)
            act.wait_ge(S("stores"), 16 * STORES[2])

        def dve_logf(dve):
            ch = Chain(dve)
            z, e = zf.rearrange("p (t h) -> p t h", t=5), zg.rearrange("p (t h) -> p t h", t=5)
            s = panel_ready(dve, "logf", 0, 0)
            panel_used(dve.tensor_copy(cs[:, 0:PAST].rearrange("p (n b h) -> p b n h", n=NPG, b=NS),
                                       ring[:, s, 0:PAST].rearrange("p (b n h) -> p b n h", b=NS, n=NPG)), s)
            dve.tensor_tensor(z, lf, bfb[:, :].unsqueeze(1).to_broadcast([P, 5, NH]), ALU.add).then_inc(S("lf_z"), 1)
            dve.wait_ge(S("lf_act"), 3)
            dve.scalar_tensor_tensor(out=lf, in0=z, scalar=0.0, in1=e, op0=ALU.min, op1=ALU.subtract).then_inc(S("lf_done"), 1)
            dve.wait_ge(S("lf_done"), 1)
            dve.tensor_tensor(lgx[0:NS, :].rearrange("p (b h) -> p b h", h=NH), const[0:NS, K_E16:K_E16 + P].rearrange("p (b h) -> p b h", h=NH),
                              lf[0:NS, QT, :].unsqueeze(1).to_broadcast([NS, NS, NH]), ALU.mult).then_inc(S("lf_x"), 1)
            dve.wait_ge(S("lf_cq"), 1)
            dve.tensor_copy(cq, ps[:, 6, 0:QT * NH].rearrange("p (t h) -> p t h", t=QT))
            dve.wait_ge(S("lf_xt"), 1)
            dve.tensor_reduce(lfT[:, PAST:PAST + 1], ps[:, 7, 0:NS], AX.X, ALU.add).then_inc(S("lf_past"), 1)
            dve.wait_ge(S("lf_past"), 2)
            ch.link(dve.tensor_tensor_scan(cs, lfT, lfT, 0.0, ALU.add, ALU.bypass))
            dve.tensor_scalar(biasS, cs[:, 0:PAST], cs[:, PAST:PAST + 1], -1.0 / SCALE, ALU.subtract, ALU.mult)

        def pe_logf(pe):
            tri = const[:, K_TRI:K_TRI + 896]
            slot, before, _ = fill("logf", 0, 0)
            pe.wait_ge(S(f"ring_free{slot}"), before + 1)
            for n in range(NPG):
                ins = pe.transpose(ps[:, 4 + n // 4, (n % 4) * P:(n % 4) * P + P], cs[:, n * P:n * P + P], ident)
            ins.then_inc(S("lf_turn"), 1)
            pe.wait_ge(S("lf_done"), 1)
            for qt in range(QT):
                for kb in range(qt + 1):
                    x = P * (qt - kb) + 384
                    ins = pe.matmul(ps[:, 6, qt * NH:qt * NH + NH], tri[:, x:x + P], lf[:, kb, :], start=(kb == 0), stop=(kb == qt))
            ins.then_inc(S("lf_cq"), 1)
            for g in range(NKV):
                for kb in range(QT):
                    ins = pe.matmul(ps[64:68, g, kb * P:SEQ], lf[:, kb, GR * g:GR * g + GR], tri[:, 384:384 + SEQ - kb * P],
                                    start=(kb == 0), stop=(kb == QT - 1))
            ins.then_inc(S("lf_ck"), 1)
            pe.wait_ge(S("lf_x"), 1)
            pe.transpose(ps[:, 7, 0:NS], lgx[0:NS, :], ident[0:NS, 0:NS]).then_inc(S("lf_xt"), 1)

        NU = QT * GR

        def pe_attn(pe, l):
            tag, K = "at", HD + GR
            with pe.Fori(0, 2) as i:
                for par in range(2):
                    g = i * 2 + par
                    n = g + l * NKV
                    s = panel_ready(pe, f"q{l}", i, par)
                    pe.wait_ge(S(f"{tag}_end"), 1 + n)
                    for t in range(2):
                        ins = mm_tile(pe, s, t * P, P, 3 - t, hT, 0, KC, True, True)
                        if t == 0:
                            ins.then_inc(S(f"{tag}_mm"), 1)
                    panel_used(ins, s)
                    if l == 0:
                        for t in range(2):
                            pe.wait_ge(S(f"{tag}_raw"), n * 2 + t + 1)
                            for half in range(2):
                                ins = pe.matmul(ps[:, 2 * (1 - t) + half, 0:HT], swap, raw2[:, t, half * HT:half * HT + HT],
                                                start=True, stop=True)
                            ins.then_inc(S(f"{tag}_rot"), 1)
                    pe.wait_ge(S(f"{tag}_q"), 1 + n * 2 + 2)
                    for u in range(NU + 4):
                        if u < NU:
                            qt, hh = u // GR, u % GR
                            w = (qt + 1) * P
                            if u >= 2:
                                pe.wait_ge(S(f"{tag}_sm"), n * NU + u - 1)
                            pe.matmul(ps[:, u % 2, 0:w], qst[0:K, hh, qt * P:qt * P + P],
                                      kaug[0:K, ds(g, 1), 0:w].rearrange("p o t -> p (o t)"), start=True, stop=True)\
                                .then_inc(S(f"{tag}_s"), 1)
                        v = u - 1
                        if 0 <= v < NU:
                            qt = v // GR
                            pe.wait_ge(S(f"{tag}_p"), n * NU + v + 1)
                            if v >= 2:
                                pe.wait_ge(S(f"{tag}_pt"), n * NU + v - 1)
                            for kb in range(qt + 1):
                                ins = pe.transpose(ps[:, 2 + v % 2, kb * P:kb * P + P], Pr[:, v % 2, kb * P:kb * P + P], ident)
                            ins.then_inc(S(f"{tag}_tr"), 1)
                        v = u - 2
                        if 0 <= v < NU:
                            qt, hh = v // GR, v % GR
                            pe.wait_ge(S(f"{tag}_pt"), n * NU + v + 1)
                            if hh == 0 and qt >= 2:
                                pe.wait_ge(S(f"{tag}_on"), n * QT + qt - 1)
                            for kb in range(qt + 1):
                                ins = pe.matmul(ps[:, 4 + qt % 2, hh * HD:hh * HD + HD], PT[:, v % 2, kb * P:kb * P + P],
                                                Vt[:, kb, ds(g * HD, HD)], start=(kb == 0), stop=(kb == qt))
                            ins.then_inc(S(f"{tag}_o"), 1)
                        v = u - 4
                        if 0 <= v < NU and v % GR == GR - 1:
                            qt = v // GR
                            pe.wait_ge(S(f"{tag}_on"), n * QT + qt + 1)
                            if qt >= 2:
                                pe.wait_ge(S(f"{tag}_ot"), n * QT + qt - 1)
                            for t in range(2):
                                ins = pe.transpose(ps[:, 6 + qt % 2, t * P:t * P + P], On[:, qt % 2, t * P:t * P + P], ident)
                            ins.then_inc(S(f"{tag}_otr"), 1)

        def act_attn(act, l):
            tag = "at"
            with act.Fori(0, 2) as i:
                for par in range(2):
                    g = i * 2 + par
                    n = g + l * NKV
                    slot, before, _ = fill(f"q{l}", i, par)
                    for t in range(2):
                        if t == 0:
                            act.wait_ge(S(f"{tag}_mm"), n + 1)
                        else:
                            act.wait_ge(S(f"ring_free{slot}"), before + 1)
                        if l == 0:
                            act.activation(v520(raw2[:, t, :]), pair(3 - t), ACT.Copy).then_inc(S(f"{tag}_raw"), 1)
                        else:
                            act.wait_ge(S(f"{tag}_qall"), 1 + n)
                            act.activation(v520(qst[0:HD, 2 * t, :]), pair(3 - t, HD), ACT.Copy)
                            act.activation(v520(qst[0:HD, 2 * t + 1, :]), pair(3 - t, HD, HD), ACT.Copy).then_inc(S(f"{tag}_q"), 1)
                    for u in range(NU + 1):
                        if u < NU:
                            w = (u // GR + 1) * P
                            act.wait_ge(S(f"{tag}_nm"), n * NU + u + 1)
                            if u >= 2:
                                act.wait_ge(S(f"{tag}_tr"), n * NU + u - 1)
                            act.activation(Pr[:, u % 2, 0:w], Sm[:, u % 2, 0:w], ACT.Exp, bias=nm[:, u:u + 1],
                                           accum_out=lsum[:, u:u + 1]).then_inc(S(f"{tag}_p"), 1)
                        v = u - 1
                        if 0 <= v:
                            w = (v // GR + 1) * P
                            act.wait_ge(S(f"{tag}_tr"), n * NU + v + 1)
                            if v >= 2:
                                act.wait_ge(S(f"{tag}_o"), n * NU + v - 1)
                            act.activation(PT[:, v % 2, 0:w], ps[:, 2 + v % 2, 0:w], ACT.Copy).then_inc(S(f"{tag}_pt"), 1)

        def dve_attn(dve, l):
            tag = "at"
            with dve.Fori(0, 2) as i:
                for par in range(2):
                    g = i * 2 + par
                    n = g + l * NKV
                    if l == 0:
                        for t in range(2):
                            dve.wait_ge(S(f"{tag}_raw"), n * 2 + t + 1)
                            dve.wait_ge(S(f"{tag}_q"), 1 + n * 2 + t)
                            dve.wait_ge(S(f"{tag}_qall"), 1 + n)
                            dve.tensor_tensor(sq[:, 0, :], raw2[:, t, :], const[:, K_COS:K_COS + TOK], ALU.mult).then_inc(S(f"{tag}_rp"), 1)
                            dve.wait_ge(S(f"{tag}_rot"), n * 2 + t + 1)
                            dve.tensor_tensor(v520(sq[:, 1, :]), pair(1 - t), v520(const[:, K_SIN:K_SIN + TOK]), ALU.mult)\
                                .then_inc(S(f"{tag}_rp"), 1)
                            dve.wait_ge(S(f"{tag}_rp"), (n * 2 + t) * 2 + 2)
                            dve.tensor_tensor(qst[0:HD, 2 * t, :], sq[0:HD, 0, :], sq[0:HD, 1, :], ALU.add)
                            dve.tensor_tensor(qst[0:HD, 2 * t + 1, :], sq[HD:P, 0, :], sq[HD:P, 1, :], ALU.add).then_inc(S(f"{tag}_q"), 1)
                    for u in range(NU + 3):
                        if u < NU:
                            qt, hh = u // GR, u % GR
                            w = (qt + 1) * P
                            mask = maskP[:, qt, 0:w] if l == 0 else const[:, K_CAU + SEQ - w:K_CAU + SEQ]
                            dve.wait_ge(S(f"{tag}_s"), n * NU + u + 1)
                            if u >= 2:
                                dve.wait_ge(S(f"{tag}_p"), n * NU + u - 1)
                            if l == 0:
                                dve.wait_ge(S("tk_step"), g * NU + u + 1)
                            settle(dve)
                            if l == 0:
                                if u % 2 == 0:
                                    dve.max(small[0:NS, 0:8], scs[0:NS, :]).then_inc(S("tk_step"), 1)
                                else:
                                    dve.match_replace(scs[0:NS, :], small[0:NS, 0:8], scs[0:NS, :], TAKEN).then_inc(S("tk_step"), 1)
                            dve.tensor_tensor_reduce(Sm[:, u % 2, 0:w], ps[:, u % 2, 0:w], mask, SCALE, -3e38, ALU.add, ALU.max, mx[:, u:u + 1])\
                                .then_inc(S(f"{tag}_sm"), 1)
                            dve.wait_ge(S(f"{tag}_sm"), n * NU + u + 1)
                            if l == 0:
                                dve.tensor_scalar(nm[:, u:u + 1], mx[:, u:u + 1], -1.0, None, ALU.mult).then_inc(S(f"{tag}_nm"), 1)
                            else:
                                c = cq[:, qt, ds(g * GR + hh, 1)]
                                dve.tensor_tensor(mx[:, u:u + 1], mx[:, u:u + 1], c, ALU.add).then_inc(S(f"{tag}_mc"), 1)
                                dve.wait_ge(S(f"{tag}_mc"), g * NU + u + 1)
                                dve.tensor_tensor(nm[:, u:u + 1], c, mx[:, u:u + 1], ALU.subtract).then_inc(S(f"{tag}_nm"), 1)
                        v = u - 3
                        if v >= 0 and v % GR == GR - 1:
                            qt = v // GR
                            if qt >= 1:
                                dve_ot(dve, tag, g, n, qt - 1)
                            dve.wait_ge(S(f"{tag}_o"), n * NU + v + 1)
                            dve.reciprocal(rl[:, qt * GR:qt * GR + GR], lsum[:, qt * GR:qt * GR + GR]).then_inc(S(f"{tag}_rl"), 1)
                            dve.wait_ge(S(f"{tag}_rl"), n * QT + qt + 1)
                            dve.tensor_tensor(On[:, qt % 2, :].rearrange("p (h d) -> p h d", h=GR),
                                              ps[:, 4 + qt % 2, 0:PC].rearrange("p (h d) -> p h d", h=GR),
                                              rl[:, qt * GR:qt * GR + GR].unsqueeze(2).to_broadcast([P, GR, HD]), ALU.mult)\
                                .then_inc(S(f"{tag}_on"), 1)
                    dve_ot(dve, tag, g, n, QT - 1, S(f"{tag}_end"))
            if l == 0:
                assert 4 * NU == 2 * NSEL_S // 8
                dve.wait_ge(S("tk_step"), 1 + 4 * NU)
                dve.tensor_scalar(scs[0:NS, :], scs[0:NS, :], 0.5 * TAKEN, NEG, ALU.is_gt, ALU.mult)

        def dve_ot(dve, tag, g, n, qt, also=None):
            dve.wait_ge(S(f"{tag}_otr"), n * QT + qt + 1)
            ins = dve.tensor_copy(OT[:, ds(g * 2, 2), qt * P:qt * P + P],
                                  ps[:, 6 + qt % 2, 0:PC].rearrange("p (t c) -> p t c", t=2))
            ins.then_inc(S(f"{tag}_ot"), 1)
            if also is not None:
                dve.wait_ge(S(f"{tag}_ot"), n * QT + QT)
                dve.sem_inc(also, 1)

        def pool_attn(pool, l):
            tag = "at"
            for j in range(2):
                gather(pool, f"K{l}", 0, j, I[f"cache_k_{'ab'[l]}"], j, PC)
            with pool.Fori(0, 2) as i:
                for par in range(2):
                    g = i * 2 + par
                    n = g + l * NKV
                    pool.wait_ge(S(f"{tag}_q"), 1 + n * 2 + 2)
                    dst = Qall[64 * par:64 * par + 64, ds(i, 1), :].rearrange("p o (b h) -> p (o b) h", h=NH)
                    for hh in range(GR):
                        ins = pool.tensor_copy(dst[:, :, ds(g * GR + hh, 1)].rearrange("p b o -> p (b o)"), qst[0:HD, hh, SEQ:TOK])
                    ins.then_inc(S(f"{tag}_qall"), 1)
                    pool.wait_ge(S(f"{tag}_qall"), 1 + n + 1)

        def pe_samp(pe, l):
            tag = f"sp{l}"
            for c in range(2):
                if l == 0:
                    pe.matmul(ps[:, 4 + c, :], const[0:NS, K_E16:K_E16 + P], by_token(biasS)[0:NS, 4 * c:4 * c + 4, :], start=True, stop=False)
                else:
                    pe.matmul(ps[:, 4 + c, :], ident, by_token(biasS)[:, 4 * c:4 * c + 4, :], start=True, stop=False)
            with pe.Fori(0, 4) as i:
                for j in range(2):
                    b = i * 2 + j
                    s = panel_ready(pe, f"K{l}", i, j)
                    for c in range(4):
                        pe.wait_ge(S(f"{tag}_kt"), 1 + b * 4)
                        for n in range(4):
                            pg = 4 * (c % 2) + n
                            ins = pe.transpose(ps[:, c, n * P:n * P + P], pages_view(s, PC)[:, pg, (c // 2) * P:(c // 2) * P + P], ident)
                        if c < 3:
                            ins.then_inc(S(f"{tag}_ktr"), 1)
                    panel_used(ins, s)
                    pe.wait_ge(S(f"{tag}_qz"), b + 1)
                    for c in range(4):
                        pe.wait_ge(S(f"{tag}_kt"), 1 + b * 4 + c + 1)
                        ins = pe.matmul(ps[:, 4 + c % 2, :], qz[:, j, c // 2, :], KT[:, c, 0:512], start=False, stop=False)
                    ins.then_inc(S(f"{tag}_qk"), 1)
            for c in range(2):
                pe.matmul(ps[:, 4 + c, :], zeros, const[:, 0:512], start=False, stop=True)
            for half in range(2):
                ins = pe.matmul(ps[:, 6, 0:NS], Qall[:, half, :], knT[:, half, :], start=(half == 0), stop=(half == 1))
            if l == 0:
                ins = pe.matmul(ps[:, 6, 16:17], const[0:NS, K_E16:K_E16 + P], maskS[0:NS, :], start=True, stop=True)
            ins.then_inc(S(f"{tag}_logits"), 1)
            pe.wait_ge(S(f"{tag}_pb"), 1)
            for n in range(NPG):
                ins = pe.transpose(ps[:, n // 4, (n % 4) * P:(n % 4) * P + P], Pb[:, n * P:n * P + P], ident)
            pe.transpose(ps[0:NS, 2, 0:P], pnx, ident).then_inc(S(f"{tag}_ptr"), 1)
            pe.wait_ge(S(f"{tag}_pts"), 2)
            for half in range(2):
                rhs = pnT[0:NS, :].rearrange("p (b h) -> p b h", h=NH)[:, :, 8 * half:8 * half + 8]
                ins = pe.matmul(ps[:, 6, 64 * half:64 * half + 64].rearrange("p (b h) -> p b h", h=8), vnew[0:NS, half * P:half * P + P], rhs,
                                start=True, stop=True)
            with pe.Fori(0, 4) as i:
                for j in range(2):
                    b = i * 2 + j
                    s = panel_ready(pe, f"V{l}", i, j)
                    for half in range(2):
                        for n in range(NPG):
                            ins = pe.matmul(ps[:, 7, ds(b * 8 + 64 * half, 8)], pages_view(s, PC)[:, n, half * P:half * P + P],
                                            PTs[:, n, ds(b * NH + 8 * half, 8)], start=(n == 0), stop=(n == NPG - 1))
                    panel_used(ins, s)
            pe.drain().then_inc(S(f"{tag}_ov"), 1)

        def act_samp(act, l):
            tag = f"sp{l}"
            with act.Fori(0, 4) as i:
                for j in range(2):
                    b = i * 2 + j
                    slot, before, _ = fill(f"K{l}", i, j)
                    act.wait_ge(S(f"{tag}_qk"), 1 + b)
                    for c in range(4):
                        if c < 3:
                            act.wait_ge(S(f"{tag}_ktr"), b * 3 + c + 1)
                        else:
                            act.wait_ge(S(f"ring_free{slot}"), before + 1)
                        act.activation(KT[:, c, 0:512], ps[:, c, :], ACT.Copy).then_inc(S(f"{tag}_kt"), 1)
            act.wait_ge(S(f"{tag}_nm"), 1)
            act.activation(Pb.rearrange("p (a c) -> p a c", a=2), ps[:, 4:6, :], ACT.Exp, bias=ssm[:, 2:3], scale=SCALE,
                           accum_out=ssm[:, 3:4]).then_inc(S(f"{tag}_e"), 1)
            act.activation(ssm[:, 4:5], ssm[:, 0:1], ACT.Exp, bias=ssm[:, 2:3], scale=SCALE).then_inc(S(f"{tag}_e"), 1)
            act.wait_ge(S(f"{tag}_ptr"), 1)
            act.activation(PTs.rearrange("p (a j) c -> p a (j c)", a=2), ps[:, 0:2, :], ACT.Copy).then_inc(S(f"{tag}_pts"), 1)
            act.activation(pnT[0:NS, :], ps[0:NS, 2, 0:P], ACT.Copy).then_inc(S(f"{tag}_pts"), 1)

        def pool_samp(pool, l):
            tag = f"sp{l}"
            K, V = (I[f"cache_{x}_{'ab'[l]}"] for x in "kv")

            def zeroed(i):
                for j in range(2):
                    pool.wait_ge(S(f"{tag}_qk"), 1 + i * 2)
                    for half in range(2):
                        ins = pool.tensor_tensor(qz[:, j, half, :], Qall[:, half, :],
                                                 colmask[:, ds(i * 2 + j, 1), :].rearrange("p o c -> p (o c)"), ALU.mult)
                    ins.then_inc(S(f"{tag}_qz"), 1)

            for j in range(2):
                gather(pool, f"V{l}", 0, j, V, j, PC)
            for i in range(3):
                zeroed(i)
                for j in range(2):
                    gather(pool, f"K{l}", i + 1, j, K, (i + 1) * 2 + j, PC)
            zeroed(3)
            for i in range(3):
                for j in range(2):
                    gather(pool, f"V{l}", i + 1, j, V, (i + 1) * 2 + j, PC)

        def dve_samp(dve, l):
            tag = f"sp{l}"
            ch = Chain(dve)
            dve.wait_ge(S(f"{tag}_logits"), 1)
            ch.link(dve.tensor_tensor_reduce(ssm[:, 8:16], ps[:, 6, 0:NS], diag16, 1.0, 0.0, ALU.mult, ALU.add, ssm[:, 0:1]))
            if l == 0:
                ch.link(dve.tensor_tensor(ssm[:, 0:1], ssm[:, 0:1], ps[:, 6, 16:17], ALU.add))
            ch.link(dve.tensor_reduce(ssm[:, 1:2], ps[:, 4:6, :], AX.XY, ALU.max))
            ch.link(dve.tensor_tensor(ssm[:, 1:2], ssm[:, 1:2], ssm[:, 0:1], ALU.max))
            dve.tensor_scalar(ssm[:, 2:3], ssm[:, 1:2], -SCALE, None, ALU.mult).then_inc(S(f"{tag}_nm"), 1)
            dve.wait_ge(S(f"{tag}_e"), 2)
            ch.link(dve.tensor_tensor(ssm[:, 3:4], ssm[:, 3:4], ssm[:, 4:5], ALU.add))
            ch.link(dve.reciprocal(ssm[:, 5:6], ssm[:, 3:4]))
            ch.link(dve.tensor_tensor(ssm[:, 4:5], ssm[:, 4:5], ssm[:, 5:6], ALU.mult))
            dve.tensor_scalar(pnx, diag16, ssm[:, 4:5], None, ALU.mult)
            dve.tensor_scalar(Pb, Pb, ssm[:, 5:6], None, ALU.mult).then_inc(S(f"{tag}_pb"), 1)
            dve.wait_ge(S(f"{tag}_ov"), 1)
            ch.link(dve.tensor_copy(ovs, ps[:, 6, 0:P]))
            ch.link(dve.tensor_tensor(ovs, ovs, ps[:, 7, 0:P], ALU.add))
            o = ovs.rearrange("p (a b h) -> p a h b", a=2, h=8)
            for half in range(2):
                for lo in range(2):
                    for odd in range(2):
                        dve.tensor_copy(OT[64 * odd:64 * odd + 64, 4 * half + 2 * lo:4 * half + 2 * lo + 2, SEQ:TOK],
                                        o[64 * lo:64 * lo + 64, half, 4 * lo + odd:4 * lo + 4:2, :])

        def residual(dve, ch, l, chunk, m, p, gate=None):
            row = ada[:, ds(l * NADA + chunk * KC + m, 1), :].rearrange("p o c -> p (o c)")
            x = xT[:, ds(m, 1), :].rearrange("p o t -> p (o t)")
            dve.scalar_tensor_tensor(out=x[:, 0:HT], in0=ps[:, 2 * p, 0:HT], scalar=row[:, 0:1], in1=x[:, 0:HT], op0=ALU.mult, op1=ALU.add)
            dve.scalar_tensor_tensor(out=x[:, HT:SEQ], in0=ps[:, 2 * p + 1, 0:SEQ - HT], scalar=row[:, 0:1], in1=x[:, HT:SEQ],
                                     op0=ALU.mult, op1=ALU.add)
            ch(dve.tensor_tensor(tmp8[:, :], ps[:, 2 * p + 1, SEQ - HT:HT], row[:, 1:CC], ALU.mult))
            return dve.tensor_tensor(x[:, SEQ:TOK], x[:, SEQ:TOK], tmp8[:, :], ALU.add)

        def pe_out(pe, l):
            for j in range(4):
                s = panel_ready(pe, f"o{l}", 0, j)
                for t in range(2):
                    m = 2 * j + t
                    if m >= 4:
                        pe.wait_ge(S(f"o{l}_res"), m - 3)
                    ins = mm_tile(pe, s, t * P, P, m % 4, OT, 0, KC, True, True)
                    if t == 0:
                        ins.then_inc(S(f"o{l}_even"), 1)
                panel_used(ins, s)

        def dve_out(dve, l):
            ch = Chain(dve)
            for m in range(KC):
                if m % 2 == 0:
                    dve.wait_ge(S(f"o{l}_even"), m // 2 + 1)
                else:
                    slot, before, _ = fill(f"o{l}", 0, m // 2)
                    dve.wait_ge(S(f"ring_free{slot}"), before + 1)
                residual(dve, ch.link, l, 2, m, m % 4).then_inc(S(f"o{l}_res"), 1)
                dve.wait_ge(S(f"o{l}_res"), m + 1)

        def pe_up(pe, l):
            tag = f"up{l}"

            def ada_products(i, q, t):
                s = panel_ready(pe, "ada1", i, 2 * q + t)
                ada_tiles(pe, s, 4 * t, HT + 2)

            def two(sec, i, q):
                sa = panel_ready(pe, sec, i, 2 * q)
                for t in range(2):
                    if t == 0:
                        sb_ = panel_ready(pe, sec, i, 2 * q + 1)
                    f = (i * 2 + q) * 2 + t if sec == tag else 20 + t
                    pe.wait_ge(S("up_afree"), l * FC + f + 1)
                    if l == 0:
                        ada_products(i, q, t) if sec == tag else ada_products(5, 0, t)
                    ins = mm_tile(pe, sa, t * P, P, 2 * t, hT, 0, KC, True, True)
                    ins.then_inc(S("up_a"), 1)
                    pe.wait_ge(S("up_bfree"), l * FC + f + 1)
                    ins = mm_tile(pe, sb_, t * P, P, 2 * t + 1, hT, 0, KC, True, True)
                    ins.then_inc(S("up_b"), 1)

            with pe.Fori(0, 5) as i:
                two(tag, i, 0)
                two(tag, i, 1)
            two(f"{tag}t", 0, 0)
            if l == 0:
                for t in range(2):
                    pe.wait_ge(S("up_afree"), FC + t + 1)
                    s = panel_ready(pe, "ada1", 5, 2 + t)
                    ada_tiles(pe, s, 4 * t, HT + 2)
            pe.wait_ge(S("up_acv"), 1 + l * FC + FC)
            pe.wait_ge(S("up_bfree"), l * FC + FC + 2)
            pe.wait_ge(S("up_afree"), l * FC + FC + 2)
            if l == 0:
                pe.wait_ge(S("up_ada"), 2)
            for q in range(NCV):
                if q >= 2:
                    pe.wait_ge(S("up_cvo"), l * NCV + q - 1)
                for n in range(min(4, FC - 4 * q)):
                    ins = pe.transpose(ps[0:10, q % 2, n * P:n * P + P], acv[:, 4 * q + n, :], ident)
                ins.then_inc(S("up_cvt"), 1)

        def act_up(act, l):
            tag = f"up{l}"
            if l == 0:
                act.sem_inc(S("up_afree"), 2)

            def tile(f, t):
                fr = ds(f, 1)
                act.wait_ge(S("up_a"), l * FC + f + 1)
                act.wait_ge(S("up_c3"), 1 + l * FC + f)
                act.wait_ge(S("up_acv"), 1 + l * FC + f)
                act.wait_ge(S("up_bfree"), l * FC + f + 1)
                if l == 0:
                    ada_result(act, 4 * t, HT + 2, f, NADA)
                act.activation(v520(aS[:, t, 2:2 + TOK]), pair(2 * t), ACT.Copy).then_inc(S("up_afree"), 1)
                act.wait_ge(S("up_afree"), l * FC + f + 3)
                cw = cwT[:, fr, :].rearrange("p o c -> p (o c)")
                act.activation(cvA[:, t, 0:SEQ], aS[:, t, 0:SEQ], ACT.Identity, scale=cw[:, 20 * l + 16:20 * l + 17],
                               bias=cw[:, 20 * l + 19:20 * l + 20]).then_inc(S("up_c1"), 1)
                act.wait_ge(S("up_c3"), 1 + l * FC + f + 1)
                act.activation(cvA[:, t, :], cvA[:, t, :], ACT.Silu).then_inc(S("up_silu"), 1)

            with act.Fori(0, 5) as i:
                for q in range(4):
                    tile(i * 4 + q, q % 2)
            for q in range(2):
                tile(20 + q, q)
            if l == 0:
                for t in range(2):
                    s, before, _ = fill("ada1", 5, 2 + t)
                    act.wait_ge(S(f"ring_free{s}"), before + 1)
                    ada_result(act, 4 * t, HT + 2, FC + t, NADA).then_inc(S("up_ada"), 1)
            for q in range(NCV):
                n = min(4, FC - 4 * q)
                act.wait_ge(S("up_cvt"), l * NCV + q + 1)
                act.activation(cvrow[0:10, 4 * q * P:(4 * q + n) * P], ps[0:10, q % 2, 0:n * P], ACT.Copy).then_inc(S("up_cvo"), 1)
            act.wait_ge(S("up_cvo"), l * NCV + NCV)
            act.dma_start(O["conv_p"][l], cvrow[0:2, :]).then_inc(S("stores"), 16)
            act.dma_start(O["conv_s"][l, :, 1, :], cvrow[2:10, :]).then_inc(S("stores"), 16)
            act.dma_start(O["conv_s"][l, :, 0, :], I["state_conv"][l, :, 1, :]).then_inc(S("stores"), 16)

        def dve_up(dve, l):
            tag = f"up{l}"
            if l == 0:
                dve.sem_inc(S("up_bfree"), 2)

            def tile(f, t, sec, q):
                fr = ds(f, 1)
                cw = cwT[:, fr, :].rearrange("p o c -> p (o c)")
                w1, w2 = cw[:, 20 * l + 17:20 * l + 18], cw[:, 20 * l + 18:20 * l + 19]
                dve.wait_ge(S("up_c1"), l * FC + f + 1)
                dve.scalar_tensor_tensor(out=cvA[:, t, 0:SEQ], in0=aS[:, t, 1:SEQ + 1], scalar=w1, in1=cvA[:, t, 0:SEQ],
                                         op0=ALU.mult, op1=ALU.add).then_inc(S("up_c2"), 1)
                dve.scalar_tensor_tensor(out=cvA[:, t, SEQ:TOK], in0=aS[:, t, SEQ + 2:TOK + 2], scalar=w2,
                                         in1=cs0[:, l, fr, :].rearrange("p o c -> p (o c)"), op0=ALU.mult, op1=ALU.add)
                dve.wait_ge(S("up_c2"), l * FC + f + 1)
                dve.scalar_tensor_tensor(out=cvA[:, t, 0:SEQ], in0=aS[:, t, 2:SEQ + 2], scalar=w2, in1=cvA[:, t, 0:SEQ],
                                         op0=ALU.mult, op1=ALU.add).then_inc(S("up_c3"), 1)
                dve.wait_ge(S("up_silu"), l * FC + f + 1)
                dve.wait_ge(S("up_b"), l * FC + f + 1)
                if t == 1:
                    for n in range(2):
                        dve.sem_inc(S(f"ring_free{RING[sec][0][2 * q + n][0]}"), 1)
                dve.tensor_tensor(v520(gT[:, fr, :].rearrange("p o t -> p (o t)")), pair(2 * t + 1), v520(cvA[:, t, :]), ALU.mult)\
                    .then_inc(S("up_bfree"), 1)

            with dve.Fori(0, 5) as i:
                for q in range(4):
                    tile(i * 4 + q, q % 2, tag, q // 2)
            for q in range(2):
                tile(20 + q, q, f"{tag}t", 0)

        def pool_up(pool, l):
            tag = f"up{l}"

            def tile(f, t):
                pool.wait_ge(S("up_c1"), l * FC + f + 1)
                pool.tensor_copy(acv[:, ds(f, 1), :].rearrange("p o c -> p (o c)"), aS[:, t, SEQ:SEQ + 10]).then_inc(S("up_acv"), 1)

            with pool.Fori(0, 5) as i:
                for q in range(4):
                    tile(i * 4 + q, q % 2)
            for q in range(2):
                tile(20 + q, q)

        def pe_down(pe, l):
            tag = f"dn{l}"
            with pe.Fori(0, 2) as i:
                for q in range(2):
                    for t in range(2):
                        pe.wait_ge(S(f"{tag}_free"), i * 4 + q * 2 + t + 1)
                    for n in range(3):
                        s = panel_ready(pe, tag, i, 3 * q + n)
                        nk = min(8, FC - 8 * n)
                        for t in range(2):
                            ins = mm_tile(pe, s, t * P, P, 2 * q + t, gT, 8 * n, nk, n == 0, n == 2)
                        panel_used(ins, s)

        def dve_down(dve, l):
            tag = f"dn{l}"
            dve.sem_inc(S(f"{tag}_free"), 4)
            with dve.Fori(0, 2) as i:
                for q in range(2):
                    slot, before, _ = fill(tag, i, 3 * q + 2)
                    dve.wait_ge(S(f"ring_free{slot}"), before + 1)
                    for t in range(2):
                        m = i * 4 + q * 2 + t

                        def link(ins, m=m):
                            ins.then_inc(S(f"{tag}_dve"), 1)
                            dve.wait_ge(S(f"{tag}_dve"), m + 1)
                        residual(dve, link, l, 5, m, 2 * q + t).then_inc(S(f"{tag}_free"), 1)
                        dve.wait_ge(S(f"{tag}_free"), m + 5)

        FIN_GROUPS = 2 * QT + 2

        @block.tensor
        def _(pe):
            pe.wait_ge(S("in_const"), 16)
            pe.wait_ge(S("in_vec"), 96)
            for kc in range(KC):
                pe.transpose(ps[:, 0, kc * CC:kc * CC + CC], cload[0:CC, kc * P:kc * P + P], ident[0:CC, 0:CC])
            pe.transpose(ps[:, 1, 0:96], vrow[0:96, :], ident[0:96, 0:96])
            pe.transpose(ps[:, 1, 96:136], vrow2[0:40, :], ident[0:40, 0:40]).then_inc(S("pr_vec"), 1)
            pe.wait_ge(S("in_x"), 32)
            for kc in range(KC):
                if kc >= 2:
                    pe.wait_ge(S("pr_xe"), 2 * (kc - 1))
                b = 2 + 2 * (kc % 2)
                for t in range(QT):
                    pe.transpose(ps[:, b, t * P:t * P + P], xload[:, t, kc * P:kc * P + P], ident)
                pe.transpose(ps[:, b + 1, 0:NS], xsload[0:NS, kc * P:kc * P + P], ident[0:NS, 0:NS]).then_inc(S("pr_x"), 1)
            pe.wait_ge(S("in_conv"), 96)
            for f in range(FC):
                ins = pe.transpose(ps[:, 6 + f // 11, (f % 11) * 40:(f % 11) * 40 + 40], crow[0:40, f * P:f * P + P], ident[0:40, 0:40])
            ins.then_inc(S("pr_cw"), 1)
            pe.wait_ge(S("pr_tab"), 1)
            pe.matmul(ps[:, 1, 256:256 + NS], const[0:NPG, K_E16:K_E16 + P], tablef[:, :], start=True, stop=True).then_inc(S("pr_pages"), 1)
            phase_end(pe, "pe")
            pe_ada(pe, "ada0a", 2, "ad0")
            phase_end(pe, "pe")
            for l in range(DEPTH):
                pe_rms(pe, 2 * l)
                phase_end(pe, "pe")
                pe_head(pe, l)
                phase_end(pe, "pe")
                if l == 0:
                    pe_score(pe)
                    phase_end(pe, "pe")
                    pe_ada(pe, "ada0b", 4, "ad1")
                else:
                    pe_logf(pe)
                phase_end(pe, "pe")
                pe_attn(pe, l)
                phase_end(pe, "pe")
                pe_samp(pe, l)
                phase_end(pe, "pe")
                pe_out(pe, l)
                phase_end(pe, "pe")
                pe_rms(pe, 2 * l + 1)
                phase_end(pe, "pe")
                pe_up(pe, l)
                phase_end(pe, "pe")
                pe_down(pe, l)
                phase_end(pe, "pe")
            pe_rms(pe, 4)
            phase_end(pe, "pe")
            for n in range(FIN_GROUPS):
                t, half = n // 2, n % 2
                if n >= 4:
                    pe.wait_ge(S("fi_y"), n - 3)
                for k in range(4):
                    if t < QT:
                        ins = pe.transpose(ps[:, n % 4, k * P:k * P + P], hT[:, 4 * half + k, t * P:t * P + P], ident)
                    else:
                        ins = pe.transpose(ps[0:NS, n % 4, k * P:k * P + P], hT[:, 4 * half + k, SEQ:TOK], ident)
                ins.then_inc(S("fi_t"), 1)
            phase_end(pe, "pe")

        @block.scalar
        def _(act):
            act.dma_start(xload, I["x_prompt"][0].rearrange("(t p) d -> p t d", p=P)).then_inc(S("in_x"), 16)
            act.dma_start(xsload[0:NS, :], I["x_sample"].rearrange("b o d -> (b o) d")).then_inc(S("in_x"), 16)
            for l in range(DEPTH):
                act.dma_start(crow[20 * l:20 * l + 16, :], I["state_conv"][l].rearrange("b w f -> (b w) f")).then_inc(S("in_conv"), 16)
                act.dma_start(crow[20 * l + 16:20 * l + 19, :], I["conv_w"][l]).then_inc(S("in_conv"), 16)
                act.dma_start(crow[20 * l + 19:20 * l + 20, :], I["conv_b"][l:l + 1, :]).then_inc(S("in_conv"), 16)
            act.dma_start(table[:, :], I["page_table"].rearrange("b j -> j b"), allow_slow_non_contiguous=True).then_inc(S("in_table"), 16)
            act.dma_start(bfb[:, :], I["b_f"].partition_broadcast(P)).then_inc(S("in_bf"), 16)
            act.wait_ge(S("pr_vec"), 1)
            act.activation(cT[:, :, :], ps[:, 0, 0:KC * CC].rearrange("p (k c) -> p k c", k=KC), ACT.Silu)
            act.activation(badaT[:, :], ps[:, 1, 0:96], ACT.Copy)
            act.activation(vT[:, :], ps[:, 1, 96:136], ACT.Copy)
            for kc in range(KC):
                act.wait_ge(S("pr_x"), kc + 1)
                act.activation(xT[:, kc, 0:SEQ], ps[:, 2 + 2 * (kc % 2), :], ACT.Copy).then_inc(S("pr_xe"), 1)
                act.activation(xT[:, kc, SEQ:TOK], ps[:, 3 + 2 * (kc % 2), 0:NS], ACT.Copy).then_inc(S("pr_xe"), 1)
            act.wait_ge(S("pr_cw"), 1)
            for h in range(2):
                act.activation(cwT[:, 11 * h:11 * h + 11, :], ps[:, 6 + h, 0:440].rearrange("p (k c) -> p k c", k=11), ACT.Copy)\
                    .then_inc(S("pr_cwe"), 1)
            phase_end(act, "act")
            act_ada(act, "ada0a", 2, 0, "ad0")
            phase_end(act, "act")
            for l in range(DEPTH):
                base = l * NADA
                act_rms(act, 2 * l, ada[:, base:base + KC, :], None)
                phase_end(act, "act")
                act_head(act, l)
                phase_end(act, "act")
                if l == 0:
                    act_score(act)
                    phase_end(act, "act")
                    act_ada(act, "ada0b", 4, 2 * KC, "ad1")
                else:
                    act_logf(act)
                phase_end(act, "act")
                act_attn(act, l)
                phase_end(act, "act")
                act_samp(act, l)
                phase_end(act, "act")
                phase_end(act, "act")
                act_rms(act, 2 * l + 1, ada[:, base + 3 * KC:base + 4 * KC, :], None)
                phase_end(act, "act")
                act_up(act, l)
                phase_end(act, "act")
                act.wait_ge(S("stores"), 16 * STORES[2 * l + 1])
                phase_end(act, "act")
            act_rms(act, 4, None, vT[:, 32:40])
            phase_end(act, "act")
            for n in range(FIN_GROUPS):
                t, half = n // 2, n % 2
                act.wait_ge(S("fi_t"), n + 1)
                if t < QT:
                    if t >= 2 and half == 0:
                        act.wait_ge(S(f"fi_out{t % 2}"), 16 * (t // 2))
                    act.activation(ytok[:, t % 2, half * 512:half * 512 + 512], ps[:, n % 4, :], ACT.Copy).then_inc(S("fi_y"), 1)
                    if half == 1:
                        act.wait_ge(S("fi_y"), n + 1)
                        act.dma_start(O["y_p"][t * P:t * P + P, :], ytok[:, t % 2, :]).then_inc(S(f"fi_out{t % 2}"), 16)
                else:
                    act.activation(ysam[0:NS, half * 512:half * 512 + 512], ps[0:NS, n % 4, :], ACT.Copy).then_inc(S("fi_y"), 1)
            act.wait_ge(S("fi_y"), FIN_GROUPS)
            act.dma_start(O["y_s"], ysam[0:NS, :]).then_inc(S("stores"), 16)
            act.wait_ge(S("fi_out0"), 32)
            act.wait_ge(S("fi_out1"), 32)
            act.wait_ge(S("stores"), 16 * STORES[4])
            phase_end(act, "act")

        @block.vector
        def _(dve):
            ch = Chain(dve)
            dve.memset(epsc[:, :], EPS)
            dve.memset(ones[:, :], 1.0)
            dve.memset(zeros[:, :], 0.0)
            dve.wait_ge(S("in_table"), 16)
            dve.tensor_copy(tablef[:, :], table[:, :]).then_inc(S("pr_tab"), 1)
            dve.wait_ge(S("pr_pages"), 1)
            dve.tensor_scalar(idx[:, :], ps[:, 1, 256:256 + NS], 16.0, const[:, K_B16:K_B16 + 1], ALU.mult, ALU.add)
            dve.wait_ge(S("pr_cwe"), 2)
            for l in range(DEPTH):
                c = cwT[:, :, 20 * l:20 * l + 20]
                st0, st1 = c[:, :, 0:16:2], c[:, :, 1:16:2]

                def tap(n, c=c):
                    return c[:, :, n:n + 1].to_broadcast([P, FC, NS])
                u = sq[:, 0, 0:FC * NS].rearrange("p (k c) -> p k c", k=FC)
                ch.link(dve.tensor_tensor(cs0[:, l, :, :], st0, tap(16), ALU.mult))
                ch.link(dve.tensor_tensor(u, st1, tap(17), ALU.mult))
                ch.link(dve.tensor_tensor(cs0[:, l, :, :], cs0[:, l, :, :], u, ALU.add))
                ch.link(dve.tensor_tensor(cs0[:, l, :, :], cs0[:, l, :, :], tap(19), ALU.add))
            phase_end(dve, "dve")
            phase_end(dve, "dve")
            for l in range(DEPTH):
                base = l * NADA
                dve_rms(dve, 2 * l, ada[:, base:base + KC, :], ada[:, base + KC:base + 2 * KC, :], vT[:, 8 * l:8 * l + 8])
                phase_end(dve, "dve")
                if l == 1:
                    dve.wait_ge(S("in_bf"), 16)
                dve_head(dve, l)
                phase_end(dve, "dve")
                if l == 0:
                    dve_score(dve)
                    phase_end(dve, "dve")
                    dve_topk(dve)
                else:
                    dve_logf(dve)
                phase_end(dve, "dve")
                dve_attn(dve, l)
                phase_end(dve, "dve")
                dve_samp(dve, l)
                phase_end(dve, "dve")
                dve_out(dve, l)
                phase_end(dve, "dve")
                dve_rms(dve, 2 * l + 1, ada[:, base + 3 * KC:base + 4 * KC, :], ada[:, base + 4 * KC:base + 5 * KC, :],
                        vT[:, 16 + 8 * l:24 + 8 * l])
                phase_end(dve, "dve")
                dve_up(dve, l)
                phase_end(dve, "dve")
                dve_down(dve, l)
                phase_end(dve, "dve")
            dve_rms(dve, 4, None, None, None)
            phase_end(dve, "dve")
            phase_end(dve, "dve")

        @block.gpsimd
        def _(pool):
            for name in CREDITED:
                pool.sem_inc(S(name), 1)
            pool.memset(colmask[:, :, :], 0.0).then_inc(S("pl_z"), 1)
            pool.memset(colmask8[:, :, :], 0.0).then_inc(S("pl_z"), 1)
            pool.wait_ge(S("pl_z"), 2)
            for b in range(NS):
                pool.memset(colmask[:, b, b * NH:b * NH + NH], 1.0)
                pool.memset(colmask8[:, b, b * NIH:b * NIH + NIH], 1.0)
            phase_end(pool, "pool")
            phase_end(pool, "pool")
            for l in range(DEPTH):
                in_turn(pool, pool.memset(Qall[:, :, :], 0.0))
                if l == 1:
                    in_turn(pool, pool.memset(lf[:, :, :], 0.0))
                else:
                    in_turn(pool, pool.memset(kaug[64:68, :, 0:SEQ], 0.0))
                pool.dma_start(qst[HD:HD + GR, :, 0:SEQ], I["hsel"]).then_inc(S("in_hsel"), 16)
                pool.wait_ge(S("in_hsel"), 16 * (l + 1))
                phase_end(pool, "pool")
                pool_head(pool, l)
                if l == 1:
                    slot_free(pool, "logf", 0, 0)
                    for b in range(NS):
                        gather_logf(pool, b)
                phase_end(pool, "pool")
                if l == 0:
                    pool_score(pool)
                    phase_end(pool, "pool")
                phase_end(pool, "pool")
                pool_attn(pool, l)
                phase_end(pool, "pool")
                pool_samp(pool, l)
                phase_end(pool, "pool")
                phase_end(pool, "pool")
                for t in range(2):
                    pool.memset(aS[:, t, 0:2], 0.0)
                phase_end(pool, "pool")
                pool_up(pool, l)
                phase_end(pool, "pool")
                phase_end(pool, "pool")
            phase_end(pool, "pool")
            phase_end(pool, "pool")


def _constants():
    f = np.float32
    c = np.zeros((P, K_N), f)
    c[:, K_ID:K_ID + P] = np.eye(P, dtype=f)
    half = HD // 4 // 2
    pos = np.concatenate([np.arange(SEQ), np.full(NS, PAST)]).astype(f)
    inv = (f(500000.0) ** (-np.arange(half, dtype=f) / f(half))).astype(f)
    ang = (pos[None, :] * inv[:, None]).astype(f)
    c[:, K_COS:K_COS + TOK] = 1.0
    for p in range(P):
        d = p % HD
        if d < 2 * half:
            c[p, K_ROT + (p ^ half)] = 1.0
            c[p, K_COS:K_COS + TOK] = np.cos(ang[d % half])
            c[p, K_SIN:K_SIN + TOK] = np.sin(ang[d % half]) * (-1.0 if d < half else 1.0)
    p = np.arange(P)[:, None]
    c[:, K_TRI:K_TRI + 896] = p <= np.arange(896)[None, :] - 384
    c[:, K_CAU:K_CAU + 512] = np.where(np.arange(512)[None, :] - 384 <= p, 0.0, NEG)
    c[:, K_D16:K_D16 + 8] = p // 16 == np.arange(8)[None, :]
    c[:, K_D8:K_D8 + 8] = p // 8 == np.arange(8)[None, :]
    c[:, K_E16:K_E16 + 128] = p == np.arange(128)[None, :] // 16
    c[:, K_E8:K_E8 + 64] = p == np.arange(64)[None, :] // 8
    c[:, K_B16] = np.arange(P) % 16
    hsel = np.zeros((GR, GR, SEQ), f)
    hsel[np.arange(GR), np.arange(GR), :] = 1.0
    return c, hsel


_POOL_PAGES = None
_INS = ["x_prompt", "x_sample", "cache_k_a", "cache_v_a", "cache_kidx_a", "cache_k_b", "cache_v_b", "cache_logf_b",
        "state_conv", "page_table", "c_prompt", "c_sample", "w_ada", "b_ada", "g_mix", "g_ffn", "w_in_a", "w_o_a",
        "w_in_b", "b_f", "w_o_b", "w_up", "conv_w", "conv_b", "w_down", "g_final"]
_OUTS = [("y_p", (SEQ, D), (1, SEQ, D)), ("y_s", (NS, D), (NS, 1, D)),
         ("k_a_p", (SEQ, PC), (1, 1, SEQ, NKV, HD)), ("v_a_p", (SEQ, PC), (1, 1, SEQ, NKV, HD)),
         ("kidx_p", (SEQ, HD), (1, 1, SEQ, HD)),
         ("k_b_p", (SEQ, PC), (1, 1, SEQ, NKV, HD)), ("v_b_p", (SEQ, PC), (1, 1, SEQ, NKV, HD)),
         ("logf_p", (SEQ, NH), (1, 1, SEQ, NH)), ("conv_p", (DEPTH, CW - 1, FF), (DEPTH, 1, CW - 1, FF)),
         ("k_a_s", (NS, PC), (1, NS, 1, NKV, HD)), ("v_a_s", (NS, PC), (1, NS, 1, NKV, HD)),
         ("kidx_s", (NS, HD), (1, NS, 1, HD)),
         ("k_b_s", (NS, PC), (1, NS, 1, NKV, HD)), ("v_b_s", (NS, PC), (1, NS, 1, NKV, HD)),
         ("logf_s", (NS, NH), (1, NS, 1, NH)), ("conv_s", (DEPTH, NS, CW - 1, FF), (DEPTH, NS, CW - 1, FF))]


def kernel(**inputs):
    import concourse.bacc as _bacc
    from concourse.bass_utils import run_bass_kernel_spmd as _run

    nc = _bacc.Bacc("TRN2", target_bir_lowering=False, num_devices=1)
    arrays, I, O = {}, {}, {}

    def give(name, a):
        a = np.ascontiguousarray(a)
        arrays[f"in_{name}"] = a
        I[name] = nc.dram_tensor(f"in_{name}", a.shape, mybir.dt.from_np(a.dtype), kind="ExternalInput").ap()

    for name in _INS:
        a = np.asarray(inputs[name])
        if name.startswith("cache"):
            a = a.reshape(a.shape[1], PAGE, -1)
        give(name, a)
    const, hsel = _constants()
    give("const", const)
    give("hsel", hsel)
    for name, shape, _ in _OUTS:
        O[name] = nc.dram_tensor(f"out_{name}", shape, F32, kind="ExternalOutput").ap()
    build(nc, I, O)
    r = _run(nc, [arrays], core_ids=[0])
    return tuple(r.results[0][f"out_{name}"].reshape(full) for name, _, full in _OUTS)
```

```python
from contextlib import ExitStack

import numpy as np

import concourse.bass as bass
from concourse import mybir

F32 = mybir.dt.float32
F32R = mybir.dt.float32r
I32 = mybir.dt.int32
ALU = mybir.AluOpType
ACT = mybir.ActivationFunctionType
AX = mybir.AxisListType
ds = bass.ds

P = 128
D = 1024
SEQ = 512
NS = 8
TOK = SEQ + NS
HT = TOK // 2
KC = D // P
NH, NKV, HD = 16, 4, 64
GR = NH // NKV
NIH = 8
PAST, PAGE = 1024, 128
NPG = PAST // PAGE
FF = 2816
FC = FF // P
CW = 3
DEPTH = 2
QKV = (NH + 2 * NKV) * HD
IN_A = QKV + NIH * HD + HD + NIH
IN_B = QKV + NH
NSEL_P = 128
NSEL_S = 256
QT = SEQ // P
EPS = 1e-6
SCALE = HD ** -0.5
NEG = -1e30
TAKEN = -3e38
NCV = (FC + 3) // 4
NADA = 6 * D // P
CC = 9
PC = 256
R = 4
HK = 4
CP = 2 * (CC + 1)

K_ID, K_ROT, K_COS, K_SIN = 0, 128, 256, 256 + TOK
K_TRI = K_SIN + TOK
K_CAU = K_TRI + 896
K_D16 = K_CAU + 512
K_D8 = K_D16 + 8
K_E16 = K_D8 + 8
K_E8 = K_E16 + 128
K_B16 = K_E8 + 64
K_SUM = K_B16 + 1
K_N = K_SUM + CC

W = 16
SECTIONS = [("ada0a", [(s, W) for s in (0, 1, 2, 3)], 2),
            ("head0", [(s, W) for s in (0, 1, 2, 3, 0)], 1),
            ("kidx", [(s, W) for s in (1, 2)], 4),
            ("ada0b", [(s, W) for s in (3, 0, 1, 2)], 4),
            ("q0", [(3, W)], 4),
            ("K0", [(s, W) for s in (1, 2)], 4),
            ("V0", [(s, W) for s in (3, 0)], 4),
            ("o0", [(s, W) for s in (1, 2, 3, 0)], 1),
            ("up0h", [(s, W) for s in (1, 2)], 1),
            ("up0", [(s, W) for s in (3, 0, 1, 2)], 5),
            ("dn0", [(s, W) for s in (3, 0, 1, 2, 3, 0)], 2),
            ("ada1", [(s, W) for s in (1, 2, 3, 0)], 6),
            ("head1", [(s, W) for s in (1, 2, 3)], 1),
            ("logf", [(0, W * NS)], 1),
            ("q1", [(1, W)], 4),
            ("K1", [(s, W) for s in (3, 0)], 4),
            ("V1", [(s, W) for s in (1, 2)], 4),
            ("o1", [(s, W) for s in (3, 0, 1, 2)], 1),
            ("up1h", [(s, W) for s in (3, 0)], 1),
            ("up1", [(s, W) for s in (1, 2, 3, 0)], 5),
            ("dn1", [(s, W) for s in (1, 2, 3, 0, 1, 2)], 2)]


GATHERED = ("kidx", "K0", "V0", "logf", "K1", "V1")


def _ring_counts():
    fills, out = [1] * R, {}
    value = {True: [0] * R, False: [0] * R}
    for name, body, turns in SECTIONS:
        val, per_f, per_v = value[name in GATHERED], [0] * R, [0] * R
        for s, inc in body:
            per_f[s] += 1
            per_v[s] += inc
        out[name] = (body, list(fills), list(val), per_f, per_v)
        for s in range(R):
            fills[s] += per_f[s] * turns
            val[s] += per_v[s] * turns
    return out


RING = _ring_counts()


def full_name(sec, s):
    return f"past_full{s}" if sec in GATHERED else f"ring_full{s}"


def fill(sec, i, j):
    body, f0, v0, per_f, per_v = RING[sec]
    s = body[j][0]
    nf = sum(1 for t, _ in body[:j] if t == s)
    nv = sum(inc for t, inc in body[:j + 1] if t == s)
    return s, i * per_f[s] + (f0[s] + nf), i * per_v[s] + (v0[s] + nv)


def _half_counts():
    out, n = {}, 0
    for name, body, turns in SECTIONS:
        if name not in GATHERED:
            out[name] = n
            n += 2 * len(body) * turns
    return out


HALVES = _half_counts()


def half_no(sec, i, j, h):
    return i * (2 * len(RING[sec][0])) + (HALVES[sec] + 2 * j + h)


def used(sec, i, j, h=1):
    return half_no(sec, i, j, h) + 3


CREDITED = [f"ring_free{s}" for s in range(R)] + ["w_used", "w_used", "tk_step", "sk_evac", "sk_dots", "up_c3", "up_acv"] + \
    ["at_pair", "at_s", "at_ot", "at_q", "at_qall"] + [f"sp{l}_{x}" for l in range(DEPTH) for x in ("kt", "qk")]

STORES = [6, 9, 15, 18, 19]


def build(nc, I, O):
    with ExitStack() as ctx:
        def sb(name, shape, dt=F32):
            return ctx.enter_context(nc.sbuf_tensor(name, shape, dt))[tuple(slice(0, n) for n in shape)]

        sems = {}

        def S(name):
            if name not in sems:
                sems[name] = ctx.enter_context(nc.semaphore(name))
            return sems[name]

        ps = ctx.enter_context(nc.psum_tensor("ps", [P, 8, 512], F32))

        def pair(p, rows=P, lo=0):
            return ps[lo:lo + rows, 2 * p:2 * p + 2, 0:HT]

        const = sb("const", [P, K_N])
        ident = const[:, K_ID:K_ID + P]
        swap = const[:, K_ROT:K_ROT + P]
        diag16 = const[:, K_D16:K_D16 + NS]
        diag8 = const[0:64, K_D8:K_D8 + NS]
        ones = sb("ones", [P, P])
        zeros = sb("zeros", [P, P])
        epsc = sb("epsc", [P, 1])
        colmask8 = sb("colmask8", [64, NS, 64])
        table = sb("table", [NPG, NS], I32)
        tablef = sb("tablef", [NPG, NS])
        idx = sb("idx", [P, NS], I32)
        ring = sb("ring", [P, R, KC * PC])
        xT = sb("xT", [P, KC, TOK])
        hH = sb("hH", [P, KC, TOK], F32R)
        hL = sb("hL", [P, KC, TOK], F32R)
        wH = sb("wH", [P, 2, HK, PC], F32R)
        wL = sb("wL", [P, 2, HK, PC], F32R)
        c2 = sb("c2", [P, KC, CP], F32R)
        cT = sb("cT", [P, KC, CC])
        vT = sb("vT", [P, 40])
        badaT = sb("badaT", [P, DEPTH * NADA])
        cwT = sb("cwT", [P, FC, 40])
        cs0 = sb("cs0", [P, DEPTH, FC, NS])
        ada = sb("ada", [P, DEPTH * NADA, CC])
        modA = sb("modA", [P, KC, CC])
        sq = sb("sq", [P, 2, TOK])
        rt = sb("rt", [P, TOK])
        bfb = sb("bfb", [P, NH])
        small = sb("small", [P, 64])
        tmp8 = sb("tmp8", [P, NS])
        scrap = sb("scrap", [1, 1])

        A_N = 19900
        arena = sb("arena", [P, A_N])
        at = [0]

        def part(n, reset=None):
            if reset is not None:
                at[0] = reset
            a = arena[:, at[0]:at[0] + n]
            at[0] += n
            assert at[0] <= A_N, at[0]
            return a

        hT = arena[:, A_N - KC * TOK:A_N].rearrange("p (k t) -> p k t", k=KC)
        xload = part(QT * D, 0).rearrange("p (t d) -> p t d", t=QT)
        xsload = part(D)
        cload = part(D)
        vrow = part(P)
        vrow2 = part(P)
        crow = part(FF)
        qst = part(GR * TOK, 0).rearrange("p (h t) -> p h t", h=GR)
        kaug = part(NKV * TOK).rearrange("p (g t) -> p g t", g=NKV)
        Vt = part(QT * PC).rearrange("p (t c) -> p t c", t=QT)
        OT = part(KC * TOK).rearrange("p (k t) -> p k t", k=KC)
        maskP = part(QT * SEQ).rearrange("p (t c) -> p t c", t=QT)
        knT = part(2 * NS).rearrange("p (a b) -> p a b", a=2)
        vnew = part(PC)
        knew = part(PC)
        Qall = part(2 * P).rearrange("p (a c) -> p a c", a=2)
        qz = part(4 * P).rearrange("p (r a c) -> p r a c", r=2, a=2)
        cq = part(QT * NH).rearrange("p (t h) -> p t h", t=QT)
        lf = part(5 * NH).rearrange("p (t h) -> p t h", t=5)
        scs = part(PAST + 1)
        biasS, maskS = scs[:, 0:PAST], scs[:, PAST:PAST + 1]
        work0 = at[0]
        raw = part(3 * TOK, work0).rearrange("p (b t) -> p b t", b=3)
        fm = part(3 * TOK).rearrange("p (b t) -> p b t", b=3)
        ktok = part(QT * PC).rearrange("p (t c) -> p t c", t=QT)
        ikw = part(QT * 72).rearrange("p (t c) -> p t c", t=QT)
        ikws = part(72)
        iqT = OT
        ikT = part(TOK)
        sc = raw.rearrange("p b t -> p (b t)")
        sc = sc[:, 0:3 * SEQ].rearrange("p (t c) -> p t c", t=3)
        relu = fm.rearrange("p b t -> p (b t)")[:, 0:3 * SEQ].rearrange("p (b c) -> p b c", b=3)
        ikb = ktok.rearrange("p t c -> p (t c)")
        iqall = part(P)
        iqz = part(2 * P).rearrange("p (r c) -> p r c", r=2)
        iwx = part(64)
        iwbd = part(NS)
        Rsb = fm.rearrange("p b t -> p (b t)")[0:64, 0:PAST + 1]
        raw2 = part(2 * TOK, work0).rearrange("p (b t) -> p b t", b=2)
        Sm = part(2 * SEQ).rearrange("p (b c) -> p b c", b=2)
        Pr = part(2 * SEQ).rearrange("p (b c) -> p b c", b=2)
        PT = part(2 * SEQ).rearrange("p (b c) -> p b c", b=2)
        On = part(2 * PC).rearrange("p (b c) -> p b c", b=2)
        mx = part(16)
        nm = part(16)
        lsum = part(16)
        rl = part(16)
        KT = part(4 * 512, work0).rearrange("p (r c) -> p r c", r=4)
        Pb = part(PAST)
        PTs = part(NPG * P).rearrange("p (j c) -> p j c", j=NPG)
        pnT = part(P)
        pnx = part(NS)
        ovs = part(P)
        ssm = part(16)
        colmask = part(NS * P).rearrange("p (b c) -> p b c", b=NS)
        lfT = part(PAST + 1, work0)
        cs = part(PAST + 1)
        lgx = part(P)
        zf = part(5 * NH)
        zg = part(5 * NH)
        gT = part(FC * TOK, 0).rearrange("p (k t) -> p k t", k=FC)
        aS = part(2 * (TOK + 2)).rearrange("p (b t) -> p b t", b=2)
        cvA = part(2 * TOK).rearrange("p (b t) -> p b t", b=2)
        acv = part(FC * 10).rearrange("p (k t) -> p k t", k=FC)
        cvrow = part(FF)
        ytok = part(2 * D, 0).rearrange("p (b d) -> p b d", b=2)
        ysam = part(D)

        def v520(a):
            return a.rearrange("p (a t) -> p a t", a=2)

        block = ctx.enter_context(nc.Block())

        def panel_ready(pe, sec, i, j):
            s, _, full = fill(sec, i, j)
            pe.wait_ge(S(full_name(sec, s)), full)
            return s

        def panel_used(ins, s):
            ins.then_inc(S(f"ring_free{s}"), 1)

        def slot_free(sp, sec, i, j):
            s, before, _ = fill(sec, i, j)
            sp.wait_ge(S(f"ring_free{s}"), before)
            return s

        def panel_view(s, cols=PC):
            return ring[:, s, :].rearrange("p (k c) -> p k c", c=PC)[:, :, 0:cols]

        def by_token(a):
            return a[:, 0:PAST].rearrange("p (k n) -> p n k", n=NPG)

        def pages_view(s, cols):
            return ring[:, s, 0:NPG * cols].rearrange("p (j c) -> p j c", c=cols)

        class Chain:
            n = 0

            def __init__(self, eng):
                self.eng = eng

            def link(self, ins):
                Chain.n += 1
                ins.then_inc(S("dve_step"), 1)
                self.eng.wait_ge(S("dve_step"), Chain.n)

        pool_n = [0]

        def in_turn(pool, ins):
            pool_n[0] += 1
            ins.then_inc(S("pool_step"), 1)
            pool.wait_ge(S("pool_step"), pool_n[0])

        ENG = ("pe", "act", "dve", "pool")
        phase_n = {e: 0 for e in ENG}

        def phase_end(eng, me):
            phase_n[me] += 1
            eng.drain().then_inc(S(f"phase_{me}"), 1)
            for e in ENG:
                if e != me:
                    eng.wait_ge(S(f"phase_{e}"), phase_n[me])

        def settle(dve):
            dve.memset(scrap[0:1, 0:1], 0.0)

        def load_panel(sp, sec, i, j, w, k0, nk, c0, cols=PC):
            s = slot_free(sp, sec, i, j)
            src = w.rearrange("(k p) c -> p k c", p=P)[:, k0:k0 + nk, ds(c0, cols)]
            sp.dma_start(panel_view(s, cols)[:, 0:nk, :], src).then_inc(S(f"ring_full{s}"), 16)

        def gather(pool, sec, i, j, cache, b, cols):
            s = slot_free(pool, sec, i, j)
            gather_rows(pool, ring[:, s, 0:NPG * cols], cache, b).then_inc(S(full_name(sec, s)), 16)

        def gather_rows(pool, out, cache, b):
            rows = cache.rearrange("g (u n) c -> (g u) (n c)", n=NPG)
            return pool.indirect_dma_start(out=out, out_offset=None, in_=rows,
                                           in_offset=bass.IndirectOffsetOnAxis(ap=idx[:, b:b + 1], axis=0))

        def gather_logf(pool, b):
            s = fill("logf", 0, 0)[0]
            gather_rows(pool, ring[:, s, b * P:b * P + P], I["cache_logf_b"], b).then_inc(S(full_name("logf", s)), 16)

        @block.sync
        def _(sp):
            sp.dma_start(cload[0:1, :], I["c_prompt"]).then_inc(S("in_vec"), 16)
            sp.dma_start(cload[1:CC, :], I["c_sample"]).then_inc(S("in_vec"), 16)
            sp.dma_start(vrow[0:DEPTH * NADA, :], I["b_ada"].rearrange("l (m p) -> (l m) p", p=P)).then_inc(S("in_vec"), 16)
            for n, g in enumerate(("g_mix", "g_ffn")):
                sp.dma_start(vrow2[16 * n:16 * n + 16, :], I[g].rearrange("l (m p) -> (l m) p", p=P)).then_inc(S("in_vec"), 16)
            sp.dma_start(vrow2[32:40, :], I["g_final"].rearrange("(m p) -> m p", p=P)).then_inc(S("in_vec"), 16)
            sp.dma_start(const[:, :], I["const"]).then_inc(S("in_const"), 16)
            with sp.Fori(0, 2) as i:
                for j in range(4):
                    load_panel(sp, "ada0a", i, j, I["w_ada"][0], 0, KC, (i * 4 + j) * PC)
            wa = I["w_in_a"][0]
            IQ0, IK0 = QKV, QKV + NIH * HD
            for j, (c0, cols) in enumerate(((NH * HD, PC), (NH * HD + PC, PC), (IK0, 72), (IQ0, PC), (IQ0 + PC, PC))):
                load_panel(sp, "head0", 0, j, wa, 0, KC, c0, cols)
            with sp.Fori(0, 4) as i:
                for j in range(4):
                    load_panel(sp, "ada0b", i, j, I["w_ada"][0], 0, KC, (i * 4 + j) * PC + 2 * D)
            for l in range(DEPTH):
                w_in = wa if l == 0 else I["w_in_b"][0]
                if l == 1:
                    with sp.Fori(0, 6) as i:
                        for j in range(4):
                            load_panel(sp, "ada1", i, j, I["w_ada"][1], 0, KC, (i * 4 + j) * PC)
                    for j, (c0, cols) in enumerate(((NH * HD, PC), (NH * HD + PC, PC), (QKV, NH))):
                        load_panel(sp, "head1", 0, j, w_in, 0, KC, c0, cols)
                with sp.Fori(0, NKV) as i:
                    load_panel(sp, f"q{l}", i, 0, w_in, 0, KC, i * PC)
                for j in range(4):
                    load_panel(sp, f"o{l}", 0, j, I[f"w_o_{'ab'[l]}"][0], 0, KC, j * PC)
                for j in range(2):
                    load_panel(sp, f"up{l}h", 0, j, I["w_up"][l], 0, KC, j * FF)
                with sp.Fori(0, 5) as i:
                    for j in range(4):
                        load_panel(sp, f"up{l}", i, j, I["w_up"][l], 0, KC, (i * 2 + (1 + j // 2)) * PC + (j % 2) * FF)
                with sp.Fori(0, 2) as i:
                    for j in range(6):
                        k0 = 8 * (j // 2)
                        load_panel(sp, f"dn{l}", i, j, I["w_down"][l], k0, min(8, FC - k0), (i * 2 + j % 2) * PC)

        def split_high(act, sec, i, j, h, nk=HK, cols=PC):
            s, _, full = fill(sec, i, j)
            if h == 0:
                act.wait_ge(S(full_name(sec, s)), full)
            act.wait_ge(S("w_used"), half_no(sec, i, j, h) + 1)
            act.activation(wH[:, h, 0:nk, 0:cols], panel_view(s)[:, HK * h:HK * h + nk, 0:cols], ACT.Copy).then_inc(S("w_hi"), 1)

        def split_low(eng, sec, i, j, h, nk=HK, cols=PC):
            s, _, _ = fill(sec, i, j)
            eng.wait_ge(S("w_hi"), half_no(sec, i, j, h) + 1)
            eng.tensor_tensor(wL[:, h, 0:nk, 0:cols], panel_view(s)[:, HK * h:HK * h + nk, 0:cols],
                              wH[:, h, 0:nk, 0:cols].bitcast(F32), ALU.subtract).then_inc(S("w_lo"), 1)

        def half_ready(pe, sec, i, j, h):
            s, _, _ = fill(sec, i, j)
            pe.wait_ge(S("w_lo"), half_no(sec, i, j, h) + 1)
            if h == 1:
                pe.sem_inc(S(f"ring_free{s}"), 1)

        def mm_half(pe, h, pairs, k0, nk, first, last, wait=None):
            for t, p in enumerate(pairs):
                for kc in range(nk):
                    if wait is not None and t == 0:
                        wait(k0 + kc)
                    for n, (w, mov) in enumerate(((wH, hH), (wH, hL), (wL, hH))):
                        for half in range(2):
                            ins = pe.matmul(ps[:, 2 * p + half, 0:HT], w[:, h, kc, t * P:t * P + P],
                                            mov[:, k0 + kc, half * HT:half * HT + HT],
                                            start=(first and kc == 0 and n == 0), stop=(last and kc == nk - 1 and n == 2))
            ins.then_inc(S("w_used"), 1)

        def mm_panel(pe, sec, i, j, pairs, wait=None):
            for h in range(2):
                half_ready(pe, sec, i, j, h)
                mm_half(pe, h, pairs, HK * h, HK, h == 0, h == 1, wait)

        def ada_turn(pe, j, t0):
            pe.wait_ge(S("ad_row"), t0 + 1)
            for m in range(2):
                ins = pe.matmul(ps[:, 4 + j, CC * m:CC * m + CC], sq[0:CP, j % 2, m * P:m * P + P], const[0:CP, K_SUM:K_SUM + CC],
                                start=True, stop=True)
            ins.then_inc(S("ad_turn"), 1)

        def pe_ada(pe, sec, turns, n0):
            with pe.Fori(0, turns) as i:
                for j in range(5):
                    if j < 4:
                        for h in range(2):
                            half_ready(pe, sec, i, j, h)
                            for kc in range(HK):
                                pe.matmul(ps[0:CP, j, 0:PC], c2[:, HK * h + kc, :], wH[:, h, kc, :], start=(h + kc == 0), stop=False)
                                ins = pe.matmul(ps[0:CP, j, 0:PC], c2[:, HK * h + kc, :], wL[:, h, kc, :], start=False,
                                                stop=(h == 1 and kc == HK - 1))
                            ins.then_inc(S("w_used"), 1)
                    if j >= 1:
                        ada_turn(pe, j - 1, i * 4 + (n0 + j - 1))

        def act_ada(act, sec, turns, m0, n0):
            def result(j, i):
                act.wait_ge(S("ad_turn"), i * 4 + (n0 + j + 1))
                for m in range(2):
                    mt = (i * 4 + j) * 2 + (m0 + m)
                    act.activation(ada[:, ds(mt, 1), :].rearrange("p o c -> p (o c)"), ps[:, 4 + j, CC * m:CC * m + CC],
                                   ACT.Identity, bias=badaT[:, ds(mt, 1)])

            def ahead(i, j, h):
                split_high(act, sec, i + (j + 1) // 4, (j + 1) % 4, h)

            for h in range(2):
                split_high(act, sec, 0, 0, h)
            with act.Fori(0, turns) as i:
                for j in range(4):
                    ahead(i, j, 0)
                    act.wait_ge(S("w_used"), used(sec, i, j))
                    if j >= 2:
                        act.wait_ge(S("ad_turn"), i * 4 + (n0 + j - 1))
                    act.activation(sq[0:CP, j % 2, 0:PC], ps[0:CP, j, 0:PC], ACT.Copy).then_inc(S("ad_row"), 1)
                    ahead(i, j, 1)
                    if j >= 1:
                        result(j - 1, i)
                result(3, i)

        def low_ada(dve, sec, turns):
            with dve.Fori(0, turns) as i:
                for j in range(4):
                    for h in range(2):
                        split_low(dve, sec, i, j, h)
            for h in range(2):
                split_low(dve, sec, turns, 0, h)

        def low_even(pool, sec, turns):
            with pool.Fori(0, turns) as i:
                for j in range(4):
                    pool.wait_ge(S("w_lo"), half_no(sec, i, j, 0))
                    split_low(pool, sec, i, j, 0)
            pool.wait_ge(S("w_lo"), half_no(sec, turns, 0, 0))
            split_low(pool, sec, turns, 0, 0)

        def low_odd(dve, sec, p):
            dve.wait_ge(S("w_lo"), half_no(sec, p // 4, p % 4, 1))
            split_low(dve, sec, p // 4, p % 4, 1)

        def x_done(eng, n, kc):
            if n % 2 == 1:
                eng.wait_ge(S(f"o{n // 2}_res"), kc + 1)
            elif n == 4:
                eng.wait_ge(S("dn1_free"), 4 + kc + 1)

        def pe_rms(pe, n):
            x_done(pe, n, 4)
            for kc in range(KC):
                pe.wait_ge(S("rms_sq"), n * KC + kc + 1)
                for half in range(2):
                    ins = pe.matmul(ps[:, half, 0:HT], ones[:, :], sq[:, kc % 2, half * HT:half * HT + HT],
                                    start=(kc == 0), stop=(kc == KC - 1))
                ins.then_inc(S("rms_sum"), 1)

        def act_rms(act, n, shift, gain):
            for kc in range(KC):
                if n % 2 == 1 and kc % 2 == 0 and kc < 4:
                    split_high(act, f"up{n // 2}h", 0, 0, kc // 2)
                if kc >= 2:
                    act.wait_ge(S("rms_sum"), n * KC + kc - 1)
                x_done(act, n, kc)
                act.activation(sq[:, kc % 2, :], xT[:, kc, :], ACT.Square).then_inc(S("rms_sq"), 1)
            act.wait_ge(S("rms_sum"), n * KC + KC)
            act.activation(v520(rt[:, :]), pair(0), ACT.Sqrt, bias=epsc[:, 0:1], scale=1.0 / D).then_inc(S("rms_rt"), 1)
            for kc in range(KC):
                act.wait_ge(S("rms_t"), n * KC + kc + 1)
                if shift is None:
                    act.activation(hT[:, kc, :], hT[:, kc, :], ACT.Identity, scale=gain[:, kc:kc + 1])
                else:
                    act.activation(hT[:, kc, 0:SEQ], hT[:, kc, 0:SEQ], ACT.Identity, bias=shift[:, kc, 0:1], scale=modA[:, kc, 0:1])\
                        .then_inc(S("rms_v"), 1)

        def pool_rms(pool, n):
            for kc in range(KC):
                pool.wait_ge(S("rms_v"), n * KC + kc + 1)
                pool.wait_ge(S("rms_s"), n * KC + kc + 1)
                pool.tensor_copy(hH[:, kc, :], hT[:, kc, :]).then_inc(S("rms_hi"), 1)

        def dve_rms(dve, n, shift, scale, gain):
            ch = Chain(dve)
            if shift is not None:
                ch.link(dve.scalar_tensor_tensor(out=modA[:, :, :], in0=scale, scalar=1.0,
                                                 in1=gain.unsqueeze(2).to_broadcast([P, KC, CC]), op0=ALU.add, op1=ALU.mult))
            if n % 2 == 1:
                for h in range(2):
                    split_low(dve, f"up{n // 2}h", 0, 0, h)
            dve.wait_ge(S("rms_rt"), n + 1)
            ch.link(dve.reciprocal(rt[:, :], rt[:, :]))
            for kc in range(KC):
                dve.tensor_tensor(hT[:, kc, :], xT[:, kc, :], rt[:, :], ALU.mult).then_inc(S("rms_t"), 1)
                if shift is not None:
                    hs = hT[:, kc, SEQ:TOK]
                    dve.wait_ge(S("rms_t"), n * KC + kc + 1)
                    ch.link(dve.tensor_tensor(hs, hs, modA[:, kc, 1:CC], ALU.mult))
                    dve.tensor_tensor(hs, hs, shift[:, kc, 1:CC], ALU.add).then_inc(S("rms_s"), 1)
            if shift is not None:
                for kc in range(KC):
                    dve.wait_ge(S("rms_hi"), n * KC + kc + 1)
                    dve.tensor_tensor(hL[:, kc, :], hT[:, kc, :], hH[:, kc, :].bitcast(F32), ALU.subtract)\
                        .then_inc(S("rms_lo"), 1)

        def split_input(pe, n):
            return lambda kc: pe.wait_ge(S("rms_lo"), n * KC + kc + 1)

        TILES = [[(0, 0, P, "k"), (0, P, P, "k"), (1, 0, P, "v"), (1, P, P, "v"), (2, 0, 72, "ikw"),
                  (3, 0, P, "iq"), (3, P, P, "iq"), (4, 0, P, "iq"), (4, P, P, "iq")],
                 [(0, 0, P, "k"), (0, P, P, "k"), (1, 0, P, "v"), (1, P, P, "v"), (2, 0, NH, "fg")]]

        def tiles_in(l, pn):
            return sum(1 for tile in TILES[l] if tile[0] == pn)

        def last_in(l, t):
            return t + 1 == len(TILES[l]) or TILES[l][t + 1][1] == 0

        def head_cols(l, pn):
            return {2: 72 if l == 0 else NH}.get(pn, PC)

        def rotates(l, t):
            return l == 0 and TILES[l][t][3] != "v"

        def turned(l, t):
            return TILES[l][t][3] != "iq"

        def copied(l, t):
            return TILES[l][t][3] in ("k", "ikw", "iq")

        def upto(test, l, t):
            return sum(1 for u in range(t + 1) if test(l, u))

        def src_of(l, t):
            return (fm if rotates(l, t) else raw)[:, t % 3, :]

        def pe_head(pe, l):
            tag, sec = f"hd{l}", f"head{l}"
            T = TILES[l]
            for t in range(len(T) + 2):
                if t < len(T) and T[t][1] == 0:
                    if t:
                        pe.wait_ge(S(f"{tag}_raw"), t)
                    mm_panel(pe, sec, 0, T[t][0], [u % 2 for u in range(t, t + tiles_in(l, T[t][0]))],
                             split_input(pe, 2 * l) if t == 0 else None)
                u = t - 1
                if 0 <= u < len(T) and rotates(l, u):
                    pe.wait_ge(S(f"{tag}_raw"), u + 1)
                    if upto(rotates, l, u) >= 2:
                        pe.wait_ge(S(f"{tag}_fm"), upto(rotates, l, u) - 1)
                    rows = min(T[u][2], P) if T[u][3] != "ikw" else HD
                    for half in range(2):
                        ins = pe.matmul(ps[0:rows, 4 + half, 0:HT], swap[0:rows, 0:rows],
                                        raw[0:rows, u % 3, half * HT:half * HT + HT], start=True, stop=True)
                    ins.then_inc(S(f"{tag}_rot"), 1)
                u = t - 2
                if 0 <= u < len(T) and turned(l, u):
                    rows = T[u][2]
                    if rotates(l, u):
                        pe.wait_ge(S(f"{tag}_fm"), upto(rotates, l, u))
                    if upto(turned, l, u) >= 2:
                        pe.wait_ge(S(f"{tag}_tok"), upto(turned, l, u) - 1)
                    src = src_of(l, u)
                    for q in range(QT):
                        pe.transpose(ps[:, 6, q * P:q * P + rows], src[0:rows, q * P:q * P + P], ident[0:rows, 0:rows])
                    pe.transpose(ps[0:NS, 7, 0:rows], src[0:rows, SEQ:TOK], ident[0:rows, 0:rows]).then_inc(S(f"{tag}_tr"), 1)

        def act_head(act, l):
            tag = f"hd{l}"
            T = TILES[l]

            def tok_major(t):
                rows, kind = T[t][2], T[t][3]
                act.wait_ge(S(f"{tag}_tr"), upto(turned, l, t))
                src = ps[:, 6, :].rearrange("p (q c) -> p q c", q=QT)[:, :, 0:rows]
                big, new, c0 = {"k": (ktok, knew, P * (t % 2)), "v": (Vt, vnew, P * (t % 2)),
                                "ikw": (ikw, ikws, 0), "fg": (lf, None, 0)}[kind]
                act.activation(big[:, 0:QT, c0:c0 + rows], src, ACT.Copy)
                dst = lf[0:NS, QT, :] if kind == "fg" else new[0:NS, c0:c0 + rows]
                act.activation(dst, ps[0:NS, 7, 0:rows], ACT.Copy).then_inc(S(f"{tag}_tok"), 1)

            sec = f"head{l}"
            for t in range(len(T) + 2):
                if t < len(T):
                    pn, m0, rows, _ = T[t]
                    ahead = pn + 1 <= T[-1][0]
                    if m0 == 0 and ahead:
                        split_high(act, sec, 0, pn + 1, 0, HK, head_cols(l, pn + 1))
                    act.wait_ge(S("w_used"), used(sec, 0, pn))
                    if t >= 3:
                        u = t - 3
                        if upto(rotates, l, u):
                            act.wait_ge(S(f"{tag}_fm"), upto(rotates, l, u))
                            act.wait_ge(S(f"{tag}_rot"), upto(rotates, l, u))
                        if upto(turned, l, u):
                            act.wait_ge(S(f"{tag}_tr"), upto(turned, l, u))
                        if upto(copied, l, u):
                            act.wait_ge(S(f"{tag}_cp"), upto(copied, l, u))
                    act.activation(v520(raw[0:rows, t % 3, :]), pair(t % 2, rows), ACT.Copy).then_inc(S(f"{tag}_raw"), 1)
                    if last_in(l, t) and ahead:
                        split_high(act, sec, 0, pn + 1, 1, HK, head_cols(l, pn + 1))
                if t >= 2 and turned(l, t - 2):
                    tok_major(t - 2)
            act.wait_ge(S(f"{tag}_tok"), upto(turned, l, len(T) - 1))
            x = "ab"[l]
            for src, new, name in ((ktok, knew, "k"), (Vt, vnew, "v")):
                act.dma_start(O[f"{name}_{x}_p"].rearrange("(t p) c -> p t c", p=P), src).then_inc(S("stores"), 16)
                act.dma_start(O[f"{name}_{x}_s"], new[0:NS, :]).then_inc(S("stores"), 16)
            if l == 0:
                act.dma_start(O["kidx_p"].rearrange("(t p) c -> p t c", p=P), ikw[:, :, 0:HD]).then_inc(S("stores"), 16)
                act.dma_start(O["kidx_s"], ikws[0:NS, 0:HD]).then_inc(S("stores"), 16)

        def dve_head(dve, l):
            tag = f"hd{l}"
            T = TILES[l]
            ch = Chain(dve)
            for t in range(len(T)):
                pn = T[t][0]
                if T[t][1] == 0 and pn + 1 <= T[-1][0]:
                    for h in range(2):
                        split_low(dve, f"head{l}", 0, pn + 1, h, HK, head_cols(l, pn + 1))
                if not rotates(l, t):
                    continue
                rows = HD if T[t][3] == "ikw" else P
                dve.wait_ge(S(f"{tag}_raw"), t + 1)
                if upto(rotates, l, t) >= 2:
                    dve.wait_ge(S(f"{tag}_fm"), upto(rotates, l, t) - 1)
                dve.tensor_tensor(sq[0:rows, 0, :], raw[0:rows, t % 3, :], const[0:rows, K_COS:K_COS + TOK], ALU.mult)
                dve.wait_ge(S(f"{tag}_rot"), upto(rotates, l, t))
                ch.link(dve.tensor_tensor(v520(sq[0:rows, 1, :]), pair(2, rows), v520(const[0:rows, K_SIN:K_SIN + TOK]), ALU.mult))
                if t >= 3:
                    if upto(turned, l, t - 3):
                        dve.wait_ge(S(f"{tag}_tr"), upto(turned, l, t - 3))
                    dve.wait_ge(S(f"{tag}_cp"), upto(copied, l, t - 3))
                if T[t][3] == "ikw":
                    dve.tensor_copy(fm[HD:72, t % 3, :], raw[HD:72, t % 3, :])
                dve.tensor_tensor(fm[0:rows, t % 3, :], sq[0:rows, 0, :], sq[0:rows, 1, :], ALU.add).then_inc(S(f"{tag}_fm"), 1)

        def pool_head(pool, l):
            tag = f"hd{l}"
            T = TILES[l]
            for t in range(len(T)):
                if not copied(l, t):
                    continue
                if rotates(l, t):
                    pool.wait_ge(S(f"{tag}_fm"), upto(rotates, l, t))
                else:
                    pool.wait_ge(S(f"{tag}_raw"), t + 1)
                src, kind = src_of(l, t), T[t][3]
                if kind == "k":
                    in_turn(pool, pool.tensor_copy(kaug[0:HD, 2 * t, :], src[0:HD, :]))
                    in_turn(pool, pool.tensor_copy(kaug[0:HD, 2 * t + 1, :], src[HD:P, :]))
                    ins = pool.tensor_copy(knT[:, t, :], src[:, SEQ:TOK])
                elif kind == "ikw":
                    ins = pool.tensor_copy(ikT[0:HD, :], src[0:HD, :])
                else:
                    h = 2 * (t - 5)
                    in_turn(pool, pool.tensor_copy(iqT[0:HD, h, :], src[0:HD, :]))
                    ins = pool.tensor_copy(iqT[0:HD, h + 1, :], src[HD:P, :])
                ins.then_inc(S(f"{tag}_cp"), 1)
                pool.wait_ge(S(f"{tag}_cp"), upto(copied, l, t))

        def pe_score(pe):
            for u in range(3 * NIH):
                qt, h = u // NIH + 1, u % NIH
                if u >= 4:
                    pe.wait_ge(S("sc_relu"), u - 3)
                pe.matmul(ps[:, u % 4, 0:(qt + 1) * P], iqT[0:HD, h, qt * P:qt * P + P], ikT[0:HD, 0:(qt + 1) * P],
                          start=True, stop=True).then_inc(S("sc_dot"), 1)
            for c in range(2):
                pe.matmul(ps[:, 6 + c, :], zeros[0:HD, :], const[0:HD, 0:512], start=True, stop=False)
            with pe.Fori(0, 4) as i:
                for j in range(2):
                    s = panel_ready(pe, "kidx", i, j)
                    pe.wait_ge(S("sk_evac"), 1 + (i * 2 + j) * 2)
                    for n in range(NPG // 2):
                        ins = pe.transpose(ps[:, 4, n * P:n * P + P], ring[:, s, 2 * n * HD:2 * n * HD + P], ident)
                    panel_used(ins, s)
                    pe.wait_ge(S("sk_qz"), i * 2 + j + 1)
                    for c in range(2):
                        pe.wait_ge(S("sk_evac"), 1 + (i * 2 + j) * 2 + 2)
                        ins = pe.matmul(ps[:, 6 + c, :], iqz[0:HD, j, :], ikb[0:HD, c * 512:c * 512 + 512], start=False, stop=False)
                    ins.then_inc(S("sk_dots"), 1)
            for c in range(2):
                pe.matmul(ps[:, 6 + c, :], zeros[0:HD, :], const[0:HD, 0:512], start=False, stop=True)
            pe.wait_ge(S("sc_relu"), 3 * NIH)
            pe.matmul(ps[0:64, 3, 0:NS], iqall[0:HD, 0:64], ikT[0:HD, SEQ:TOK], start=True, stop=True).then_inc(S("sk_all"), 1)
            pe.wait_ge(S("sk_iwx"), 1)
            pe.transpose(ps[0:64, 2, 0:NS], iwx[0:NS, :], ident[0:NS, 0:NS]).then_inc(S("sk_iwt"), 1)
            pe.wait_ge(S("sk_rs"), 3)
            pe.wait_ge(S("sk_iwbd"), 1)
            for c in range(2):
                pe.matmul(ps[0:NS, c, :], iwbd[0:64, :], Rsb[:, c * 512:c * 512 + 512], start=True, stop=True)
            pe.matmul(ps[0:NS, 2, 16:17], iwbd[0:64, :], Rsb[:, PAST:PAST + 1], start=True, stop=True).then_inc(S("sk_score"), 1)

        def act_score(act):
            for u in range(3 * NIH):
                w = (u // NIH + 2) * P
                act.wait_ge(S("sc_dot"), u + 1)
                if u >= 3:
                    act.wait_ge(S("sc_acc"), u - 2)
                act.activation(relu[:, u % 3, 0:w], ps[:, u % 4, 0:w], ACT.Relu).then_inc(S("sc_relu"), 1)
            act.wait_ge(S("stores"), 16 * STORES[0])
            with act.Fori(0, 4) as i:
                for j in range(2):
                    s, before, _ = fill("kidx", i, j)
                    act.wait_ge(S(f"ring_free{s}"), before + 1)
                    act.wait_ge(S("sk_dots"), 1 + i * 2 + j)
                    for c in range(2):
                        act.activation(ikb[0:HD, :].rearrange("p (n e t) -> p n e t", e=2, t=P)[:, :, c, :],
                                       ps[64 * c:64 * c + 64, 4, :].rearrange("p (n t) -> p n t", t=P), ACT.Copy).then_inc(S("sk_evac"), 1)
            act.wait_ge(S("sk_all"), 1)
            act.wait_ge(S("sc_acc"), 3 * NIH)
            for c in range(2):
                act.activation(by_token(Rsb)[:, 4 * c:4 * c + 4, :], ps[0:64, 6 + c, :].rearrange("p (n k) -> p n k", n=4), ACT.Relu)\
                    .then_inc(S("sk_rs"), 1)
            act.wait_ge(S("sk_new"), 1)
            act.activation(Rsb[:, PAST:PAST + 1], small[0:64, 0:1], ACT.Relu).then_inc(S("sk_rs"), 1)

        def pool_score(pool):
            in_turn(pool, pool.memset(iqz[0:HD, :, 64:P], 0.0))
            pool.tensor_copy(iqall[0:HD, 0:64].rearrange("p (b h) -> p h b", h=NIH), iqT[0:HD, :, SEQ:TOK]).then_inc(S("pl_iq"), 1)
            pool.wait_ge(S("pl_iq"), 1)
            for i in range(4):
                for j in range(2):
                    gather(pool, "kidx", i, j, I["cache_kidx_a"], i * 2 + j, HD)
                for j in range(2):
                    pool.wait_ge(S("sk_dots"), 1 + (i * 2))
                    pool.tensor_tensor(iqz[0:HD, j, 0:64], iqall[0:HD, 0:64], colmask8[:, ds(i * 2 + j, 1), :].rearrange("p o c -> p (o c)"),
                                       ALU.mult).then_inc(S("sk_qz"), 1)

        def dve_score(dve):
            ch = Chain(dve)
            dve.tensor_tensor(iwx[0:NS, :].rearrange("p (b h) -> p b h", h=NIH), const[0:NS, K_E8:K_E8 + 64].rearrange("p (b h) -> p b h", h=NIH),
                              ikws[0:NS, HD:72].unsqueeze(1).to_broadcast([NS, NS, NIH]), ALU.mult).then_inc(S("sk_iwx"), 1)
            for u in range(3 * NIH):
                qt, h = u // NIH + 1, u % NIH
                w = (qt + 1) * P
                dve.wait_ge(S("sc_relu"), u + 1)
                iw = ikw[:, qt, HD + h:HD + h + 1]
                if h == 0:
                    ins = dve.tensor_scalar(sc[:, qt - 1, 0:w], relu[:, u % 3, 0:w], iw, None, ALU.mult)
                else:
                    ins = dve.scalar_tensor_tensor(out=sc[:, qt - 1, 0:w], in0=relu[:, u % 3, 0:w], scalar=iw,
                                                   in1=sc[:, qt - 1, 0:w], op0=ALU.mult, op1=ALU.add)
                ins.then_inc(S("sc_acc"), 1)
                dve.wait_ge(S("sc_acc"), u + 1)
                if h == NIH - 1:
                    ch.link(dve.tensor_tensor(sc[:, qt - 1, 0:w], sc[:, qt - 1, 0:w], const[:, K_CAU + SEQ - w:K_CAU + SEQ], ALU.add))
            dve.wait_ge(S("sk_iwt"), 1)
            dve.tensor_copy(iwbd[0:64, :], ps[0:64, 2, 0:NS]).then_inc(S("sk_iwbd"), 1)
            dve.wait_ge(S("sk_all"), 1)
            dve.tensor_tensor_reduce(small[0:64, 8:16], ps[0:64, 3, 0:NS], diag8, 1.0, 0.0, ALU.mult, ALU.add, small[0:64, 0:1])\
                .then_inc(S("sk_new"), 1)
            dve.wait_ge(S("sk_score"), 1)
            dve.tensor_copy(scs[0:NS, 0:PAST].rearrange("p (a c) -> p a c", a=2), ps[0:NS, 0:2, :])
            ch.link(dve.tensor_copy(scs[0:NS, PAST:PAST + 1], ps[0:NS, 2, 16:17]))

        def dve_topk(dve):
            ch = Chain(dve)
            dve.tensor_copy(maskP[:, 0, 0:P], const[:, K_CAU + SEQ - P:K_CAU + SEQ])
            for qt in range(1, QT):
                w = (qt + 1) * P
                scores, m8 = sc[:, qt - 1, 0:w], small[:, 0:8]
                for n in range(NSEL_P // 8):
                    ch.link(dve.max(m8, scores))
                    ch.link(dve.match_replace(scores, m8, scores, TAKEN))
                    step = (qt - 1) * (NSEL_P // 8) + n
                    if step % 3 == 0:
                        low_odd(dve, "ada0b", step // 3)
                dve.tensor_scalar(maskP[:, qt, 0:w], sc[:, qt - 1, 0:w], 0.5 * TAKEN, NEG, ALU.is_gt, ALU.mult)
            low_odd(dve, "ada0b", 16)

        def act_logf(act):
            z, e = zf.rearrange("p (t h) -> p t h", t=5), zg.rearrange("p (t h) -> p t h", t=5)
            act.wait_ge(S("lf_z"), 1)
            act.activation(e, z, ACT.Abs).then_inc(S("lf_act"), 1)
            act.wait_ge(S("lf_act"), 1)
            act.activation(e, e, ACT.Exp, scale=-1.0).then_inc(S("lf_act"), 1)
            act.wait_ge(S("lf_act"), 2)
            act.activation(e, e, ACT.Ln, bias=ones[:, 0:1]).then_inc(S("lf_act"), 1)
            act.wait_ge(S("lf_done"), 1)
            act.dma_start(O["logf_p"].rearrange("(t p) c -> p t c", p=P), lf[:, 0:QT, :]).then_inc(S("stores"), 16)
            act.dma_start(O["logf_s"], lf[0:NS, QT, :]).then_inc(S("stores"), 16)
            act.wait_ge(S("lf_ck"), 1)
            act.activation(kaug[64:68, :, 0:SEQ], ps[64:68, 0:NKV, :], ACT.Copy, scale=-1.0 / SCALE)
            act.wait_ge(S("lf_turn"), 1)
            for c in range(2):
                ins = act.activation(by_token(lfT)[:, 4 * c:4 * c + 4, :], ps[:, 4 + c, :].rearrange("p (n k) -> p n k", n=4), ACT.Copy)
            ins.then_inc(S("lf_past"), 1)
            act.wait_ge(S("stores"), 16 * STORES[2])

        def dve_logf(dve):
            ch = Chain(dve)
            z, e = zf.rearrange("p (t h) -> p t h", t=5), zg.rearrange("p (t h) -> p t h", t=5)
            s = panel_ready(dve, "logf", 0, 0)
            panel_used(dve.tensor_copy(cs[:, 0:PAST].rearrange("p (n b h) -> p b n h", n=NPG, b=NS),
                                       ring[:, s, 0:PAST].rearrange("p (b n h) -> p b n h", b=NS, n=NPG)), s)
            dve.tensor_tensor(z, lf, bfb[:, :].unsqueeze(1).to_broadcast([P, 5, NH]), ALU.add).then_inc(S("lf_z"), 1)
            dve.wait_ge(S("lf_act"), 3)
            dve.scalar_tensor_tensor(out=lf, in0=z, scalar=0.0, in1=e, op0=ALU.min, op1=ALU.subtract).then_inc(S("lf_done"), 1)
            dve.wait_ge(S("lf_done"), 1)
            dve.tensor_tensor(lgx[0:NS, :].rearrange("p (b h) -> p b h", h=NH), const[0:NS, K_E16:K_E16 + P].rearrange("p (b h) -> p b h", h=NH),
                              lf[0:NS, QT, :].unsqueeze(1).to_broadcast([NS, NS, NH]), ALU.mult).then_inc(S("lf_x"), 1)
            dve.wait_ge(S("lf_cq"), 1)
            dve.tensor_copy(cq, ps[:, 6, 0:QT * NH].rearrange("p (t h) -> p t h", t=QT))
            dve.wait_ge(S("lf_xt"), 1)
            dve.tensor_reduce(lfT[:, PAST:PAST + 1], ps[:, 7, 0:NS], AX.X, ALU.add).then_inc(S("lf_past"), 1)
            dve.wait_ge(S("lf_past"), 2)
            ch.link(dve.tensor_tensor_scan(cs, lfT, lfT, 0.0, ALU.add, ALU.bypass))
            dve.tensor_scalar(biasS, cs[:, 0:PAST], cs[:, PAST:PAST + 1], -1.0 / SCALE, ALU.subtract, ALU.mult)

        def pe_logf(pe):
            tri = const[:, K_TRI:K_TRI + 896]
            slot, before, _ = fill("logf", 0, 0)
            pe.wait_ge(S(f"ring_free{slot}"), before + 1)
            for n in range(NPG):
                ins = pe.transpose(ps[:, 4 + n // 4, (n % 4) * P:(n % 4) * P + P], cs[:, n * P:n * P + P], ident)
            ins.then_inc(S("lf_turn"), 1)
            pe.wait_ge(S("lf_done"), 1)
            for qt in range(QT):
                for kb in range(qt + 1):
                    x = P * (qt - kb) + 384
                    ins = pe.matmul(ps[:, 6, qt * NH:qt * NH + NH], tri[:, x:x + P], lf[:, kb, :], start=(kb == 0), stop=(kb == qt))
            ins.then_inc(S("lf_cq"), 1)
            for g in range(NKV):
                for kb in range(QT):
                    ins = pe.matmul(ps[64:68, g, kb * P:SEQ], lf[:, kb, GR * g:GR * g + GR], tri[:, 384:384 + SEQ - kb * P],
                                    start=(kb == 0), stop=(kb == QT - 1))
            ins.then_inc(S("lf_ck"), 1)
            pe.wait_ge(S("lf_x"), 1)
            pe.transpose(ps[:, 7, 0:NS], lgx[0:NS, :], ident[0:NS, 0:NS]).then_inc(S("lf_xt"), 1)

        NU = QT * GR
        QPARTS = {3: (0, 1), 4: (2, 3), 5: (4, 5), 6: (6, 7), 10: (8, 9), 11: (10, 11), 12: (12, 13), 13: (14, 15)}
        QPAIR = 3

        def pe_qpart(pe, sec, i, n, part):
            t, h, kc = part // 8, part // HK % 2, part % HK
            if h + kc == 0:
                pe.wait_ge(S("at_pair"), n * 2 + (t + 1))
            if t == 0 and kc == 0:
                half_ready(pe, sec, i, 0, h)
            for m, (w, mov) in enumerate(((wH, hH), (wH, hL), (wL, hH))):
                for half in range(2):
                    ins = pe.matmul(ps[:, 2 * QPAIR + half, 0:HT], w[:, h, kc, t * P:t * P + P],
                                    mov[:, HK * h + kc, half * HT:half * HT + HT],
                                    start=(h + kc + m == 0), stop=(h == 1 and kc == HK - 1 and m == 2))
            if kc == HK - 1:
                if t == 1:
                    ins.then_inc(S("w_used"), 1)
                elif h == 1:
                    ins.then_inc(S("at_mm"), 1)

        def pe_qrot(pe, n, t):
            pe.wait_ge(S("at_raw"), n * 2 + (t + 1))
            for half in range(2):
                ins = pe.matmul(ps[:, 2 * QPAIR + half, 0:HT], swap, raw2[:, t, half * HT:half * HT + HT], start=True, stop=True)
            ins.then_inc(S("at_rot"), 1)

        def pe_units(pe, l, g, n, nxt):
            K = HD + GR
            pe.wait_ge(S("at_q"), n * 2 + 3)
            for u in range(NU + 4):
                if u < NU:
                    qt, hh = u // GR, u % GR
                    w = (qt + 1) * P
                    if u >= 2:
                        pe.wait_ge(S("at_sm"), n * NU + (u - 1))
                    pe.matmul(ps[:, u % 2, 0:w], qst[0:K, hh, qt * P:qt * P + P],
                              kaug[0:K, ds(g, 1), 0:w].rearrange("p o t -> p (o t)"), start=True, stop=True).then_inc(S("at_s"), 1)
                v = u - 1
                if 0 <= v < NU:
                    qt = v // GR
                    pe.wait_ge(S("at_p"), n * NU + (v + 1))
                    if v >= 2:
                        pe.wait_ge(S("at_pt"), n * NU + (v - 1))
                    for kb in range(qt + 1):
                        ins = pe.transpose(ps[:, 2 + v % 2, kb * P:kb * P + P], Pr[:, v % 2, kb * P:kb * P + P], ident)
                    ins.then_inc(S("at_tr"), 1)
                v = u - 2
                if 0 <= v < NU:
                    qt, hh = v // GR, v % GR
                    pe.wait_ge(S("at_pt"), n * NU + (v + 1))
                    if hh == 0 and qt >= 1:
                        pe.wait_ge(S("at_on"), n * QT + qt)
                    for kb in range(qt + 1):
                        ins = pe.matmul(ps[:, 4, hh * HD:hh * HD + HD], PT[:, v % 2, kb * P:kb * P + P],
                                        Vt[:, kb, ds(g * HD, HD)], start=(kb == 0), stop=(kb == qt))
                    ins.then_inc(S("at_o"), 1)
                v = u - 4
                if 0 <= v < NU and v % GR == GR - 1:
                    qt = v // GR
                    pe.wait_ge(S("at_on"), n * QT + (qt + 1))
                    pe.wait_ge(S("at_ot"), n * QT + (qt + 1))
                    for t in range(2):
                        ins = pe.transpose(ps[:, 5, t * P:t * P + P], On[:, qt % 2, t * P:t * P + P], ident)
                    ins.then_inc(S("at_otr"), 1)
                if nxt is not None:
                    for part in QPARTS.get(u, ()):
                        pe_qpart(pe, f"q{l}", nxt, n + 1, part)
                    if l == 0 and u in (8, 15):
                        pe_qrot(pe, n + 1, u // 15)

        def pe_attn(pe, l):
            n0 = l * NKV
            for t in range(2):
                for part in range(8):
                    pe_qpart(pe, f"q{l}", 0, n0, 8 * t + part)
                if l == 0:
                    pe_qrot(pe, n0, t)
            with pe.Fori(0, NKV - 1) as g:
                pe_units(pe, l, g, g + n0, g + 1)
            pe_units(pe, l, NKV - 1, n0 + NKV - 1, None)

        def act_raw(act, l, i, n, t):
            if t == 0:
                act.wait_ge(S("at_mm"), n + 1)
            else:
                act.wait_ge(S("w_used"), used(f"q{l}", i, 0))
            act.wait_ge(S("at_q"), n * 2 + 1)
            act.activation(v520(raw2[:, t, :]), pair(QPAIR), ACT.Copy).then_inc(S("at_raw"), 1)
            if l == 1:
                act.wait_ge(S("at_raw"), n * 2 + (t + 1))
                act.sem_inc(S("at_pair"), 1)

        def to_qst(eng, copy, l, n, t):
            eng.wait_ge(S("at_s"), n * NU + 1)
            eng.wait_ge(S("at_qall"), n + 1)
            copy(qst[0:HD, 2 * t, :], raw2[0:HD, t, :])
            copy(qst[0:HD, 2 * t + 1, :], raw2[HD:P, t, :]).then_inc(S("at_q"), 1)

        def act_attn(act, l):
            n0 = l * NKV

            def to_place(n):
                if l == 0:
                    act.wait_ge(S("at_rope"), n * 2 + 1)
                else:
                    act.wait_ge(S("at_raw"), n * 2 + 1)
                to_qst(act, lambda out, x: act.activation(out, x, ACT.Copy), l, n, 0)

            def units(n, nxt):
                for u in range(NU + 1):
                    if u < NU:
                        w = (u // GR + 1) * P
                        act.wait_ge(S("at_nm"), n * NU + (u + 1))
                        if u >= 2:
                            act.wait_ge(S("at_tr"), n * NU + (u - 1))
                        act.activation(Pr[:, u % 2, 0:w], Sm[:, u % 2, 0:w], ACT.Exp, bias=nm[:, u:u + 1],
                                       accum_out=lsum[:, u:u + 1]).then_inc(S("at_p"), 1)
                    v = u - 1
                    if 0 <= v:
                        w = (v // GR + 1) * P
                        act.wait_ge(S("at_tr"), n * NU + (v + 1))
                        if v >= 2:
                            act.wait_ge(S("at_o"), n * NU + (v - 1))
                        act.activation(PT[:, v % 2, 0:w], ps[:, 2 + v % 2, 0:w], ACT.Copy).then_inc(S("at_pt"), 1)
                    if nxt is not None:
                        if u < 2:
                            split_high(act, f"q{l}", nxt, 0, u)
                        if u in (7, 14):
                            act_raw(act, l, nxt, n + 1, u // 14)
                if nxt is not None:
                    to_place(n + 1)

            if l == 1:
                for h in range(2):
                    split_high(act, "q1", 0, 0, h)
            for t in range(2):
                act_raw(act, l, 0, n0, t)
            to_place(n0)
            with act.Fori(0, NKV - 1) as g:
                units(g + n0, g + 1)
            units(n0 + NKV - 1, None)

        def dve_attn(dve, l):
            n0 = l * NKV

            def rope(n, t):
                dve.wait_ge(S("at_raw"), n * 2 + (t + 1))
                dve.tensor_tensor(sq[:, 0, :], raw2[:, t, :], const[:, K_COS:K_COS + TOK], ALU.mult).then_inc(S("at_rp"), 1)
                dve.wait_ge(S("at_rot"), n * 2 + (t + 1))
                dve.tensor_tensor(v520(sq[:, 1, :]), pair(QPAIR), v520(const[:, K_SIN:K_SIN + TOK]), ALU.mult).then_inc(S("at_pair"), 1)
                dve.wait_ge(S("at_rp"), n * 2 + (t + 1))
                dve.wait_ge(S("at_pair"), n * 2 + (t + 2))
                dve.tensor_tensor(raw2[:, t, :], sq[:, 0, :], sq[:, 1, :], ALU.add).then_inc(S("at_rope"), 1)
                dve.wait_ge(S("at_rope"), n * 2 + (t + 1))

            def to_place(n):
                if l == 1:
                    dve.wait_ge(S("at_raw"), n * 2 + 2)
                to_qst(dve, dve.tensor_copy, l, n, 1)

            def outputs(g, n, qt):
                dve.wait_ge(S("at_o"), n * NU + (qt * GR + GR))
                dve.reciprocal(rl[:, qt * GR:qt * GR + GR], lsum[:, qt * GR:qt * GR + GR]).then_inc(S("at_rl"), 1)
                dve.wait_ge(S("at_rl"), n * QT + (qt + 1))
                dve.tensor_tensor(On[:, qt % 2, :].rearrange("p (h d) -> p h d", h=GR),
                                  ps[:, 4, 0:PC].rearrange("p (h d) -> p h d", h=GR),
                                  rl[:, qt * GR:qt * GR + GR].unsqueeze(2).to_broadcast([P, GR, HD]), ALU.mult)\
                    .then_inc(S("at_on"), 1)

            def turned_outputs(g, n, qt):
                dve.wait_ge(S("at_otr"), n * QT + (qt + 1))
                dve.tensor_copy(OT[:, ds(g * 2, 2), qt * P:qt * P + P], ps[:, 5, 0:PC].rearrange("p (t c) -> p t c", t=2))\
                    .then_inc(S("at_ot"), 1)

            def units(g, n, nxt):
                for u in range(NU + 3):
                    if u >= GR + 2 and (u - 3) % GR == GR - 1:
                        qt = (u - 3) // GR
                        outputs(g, n, qt)
                    if u < NU:
                        qt, hh = u // GR, u % GR
                        w = (qt + 1) * P
                        mask = maskP[:, qt, 0:w] if l == 0 else const[:, K_CAU + SEQ - w:K_CAU + SEQ]
                        dve.wait_ge(S("at_s"), n * NU + (u + 2))
                        if u >= 2:
                            dve.wait_ge(S("at_p"), n * NU + (u - 1))
                        if l == 0:
                            dve.wait_ge(S("tk_step"), n * NU + (u + 1))
                        settle(dve)
                        if l == 0:
                            if u % 2 == 0:
                                dve.max(small[0:NS, 0:8], scs[0:NS, :]).then_inc(S("tk_step"), 1)
                            else:
                                dve.match_replace(scs[0:NS, :], small[0:NS, 0:8], scs[0:NS, :], TAKEN).then_inc(S("tk_step"), 1)
                        dve.tensor_tensor_reduce(Sm[:, u % 2, 0:w], ps[:, u % 2, 0:w], mask, SCALE, -3e38, ALU.add, ALU.max, mx[:, u:u + 1])\
                            .then_inc(S("at_sm"), 1)
                        dve.wait_ge(S("at_sm"), n * NU + (u + 1))
                        if l == 0:
                            dve.tensor_scalar(nm[:, u:u + 1], mx[:, u:u + 1], -1.0, None, ALU.mult).then_inc(S("at_nm"), 1)
                        else:
                            c = cq[:, qt, ds(g * GR + hh, 1)]
                            dve.tensor_tensor(mx[:, u:u + 1], mx[:, u:u + 1], c, ALU.add).then_inc(S("at_mc"), 1)
                            dve.wait_ge(S("at_mc"), g * NU + (u + 1))
                            dve.tensor_tensor(nm[:, u:u + 1], c, mx[:, u:u + 1], ALU.subtract).then_inc(S("at_nm"), 1)
                    if u >= 2 * GR + 2 and (u - 3) % GR == GR - 1:
                        turned_outputs(g, n, (u - 3) // GR - 1)
                    if nxt is not None:
                        if u in (1, 2):
                            split_low(dve, f"q{l}", nxt, 0, u - 1)
                        if l == 0 and u in (9, 16):
                            rope(n + 1, u // 16)
                        if u == 16:
                            to_place(n + 1)
                turned_outputs(g, n, QT - 1)

            if l == 1:
                for h in range(2):
                    split_low(dve, "q1", 0, 0, h)
            for t in range(2):
                if l == 0:
                    rope(n0, t)
            to_place(n0)
            with dve.Fori(0, NKV - 1) as g:
                units(g, g + n0, g + 1)
            units(NKV - 1, n0 + NKV - 1, None)
            if l == 0:
                assert 4 * NU == 2 * NSEL_S // 8
                dve.wait_ge(S("tk_step"), 1 + 4 * NU)
                dve.tensor_scalar(scs[0:NS, :], scs[0:NS, :], 0.5 * TAKEN, NEG, ALU.is_gt, ALU.mult)

        def pool_attn(pool, l):
            for j in range(2):
                gather(pool, f"K{l}", 0, j, I[f"cache_k_{'ab'[l]}"], j, PC)
            with pool.Fori(0, 2) as i:
                for par in range(2):
                    g = i * 2 + par
                    n = g + l * NKV
                    pool.wait_ge(S("at_q"), n * 2 + 2 + 1)
                    dst = Qall[64 * par:64 * par + 64, ds(i, 1), :].rearrange("p o (b h) -> p (o b) h", h=NH)
                    for hh in range(GR):
                        ins = pool.tensor_copy(dst[:, :, ds(g * GR + hh, 1)].rearrange("p b o -> p (b o)"), qst[0:HD, hh, SEQ:TOK])
                    ins.then_inc(S("at_qall"), 1)
                    pool.wait_ge(S("at_qall"), n + 2)

        def pe_samp(pe, l):
            tag = f"sp{l}"
            for c in range(2):
                if l == 0:
                    pe.matmul(ps[:, 4 + c, :], const[0:NS, K_E16:K_E16 + P], by_token(biasS)[0:NS, 4 * c:4 * c + 4, :], start=True, stop=False)
                else:
                    pe.matmul(ps[:, 4 + c, :], ident, by_token(biasS)[:, 4 * c:4 * c + 4, :], start=True, stop=False)
            with pe.Fori(0, 4) as i:
                for j in range(2):
                    b = i * 2 + j
                    s = panel_ready(pe, f"K{l}", i, j)
                    for c in range(4):
                        pe.wait_ge(S(f"{tag}_kt"), 1 + b * 4)
                        for n in range(4):
                            pg = 4 * (c % 2) + n
                            ins = pe.transpose(ps[:, c, n * P:n * P + P], pages_view(s, PC)[:, pg, (c // 2) * P:(c // 2) * P + P], ident)
                        if c < 3:
                            ins.then_inc(S(f"{tag}_ktr"), 1)
                    panel_used(ins, s)
                    pe.wait_ge(S(f"{tag}_qz"), b + 1)
                    for c in range(4):
                        pe.wait_ge(S(f"{tag}_kt"), 1 + b * 4 + c + 1)
                        ins = pe.matmul(ps[:, 4 + c % 2, :], qz[:, j, c // 2, :], KT[:, c, 0:512], start=False, stop=False)
                    ins.then_inc(S(f"{tag}_qk"), 1)
            for c in range(2):
                pe.matmul(ps[:, 4 + c, :], zeros, const[:, 0:512], start=False, stop=True)
            for half in range(2):
                ins = pe.matmul(ps[:, 6, 0:NS], Qall[:, half, :], knT[:, half, :], start=(half == 0), stop=(half == 1))
            if l == 0:
                ins = pe.matmul(ps[:, 6, 16:17], const[0:NS, K_E16:K_E16 + P], maskS[0:NS, :], start=True, stop=True)
            ins.then_inc(S(f"{tag}_logits"), 1)
            pe.wait_ge(S(f"{tag}_pb"), 1)
            for n in range(NPG):
                ins = pe.transpose(ps[:, n // 4, (n % 4) * P:(n % 4) * P + P], Pb[:, n * P:n * P + P], ident)
            pe.transpose(ps[0:NS, 2, 0:P], pnx, ident).then_inc(S(f"{tag}_ptr"), 1)
            pe.wait_ge(S(f"{tag}_pts"), 2)
            for half in range(2):
                rhs = pnT[0:NS, :].rearrange("p (b h) -> p b h", h=NH)[:, :, 8 * half:8 * half + 8]
                ins = pe.matmul(ps[:, 6, 64 * half:64 * half + 64].rearrange("p (b h) -> p b h", h=8), vnew[0:NS, half * P:half * P + P], rhs,
                                start=True, stop=True)
            with pe.Fori(0, 4) as i:
                for j in range(2):
                    b = i * 2 + j
                    s = panel_ready(pe, f"V{l}", i, j)
                    for half in range(2):
                        for n in range(NPG):
                            ins = pe.matmul(ps[:, 7, ds(b * 8 + 64 * half, 8)], pages_view(s, PC)[:, n, half * P:half * P + P],
                                            PTs[:, n, ds(b * NH + 8 * half, 8)], start=(n == 0), stop=(n == NPG - 1))
                    panel_used(ins, s)
            pe.drain().then_inc(S(f"{tag}_ov"), 1)

        def act_samp(act, l):
            tag = f"sp{l}"
            with act.Fori(0, 4) as i:
                for j in range(2):
                    b = i * 2 + j
                    slot, before, _ = fill(f"K{l}", i, j)
                    act.wait_ge(S(f"{tag}_qk"), 1 + b)
                    for c in range(4):
                        if c < 3:
                            act.wait_ge(S(f"{tag}_ktr"), b * 3 + c + 1)
                        else:
                            act.wait_ge(S(f"ring_free{slot}"), before + 1)
                        act.activation(KT[:, c, 0:512], ps[:, c, :], ACT.Copy).then_inc(S(f"{tag}_kt"), 1)
            act.wait_ge(S(f"{tag}_nm"), 1)
            act.activation(Pb.rearrange("p (a c) -> p a c", a=2), ps[:, 4:6, :], ACT.Exp, bias=ssm[:, 2:3], scale=SCALE,
                           accum_out=ssm[:, 3:4]).then_inc(S(f"{tag}_e"), 1)
            act.activation(ssm[:, 4:5], ssm[:, 0:1], ACT.Exp, bias=ssm[:, 2:3], scale=SCALE).then_inc(S(f"{tag}_e"), 1)
            act.wait_ge(S(f"{tag}_ptr"), 1)
            act.activation(PTs.rearrange("p (a j) c -> p a (j c)", a=2), ps[:, 0:2, :], ACT.Copy).then_inc(S(f"{tag}_pts"), 1)
            act.activation(pnT[0:NS, :], ps[0:NS, 2, 0:P], ACT.Copy).then_inc(S(f"{tag}_pts"), 1)

        def pool_samp(pool, l):
            tag = f"sp{l}"
            K, V = (I[f"cache_{x}_{'ab'[l]}"] for x in "kv")
            in_turn(pool, pool.memset(colmask[:, :, :], 0.0))
            for b in range(NS):
                ins = pool.memset(colmask[:, b, b * NH:b * NH + NH], 1.0)
            in_turn(pool, ins)

            def zeroed(i):
                for j in range(2):
                    pool.wait_ge(S(f"{tag}_qk"), 1 + i * 2)
                    for half in range(2):
                        ins = pool.tensor_tensor(qz[:, j, half, :], Qall[:, half, :],
                                                 colmask[:, ds(i * 2 + j, 1), :].rearrange("p o c -> p (o c)"), ALU.mult)
                    ins.then_inc(S(f"{tag}_qz"), 1)

            for j in range(2):
                gather(pool, f"V{l}", 0, j, V, j, PC)
            for i in range(3):
                zeroed(i)
                for j in range(2):
                    gather(pool, f"K{l}", i + 1, j, K, (i + 1) * 2 + j, PC)
            zeroed(3)
            for i in range(3):
                for j in range(2):
                    gather(pool, f"V{l}", i + 1, j, V, (i + 1) * 2 + j, PC)

        def dve_samp(dve, l):
            tag = f"sp{l}"
            ch = Chain(dve)
            dve.wait_ge(S(f"{tag}_logits"), 1)
            ch.link(dve.tensor_tensor_reduce(ssm[:, 8:16], ps[:, 6, 0:NS], diag16, 1.0, 0.0, ALU.mult, ALU.add, ssm[:, 0:1]))
            if l == 0:
                ch.link(dve.tensor_tensor(ssm[:, 0:1], ssm[:, 0:1], ps[:, 6, 16:17], ALU.add))
            ch.link(dve.tensor_reduce(ssm[:, 1:2], ps[:, 4:6, :], AX.XY, ALU.max))
            ch.link(dve.tensor_tensor(ssm[:, 1:2], ssm[:, 1:2], ssm[:, 0:1], ALU.max))
            dve.tensor_scalar(ssm[:, 2:3], ssm[:, 1:2], -SCALE, None, ALU.mult).then_inc(S(f"{tag}_nm"), 1)
            dve.wait_ge(S(f"{tag}_e"), 2)
            ch.link(dve.tensor_tensor(ssm[:, 3:4], ssm[:, 3:4], ssm[:, 4:5], ALU.add))
            ch.link(dve.reciprocal(ssm[:, 5:6], ssm[:, 3:4]))
            ch.link(dve.tensor_tensor(ssm[:, 4:5], ssm[:, 4:5], ssm[:, 5:6], ALU.mult))
            dve.tensor_scalar(pnx, diag16, ssm[:, 4:5], None, ALU.mult)
            dve.tensor_scalar(Pb, Pb, ssm[:, 5:6], None, ALU.mult).then_inc(S(f"{tag}_pb"), 1)
            dve.wait_ge(S(f"{tag}_ov"), 1)
            ch.link(dve.tensor_copy(ovs, ps[:, 6, 0:P]))
            ch.link(dve.tensor_tensor(ovs, ovs, ps[:, 7, 0:P], ALU.add))
            o = ovs.rearrange("p (a b h) -> p a h b", a=2, h=8)
            for half in range(2):
                for lo in range(2):
                    for odd in range(2):
                        dve.tensor_copy(OT[64 * odd:64 * odd + 64, 4 * half + 2 * lo:4 * half + 2 * lo + 2, SEQ:TOK],
                                        o[64 * lo:64 * lo + 64, half, 4 * lo + odd:4 * lo + 4:2, :])

        def residual(dve, ch, l, chunk, m, p, gate=None):
            row = ada[:, ds(l * NADA + chunk * KC + m, 1), :].rearrange("p o c -> p (o c)")
            x = xT[:, ds(m, 1), :].rearrange("p o t -> p (o t)")
            dve.scalar_tensor_tensor(out=x[:, 0:HT], in0=ps[:, 2 * p, 0:HT], scalar=row[:, 0:1], in1=x[:, 0:HT], op0=ALU.mult, op1=ALU.add)
            dve.scalar_tensor_tensor(out=x[:, HT:SEQ], in0=ps[:, 2 * p + 1, 0:SEQ - HT], scalar=row[:, 0:1], in1=x[:, HT:SEQ],
                                     op0=ALU.mult, op1=ALU.add)
            ch(dve.tensor_tensor(tmp8[:, :], ps[:, 2 * p + 1, SEQ - HT:HT], row[:, 1:CC], ALU.mult))
            return dve.tensor_tensor(x[:, SEQ:TOK], x[:, SEQ:TOK], tmp8[:, :], ALU.add)

        def pe_out(pe, l):
            for j in range(4):
                for h in range(2):
                    half_ready(pe, f"o{l}", 0, j, h)
                    if j == 0:
                        pe.wait_ge(S("o_lo"), 2 * l + h + 1)
                    if j >= 2 and h == 0:
                        pe.wait_ge(S(f"o{l}_res"), 2 * j - 2)
                    mm_half(pe, h, (2 * j % 4, 2 * j % 4 + 1), HK * h, HK, h == 0, h == 1)

        def act_out(act, l):
            for j in range(4):
                for h in range(2):
                    split_high(act, f"o{l}", 0, j, h)
                    if j == 0:
                        act.activation(hH[:, HK * h:HK * h + HK, :], OT[:, HK * h:HK * h + HK, :], ACT.Copy).then_inc(S("o_hi"), 1)

        def dve_out(dve, l):
            ch = Chain(dve)
            for j in range(5):
                if j < 4:
                    for h in range(2):
                        split_low(dve, f"o{l}", 0, j, h)
                        if j == 0:
                            dve.wait_ge(S("o_hi"), 2 * l + h + 1)
                            dve.tensor_tensor(hL[:, HK * h:HK * h + HK, :], OT[:, HK * h:HK * h + HK, :],
                                              hH[:, HK * h:HK * h + HK, :].bitcast(F32), ALU.subtract).then_inc(S("o_lo"), 1)
                if j >= 1:
                    dve.wait_ge(S("w_used"), used(f"o{l}", 0, j - 1))
                    for m in (2 * j - 2, 2 * j - 1):
                        residual(dve, ch.link, l, 2, m, m % 4).then_inc(S(f"o{l}_res"), 1)
                        dve.wait_ge(S(f"o{l}_res"), m + 1)

        def pe_up(pe, l):
            tag = f"up{l}"

            def two(sec, i, q, k, wait=None):
                pe.wait_ge(S("up_afree"), k * 2 + (l * FC + 2))
                mm_panel(pe, sec, i, 2 * q, (0, 2), wait)
                pe.wait_ge(S("up_bfree"), k * 2 + (l * FC + 2))
                mm_panel(pe, sec, i, 2 * q + 1, (1, 3))

            two(f"{tag}h", 0, 0, 0, split_input(pe, 2 * l + 1))
            with pe.Fori(0, 5) as i:
                for q in range(2):
                    two(tag, i, q, i * 2 + (1 + q))
            pe.wait_ge(S("up_acv"), 1 + l * FC + FC)
            pe.wait_ge(S("up_bfree"), l * FC + FC + 2)
            pe.wait_ge(S("up_afree"), l * FC + FC + 2)
            for q in range(NCV):
                if q >= 2:
                    pe.wait_ge(S("up_cvo"), l * NCV + q - 1)
                for n in range(min(4, FC - 4 * q)):
                    ins = pe.transpose(ps[0:10, q % 2, n * P:n * P + P], acv[:, 4 * q + n, :], ident)
                ins.then_inc(S("up_cvt"), 1)

        def act_up(act, l):
            tag = f"up{l}"
            if l == 0:
                act.sem_inc(S("up_afree"), 2)

            def tile(f, t):
                fr = ds(f, 1)
                act.wait_ge(S("up_c3"), f + (1 + l * FC))
                act.wait_ge(S("up_acv"), f + (1 + l * FC))
                act.wait_ge(S("up_bfree"), f + (l * FC + 1))
                act.activation(v520(aS[:, t, 2:2 + TOK]), pair(2 * t), ACT.Copy).then_inc(S("up_afree"), 1)
                act.wait_ge(S("up_afree"), l * FC + f + 3)
                cw = cwT[:, fr, :].rearrange("p o c -> p (o c)")
                act.activation(cvA[:, t, 0:SEQ], aS[:, t, 0:SEQ], ACT.Identity, scale=cw[:, 20 * l + 16:20 * l + 17],
                               bias=cw[:, 20 * l + 19:20 * l + 20]).then_inc(S("up_c1"), 1)
                act.wait_ge(S("up_c3"), 1 + l * FC + f + 1)
                act.activation(cvA[:, t, :], cvA[:, t, :], ACT.Silu).then_inc(S("up_silu"), 1)

            def two(sec, i, q, k, panels=range(2)):
                for j in [2 * q + p for p in panels]:
                    for h in range(2):
                        split_high(act, sec, i, j, h)
                act.wait_ge(S("w_used"), used(sec, i, 2 * q))
                for t in range(2):
                    tile(k * 2 + t, t)

            two(f"{tag}h", 0, 0, 0, range(1, 2))
            with act.Fori(0, 5) as i:
                for q in range(2):
                    two(tag, i, q, i * 2 + (1 + q))
            for q in range(NCV):
                n = min(4, FC - 4 * q)
                act.wait_ge(S("up_cvt"), l * NCV + q + 1)
                act.activation(cvrow[0:10, 4 * q * P:(4 * q + n) * P], ps[0:10, q % 2, 0:n * P], ACT.Copy).then_inc(S("up_cvo"), 1)
            act.wait_ge(S("up_cvo"), l * NCV + NCV)
            act.dma_start(O["conv_p"][l], cvrow[0:2, :]).then_inc(S("stores"), 16)
            act.dma_start(O["conv_s"][l, :, 1, :], cvrow[2:10, :]).then_inc(S("stores"), 16)
            act.dma_start(O["conv_s"][l, :, 0, :], I["state_conv"][l, :, 1, :]).then_inc(S("stores"), 16)

        def dve_up(dve, l):
            tag = f"up{l}"
            if l == 0:
                dve.sem_inc(S("up_bfree"), 2)

            def conv(f, t):
                fr = ds(f, 1)
                cw = cwT[:, fr, :].rearrange("p o c -> p (o c)")
                w1, w2 = cw[:, 20 * l + 17:20 * l + 18], cw[:, 20 * l + 18:20 * l + 19]
                dve.wait_ge(S("up_c1"), l * FC + f + 1)
                dve.scalar_tensor_tensor(out=cvA[:, t, 0:SEQ], in0=aS[:, t, 1:SEQ + 1], scalar=w1, in1=cvA[:, t, 0:SEQ],
                                         op0=ALU.mult, op1=ALU.add).then_inc(S("up_c2"), 1)
                dve.scalar_tensor_tensor(out=cvA[:, t, SEQ:TOK], in0=aS[:, t, SEQ + 2:TOK + 2], scalar=w2,
                                         in1=cs0[:, l, fr, :].rearrange("p o c -> p (o c)"), op0=ALU.mult, op1=ALU.add)
                dve.wait_ge(S("up_c2"), l * FC + f + 1)
                dve.scalar_tensor_tensor(out=cvA[:, t, 0:SEQ], in0=aS[:, t, 2:SEQ + 2], scalar=w2, in1=cvA[:, t, 0:SEQ],
                                         op0=ALU.mult, op1=ALU.add).then_inc(S("up_c3"), 1)

            def gates(done, k):
                dve.wait_ge(S("w_used"), done)
                for t in range(2):
                    f = k * 2 + t
                    dve.wait_ge(S("up_silu"), l * FC + f + 1)
                    dve.tensor_tensor(v520(gT[:, ds(f, 1), :].rearrange("p o t -> p (o t)")), pair(2 * t + 1), v520(cvA[:, t, :]), ALU.mult)\
                        .then_inc(S("up_bfree"), 1)

            def lows(sec, i, j):
                for h in range(2):
                    split_low(dve, sec, i, j, h)

            lows(f"{tag}h", 0, 1)
            for t in range(2):
                conv(t, t)
            with dve.Fori(0, 5) as i:
                for q in range(2):
                    lows(tag, i, 2 * q)
                    gates(half_no(tag, i, 2 * q, 0) + 2, i * 2 + q)
                    lows(tag, i, 2 * q + 1)
                    for t in range(2):
                        conv((i * 2 + (1 + q)) * 2 + t, t)
            gates(used(tag, 4, 3), 10)

        def pool_up(pool, l):
            tag = f"up{l}"

            def tile(f, t):
                pool.wait_ge(S("up_c1"), l * FC + f + 1)
                pool.tensor_copy(acv[:, ds(f, 1), :].rearrange("p o c -> p (o c)"), aS[:, t, SEQ:SEQ + 10]).then_inc(S("up_acv"), 1)

            with pool.Fori(0, 5) as i:
                for q in range(4):
                    tile(i * 4 + q, q % 2)
            for q in range(2):
                tile(20 + q, q)

        GROUPS = [(8 * n, min(8, FC - 8 * n)) for n in range((FC + 7) // 8)]

        def halves_of(n):
            return [(h, min(HK, GROUPS[n][1] - HK * h)) for h in range(2)]

        def pe_down(pe, l):
            tag = f"dn{l}"
            with pe.Fori(0, 2) as i:
                for n in range(len(GROUPS)):
                    for q in range(2):
                        if n == 0:
                            pe.wait_ge(S(f"{tag}_free"), i * 4 + (2 * q + 2))
                        for h, nk in halves_of(n):
                            half_ready(pe, tag, i, 2 * n + q, h)
                            if q == 0:
                                pe.wait_ge(S("g_lo"), i * 6 + (12 * l + 2 * n + h + 1))
                            mm_half(pe, h, (2 * q, 2 * q + 1), HK * h, nk, n == 0 and h == 0, n == 2 and h == 1)

        def act_down(act, l):
            tag = f"dn{l}"
            with act.Fori(0, 2) as i:
                for n, (g0, _) in enumerate(GROUPS):
                    for q in range(2):
                        for h, nk in halves_of(n):
                            split_high(act, tag, i, 2 * n + q, h, nk)
                            if q == 0:
                                act.activation(hH[:, HK * h:HK * h + nk, :], gT[:, g0 + HK * h:g0 + HK * h + nk, :], ACT.Copy)\
                                    .then_inc(S("g_hi"), 1)

        def dve_down(dve, l):
            tag = f"dn{l}"
            dve.sem_inc(S(f"{tag}_free"), 4)
            with dve.Fori(0, 2) as i:
                for n, (g0, _) in enumerate(GROUPS):
                    for q in range(2):
                        for h, nk in halves_of(n):
                            split_low(dve, tag, i, 2 * n + q, h, nk)
                            if q == 0:
                                dve.wait_ge(S("g_hi"), i * 6 + (12 * l + 2 * n + h + 1))
                                dve.tensor_tensor(hL[:, HK * h:HK * h + nk, :], gT[:, g0 + HK * h:g0 + HK * h + nk, :],
                                                  hH[:, HK * h:HK * h + nk, :].bitcast(F32), ALU.subtract).then_inc(S("g_lo"), 1)
                for q in range(2):
                    dve.wait_ge(S("w_used"), used(tag, i, 4 + q))
                    for t in range(2):
                        m = i * 4 + q * 2 + t

                        def link(ins, m=m):
                            ins.then_inc(S(f"{tag}_dve"), 1)
                            dve.wait_ge(S(f"{tag}_dve"), m + 1)
                        residual(dve, link, l, 5, m, 2 * q + t).then_inc(S(f"{tag}_free"), 1)
                        dve.wait_ge(S(f"{tag}_free"), m + 5)

        FIN_GROUPS = 2 * QT + 2

        @block.tensor
        def _(pe):
            pe.wait_ge(S("in_const"), 16)
            pe.wait_ge(S("in_vec"), 96)
            for kc in range(KC):
                pe.transpose(ps[:, 0, kc * CC:kc * CC + CC], cload[0:CC, kc * P:kc * P + P], ident[0:CC, 0:CC])
            pe.transpose(ps[:, 1, 0:96], vrow[0:96, :], ident[0:96, 0:96])
            pe.transpose(ps[:, 1, 96:136], vrow2[0:40, :], ident[0:40, 0:40]).then_inc(S("pr_vec"), 1)
            pe.wait_ge(S("in_x"), 32)
            for kc in range(KC):
                if kc >= 2:
                    pe.wait_ge(S("pr_xe"), 2 * (kc - 1))
                b = 2 + 2 * (kc % 2)
                for t in range(QT):
                    pe.transpose(ps[:, b, t * P:t * P + P], xload[:, t, kc * P:kc * P + P], ident)
                pe.transpose(ps[:, b + 1, 0:NS], xsload[0:NS, kc * P:kc * P + P], ident[0:NS, 0:NS]).then_inc(S("pr_x"), 1)
            pe.wait_ge(S("in_conv"), 96)
            for f in range(FC):
                ins = pe.transpose(ps[:, 6 + f // 11, (f % 11) * 40:(f % 11) * 40 + 40], crow[0:40, f * P:f * P + P], ident[0:40, 0:40])
            ins.then_inc(S("pr_cw"), 1)
            pe.wait_ge(S("pr_tab"), 1)
            pe.matmul(ps[:, 1, 256:256 + NS], const[0:NPG, K_E16:K_E16 + P], tablef[:, :], start=True, stop=True).then_inc(S("pr_pages"), 1)
            phase_end(pe, "pe")
            pe_ada(pe, "ada0a", 2, 0)
            phase_end(pe, "pe")
            for l in range(DEPTH):
                if l == 1:
                    pe_ada(pe, "ada1", 6, 24)
                    phase_end(pe, "pe")
                pe_rms(pe, 2 * l)
                pe_head(pe, l)
                phase_end(pe, "pe")
                if l == 0:
                    pe_score(pe)
                    phase_end(pe, "pe")
                    pe_ada(pe, "ada0b", 4, 8)
                else:
                    pe_logf(pe)
                phase_end(pe, "pe")
                pe_attn(pe, l)
                phase_end(pe, "pe")
                pe_samp(pe, l)
                phase_end(pe, "pe")
                pe_out(pe, l)
                pe_rms(pe, 2 * l + 1)
                pe_up(pe, l)
                phase_end(pe, "pe")
                pe_down(pe, l)
                if l == 0:
                    phase_end(pe, "pe")
            pe_rms(pe, 4)
            phase_end(pe, "pe")
            for n in range(FIN_GROUPS):
                t, half = n // 2, n % 2
                if n >= 4:
                    pe.wait_ge(S("fi_y"), n - 3)
                for k in range(4):
                    if t < QT:
                        ins = pe.transpose(ps[:, n % 4, k * P:k * P + P], hT[:, 4 * half + k, t * P:t * P + P], ident)
                    else:
                        ins = pe.transpose(ps[0:NS, n % 4, k * P:k * P + P], hT[:, 4 * half + k, SEQ:TOK], ident)
                ins.then_inc(S("fi_t"), 1)
            phase_end(pe, "pe")

        @block.scalar
        def _(act):
            act.dma_start(xload, I["x_prompt"][0].rearrange("(t p) d -> p t d", p=P)).then_inc(S("in_x"), 16)
            act.dma_start(xsload[0:NS, :], I["x_sample"].rearrange("b o d -> (b o) d")).then_inc(S("in_x"), 16)
            for l in range(DEPTH):
                act.dma_start(crow[20 * l:20 * l + 16, :], I["state_conv"][l].rearrange("b w f -> (b w) f")).then_inc(S("in_conv"), 16)
                act.dma_start(crow[20 * l + 16:20 * l + 19, :], I["conv_w"][l]).then_inc(S("in_conv"), 16)
                act.dma_start(crow[20 * l + 19:20 * l + 20, :], I["conv_b"][l:l + 1, :]).then_inc(S("in_conv"), 16)
            act.dma_start(table[:, :], I["page_table"].rearrange("b j -> j b"), allow_slow_non_contiguous=True).then_inc(S("in_table"), 16)
            act.dma_start(bfb[:, :], I["b_f"].partition_broadcast(P)).then_inc(S("in_bf"), 16)
            act.wait_ge(S("pr_vec"), 1)
            act.activation(cT[:, :, :], ps[:, 0, 0:KC * CC].rearrange("p (k c) -> p k c", k=KC), ACT.Silu).then_inc(S("pr_silu"), 1)
            act.activation(badaT[:, :], ps[:, 1, 0:96], ACT.Copy)
            act.wait_ge(S("pr_c2z"), 1)
            act.wait_ge(S("pr_silu"), 1)
            act.activation(c2[:, :, 0:CC], cT[:, :, :], ACT.Copy).then_inc(S("pr_chi"), 1)
            act.activation(vT[:, :], ps[:, 1, 96:136], ACT.Copy)
            for kc in range(KC):
                act.wait_ge(S("pr_x"), kc + 1)
                act.activation(xT[:, kc, 0:SEQ], ps[:, 2 + 2 * (kc % 2), :], ACT.Copy).then_inc(S("pr_xe"), 1)
                act.activation(xT[:, kc, SEQ:TOK], ps[:, 3 + 2 * (kc % 2), 0:NS], ACT.Copy).then_inc(S("pr_xe"), 1)
            act.wait_ge(S("pr_cw"), 1)
            for h in range(2):
                act.activation(cwT[:, 11 * h:11 * h + 11, :], ps[:, 6 + h, 0:440].rearrange("p (k c) -> p k c", k=11), ACT.Copy)\
                    .then_inc(S("pr_cwe"), 1)
            phase_end(act, "act")
            act_ada(act, "ada0a", 2, 0, 0)
            phase_end(act, "act")
            for l in range(DEPTH):
                base = l * NADA
                if l == 1:
                    act_ada(act, "ada1", 6, NADA, 24)
                    phase_end(act, "act")
                act_rms(act, 2 * l, ada[:, base:base + KC, :], None)
                act_head(act, l)
                phase_end(act, "act")
                if l == 0:
                    act_score(act)
                    phase_end(act, "act")
                    act_ada(act, "ada0b", 4, 2 * KC, 8)
                else:
                    act_logf(act)
                phase_end(act, "act")
                act_attn(act, l)
                phase_end(act, "act")
                act_samp(act, l)
                phase_end(act, "act")
                act_out(act, l)
                act_rms(act, 2 * l + 1, ada[:, base + 3 * KC:base + 4 * KC, :], None)
                act_up(act, l)
                phase_end(act, "act")
                act_down(act, l)
                act.wait_ge(S("stores"), 16 * STORES[2 * l + 1])
                if l == 0:
                    phase_end(act, "act")
            act_rms(act, 4, None, vT[:, 32:40])
            phase_end(act, "act")
            for n in range(FIN_GROUPS):
                t, half = n // 2, n % 2
                act.wait_ge(S("fi_t"), n + 1)
                if t < QT:
                    if t >= 2 and half == 0:
                        act.wait_ge(S(f"fi_out{t % 2}"), 16 * (t // 2))
                    act.activation(ytok[:, t % 2, half * 512:half * 512 + 512], ps[:, n % 4, :], ACT.Copy).then_inc(S("fi_y"), 1)
                    if half == 1:
                        act.wait_ge(S("fi_y"), n + 1)
                        act.dma_start(O["y_p"][t * P:t * P + P, :], ytok[:, t % 2, :]).then_inc(S(f"fi_out{t % 2}"), 16)
                else:
                    act.activation(ysam[0:NS, half * 512:half * 512 + 512], ps[0:NS, n % 4, :], ACT.Copy).then_inc(S("fi_y"), 1)
            act.wait_ge(S("fi_y"), FIN_GROUPS)
            act.dma_start(O["y_s"], ysam[0:NS, :]).then_inc(S("stores"), 16)
            act.wait_ge(S("fi_out0"), 32)
            act.wait_ge(S("fi_out1"), 32)
            act.wait_ge(S("stores"), 16 * STORES[4])
            phase_end(act, "act")

        @block.vector
        def _(dve):
            ch = Chain(dve)
            dve.memset(epsc[:, :], EPS)
            dve.memset(ones[:, :], 1.0)
            ch.link(dve.memset(zeros[:, :], 0.0))
            for n in range(2):
                ins = dve.tensor_copy(c2[:, :, n * (CC + 1):n * (CC + 1) + CC + 1], zeros[:, 0:KC * (CC + 1)].rearrange("p (k c) -> p k c", k=KC))
            ins.then_inc(S("pr_c2z"), 1)
            dve.wait_ge(S("in_table"), 16)
            dve.tensor_copy(tablef[:, :], table[:, :]).then_inc(S("pr_tab"), 1)
            dve.wait_ge(S("pr_pages"), 1)
            dve.tensor_scalar(idx[:, :], ps[:, 1, 256:256 + NS], 16.0, const[:, K_B16:K_B16 + 1], ALU.mult, ALU.add)
            dve.wait_ge(S("pr_chi"), 1)
            dve.tensor_tensor(c2[:, :, CC + 1:CC + 1 + CC], cT[:, :, :], c2[:, :, 0:CC].bitcast(F32), ALU.subtract)
            dve.wait_ge(S("pr_cwe"), 2)
            for l in range(DEPTH):
                c = cwT[:, :, 20 * l:20 * l + 20]
                st0, st1 = c[:, :, 0:16:2], c[:, :, 1:16:2]

                def tap(n, c=c):
                    return c[:, :, n:n + 1].to_broadcast([P, FC, NS])
                u = sq[:, 0, 0:FC * NS].rearrange("p (k c) -> p k c", k=FC)
                ch.link(dve.tensor_tensor(cs0[:, l, :, :], st0, tap(16), ALU.mult))
                ch.link(dve.tensor_tensor(u, st1, tap(17), ALU.mult))
                ch.link(dve.tensor_tensor(cs0[:, l, :, :], cs0[:, l, :, :], u, ALU.add))
                ch.link(dve.tensor_tensor(cs0[:, l, :, :], cs0[:, l, :, :], tap(19), ALU.add))
            phase_end(dve, "dve")
            low_ada(dve, "ada0a", 2)
            phase_end(dve, "dve")
            for l in range(DEPTH):
                base = l * NADA
                if l == 1:
                    low_ada(dve, "ada1", 6)
                    phase_end(dve, "dve")
                dve_rms(dve, 2 * l, ada[:, base:base + KC, :], ada[:, base + KC:base + 2 * KC, :], vT[:, 8 * l:8 * l + 8])
                if l == 1:
                    dve.wait_ge(S("in_bf"), 16)
                dve_head(dve, l)
                phase_end(dve, "dve")
                if l == 0:
                    dve_score(dve)
                    phase_end(dve, "dve")
                    dve_topk(dve)
                else:
                    dve_logf(dve)
                phase_end(dve, "dve")
                dve_attn(dve, l)
                phase_end(dve, "dve")
                dve_samp(dve, l)
                phase_end(dve, "dve")
                dve_out(dve, l)
                dve_rms(dve, 2 * l + 1, ada[:, base + 3 * KC:base + 4 * KC, :], ada[:, base + 4 * KC:base + 5 * KC, :],
                        vT[:, 16 + 8 * l:24 + 8 * l])
                dve_up(dve, l)
                phase_end(dve, "dve")
                dve_down(dve, l)
                if l == 0:
                    phase_end(dve, "dve")
            dve_rms(dve, 4, None, None, None)
            phase_end(dve, "dve")
            phase_end(dve, "dve")

        @block.gpsimd
        def _(pool):
            for name in CREDITED:
                pool.sem_inc(S(name), 1)
            pool.memset(colmask8[:, :, :], 0.0).then_inc(S("pl_z"), 1)
            pool.wait_ge(S("pl_z"), 1)
            for b in range(NS):
                pool.memset(colmask8[:, b, b * NIH:b * NIH + NIH], 1.0)
            phase_end(pool, "pool")
            phase_end(pool, "pool")
            for l in range(DEPTH):
                if l == 1:
                    phase_end(pool, "pool")
                in_turn(pool, pool.memset(Qall[:, :, :], 0.0))
                if l == 1:
                    in_turn(pool, pool.memset(lf[:, :, :], 0.0))
                else:
                    in_turn(pool, pool.memset(kaug[64:68, :, 0:SEQ], 0.0))
                pool.dma_start(qst[HD:HD + GR, :, 0:SEQ], I["hsel"]).then_inc(S("in_hsel"), 16)
                pool.wait_ge(S("in_hsel"), 16 * (l + 1))
                pool_rms(pool, 2 * l)
                pool_head(pool, l)
                if l == 1:
                    slot_free(pool, "logf", 0, 0)
                    for b in range(NS):
                        gather_logf(pool, b)
                phase_end(pool, "pool")
                if l == 0:
                    pool_score(pool)
                    phase_end(pool, "pool")
                    low_even(pool, "ada0b", 4)
                phase_end(pool, "pool")
                pool_attn(pool, l)
                phase_end(pool, "pool")
                pool_samp(pool, l)
                phase_end(pool, "pool")
                for t in range(2):
                    pool.memset(aS[:, t, 0:2], 0.0)
                pool_rms(pool, 2 * l + 1)
                pool_up(pool, l)
                phase_end(pool, "pool")
                if l == 0:
                    phase_end(pool, "pool")
            phase_end(pool, "pool")
            phase_end(pool, "pool")


def _constants():
    f = np.float32
    c = np.zeros((P, K_N), f)
    c[:, K_ID:K_ID + P] = np.eye(P, dtype=f)
    half = HD // 4 // 2
    pos = np.concatenate([np.arange(SEQ), np.full(NS, PAST)]).astype(f)
    inv = (f(500000.0) ** (-np.arange(half, dtype=f) / f(half))).astype(f)
    ang = (pos[None, :] * inv[:, None]).astype(f)
    c[:, K_COS:K_COS + TOK] = 1.0
    for p in range(P):
        d = p % HD
        if d < 2 * half:
            c[p, K_ROT + (p ^ half)] = 1.0
            c[p, K_COS:K_COS + TOK] = np.cos(ang[d % half])
            c[p, K_SIN:K_SIN + TOK] = np.sin(ang[d % half]) * (-1.0 if d < half else 1.0)
    p = np.arange(P)[:, None]
    c[:, K_TRI:K_TRI + 896] = p <= np.arange(896)[None, :] - 384
    c[:, K_CAU:K_CAU + 512] = np.where(np.arange(512)[None, :] - 384 <= p, 0.0, NEG)
    c[:, K_D16:K_D16 + 8] = p // 16 == np.arange(8)[None, :]
    c[:, K_D8:K_D8 + 8] = p // 8 == np.arange(8)[None, :]
    c[:, K_E16:K_E16 + 128] = p == np.arange(128)[None, :] // 16
    c[:, K_E8:K_E8 + 64] = p == np.arange(64)[None, :] // 8
    c[:, K_B16] = np.arange(P) % 16
    c[0:CP, K_SUM:K_SUM + CC] = np.arange(CP)[:, None] % (CC + 1) == np.arange(CC)[None, :]
    hsel = np.zeros((GR, GR, SEQ), f)
    hsel[np.arange(GR), np.arange(GR), :] = 1.0
    return c, hsel


_POOL_PAGES = None
_INS = ["x_prompt", "x_sample", "cache_k_a", "cache_v_a", "cache_kidx_a", "cache_k_b", "cache_v_b", "cache_logf_b",
        "state_conv", "page_table", "c_prompt", "c_sample", "w_ada", "b_ada", "g_mix", "g_ffn", "w_in_a", "w_o_a",
        "w_in_b", "b_f", "w_o_b", "w_up", "conv_w", "conv_b", "w_down", "g_final"]
_OUTS = [("y_p", (SEQ, D), (1, SEQ, D)), ("y_s", (NS, D), (NS, 1, D)),
         ("k_a_p", (SEQ, PC), (1, 1, SEQ, NKV, HD)), ("v_a_p", (SEQ, PC), (1, 1, SEQ, NKV, HD)),
         ("kidx_p", (SEQ, HD), (1, 1, SEQ, HD)),
         ("k_b_p", (SEQ, PC), (1, 1, SEQ, NKV, HD)), ("v_b_p", (SEQ, PC), (1, 1, SEQ, NKV, HD)),
         ("logf_p", (SEQ, NH), (1, 1, SEQ, NH)), ("conv_p", (DEPTH, CW - 1, FF), (DEPTH, 1, CW - 1, FF)),
         ("k_a_s", (NS, PC), (1, NS, 1, NKV, HD)), ("v_a_s", (NS, PC), (1, NS, 1, NKV, HD)),
         ("kidx_s", (NS, HD), (1, NS, 1, HD)),
         ("k_b_s", (NS, PC), (1, NS, 1, NKV, HD)), ("v_b_s", (NS, PC), (1, NS, 1, NKV, HD)),
         ("logf_s", (NS, NH), (1, NS, 1, NH)), ("conv_s", (DEPTH, NS, CW - 1, FF), (DEPTH, NS, CW - 1, FF))]


def kernel(**inputs):
    import concourse.bacc as _bacc
    from concourse.bass_utils import run_bass_kernel_spmd as _run

    nc = _bacc.Bacc("TRN2", target_bir_lowering=False, num_devices=1)
    arrays, I, O = {}, {}, {}

    def give(name, a):
        a = np.ascontiguousarray(a)
        arrays[f"in_{name}"] = a
        I[name] = nc.dram_tensor(f"in_{name}", a.shape, mybir.dt.from_np(a.dtype), kind="ExternalInput").ap()

    for name in _INS:
        a = np.asarray(inputs[name])
        if name.startswith("cache"):
            a = a.reshape(a.shape[1], PAGE, -1)
        give(name, a)
    const, hsel = _constants()
    give("const", const)
    give("hsel", hsel)
    for name, shape, _ in _OUTS:
        O[name] = nc.dram_tensor(f"out_{name}", shape, F32, kind="ExternalOutput").ap()
    build(nc, I, O)
    r = _run(nc, [arrays], core_ids=[0])
    return tuple(r.results[0][f"out_{name}"].reshape(full) for name, _, full in _OUTS)
```

```python
from contextlib import ExitStack

import numpy as np

import concourse.bass as bass
from concourse import mybir

F32 = mybir.dt.float32
F32R = mybir.dt.float32r
I32 = mybir.dt.int32
ALU = mybir.AluOpType
ACT = mybir.ActivationFunctionType
AX = mybir.AxisListType
ds = bass.ds

P = 128
D = 1024
SEQ = 512
NS = 8
TOK = SEQ + NS
HT = TOK // 2
KC = D // P
NH, NKV, HD = 16, 4, 64
GR = NH // NKV
NIH = 8
PAST, PAGE = 1024, 128
NPG = PAST // PAGE
FF = 2816
FC = FF // P
CW = 3
DEPTH = 2
QKV = (NH + 2 * NKV) * HD
IN_A = QKV + NIH * HD + HD + NIH
IN_B = QKV + NH
NSEL_P = 128
NSEL_S = 256
QT = SEQ // P
EPS = 1e-6
SCALE = HD ** -0.5
NEG = -1e30
TAKEN = -3e38
NCV = (FC + 3) // 4
NADA = 6 * D // P
CC = 9
PC = 256
R = 4
HK = 4
CP = 2 * (CC + 1)

K_ID, K_ROT, K_COS, K_SIN = 0, 128, 256, 256 + TOK
K_TRI = K_SIN + TOK
K_CAU = K_TRI + 896
K_D16 = K_CAU + 512
K_D8 = K_D16 + 8
K_E16 = K_D8 + 8
K_E8 = K_E16 + 128
K_B16 = K_E8 + 64
K_SUM = K_B16 + 1
K_N = K_SUM + CC

W = 16
SECTIONS = [("ada0a", [(s, W) for s in (0, 1, 2, 3)], 2),
            ("head0", [(s, W) for s in (0, 1, 2, 3, 0)], 1),
            ("kidx", [(s, W) for s in (1, 2)], 4),
            ("ada0b", [(s, W) for s in (3, 0, 1, 2)], 4),
            ("q0", [(3, W)], 4),
            ("K0", [(s, W) for s in (1, 2)], 4),
            ("V0", [(s, W) for s in (3, 0, 1, 2)], 2),
            ("o0", [(s, W) for s in (3, 0, 1, 2)], 1),
            ("up0h", [(s, W) for s in (3, 0)], 1),
            ("up0", [(s, W) for s in (1, 2, 3, 0)], 5),
            ("dn0", [(s, W) for s in (1, 2, 3, 0, 1, 2)], 2),
            ("ada1", [(s, W) for s in (3, 0, 1, 2)], 6),
            ("head1", [(s, W) for s in (3, 0, 1)], 1),
            ("logf", [(2, W * NS)], 1),
            ("q1", [(3, W)], 4),
            ("K1", [(s, W) for s in (0, 1)], 4),
            ("V1", [(s, W) for s in (2, 3, 0, 1)], 2),
            ("o1", [(s, W) for s in (2, 3, 0, 1)], 1),
            ("up1h", [(s, W) for s in (2, 3)], 1),
            ("up1", [(s, W) for s in (0, 1, 2, 3)], 5),
            ("dn1", [(s, W) for s in (0, 1, 2, 3, 0, 1)], 2)]


GROUPS = [(0, FC - 16), (FC - 16, 8), (FC - 8, 8)]
GATHERED = ("kidx", "K0", "V0", "logf", "K1", "V1")


def _ring_counts():
    fills, out = [1] * R, {}
    value = {True: [0] * R, False: [0] * R}
    for name, body, turns in SECTIONS:
        val, per_f, per_v = value[name in GATHERED], [0] * R, [0] * R
        for s, inc in body:
            per_f[s] += 1
            per_v[s] += inc
        out[name] = (body, list(fills), list(val), per_f, per_v)
        for s in range(R):
            fills[s] += per_f[s] * turns
            val[s] += per_v[s] * turns
    return out


RING = _ring_counts()


def full_name(sec, s):
    return f"past_full{s}" if sec in GATHERED else f"ring_full{s}"


def fill(sec, i, j):
    body, f0, v0, per_f, per_v = RING[sec]
    s = body[j][0]
    nf = sum(1 for t, _ in body[:j] if t == s)
    nv = sum(inc for t, inc in body[:j + 1] if t == s)
    return s, i * per_f[s] + (f0[s] + nf), i * per_v[s] + (v0[s] + nv)


def _half_counts():
    out, n = {}, 0
    for name, body, turns in SECTIONS:
        if name not in GATHERED:
            out[name] = n
            n += 2 * len(body) * turns
    return out


HALVES = _half_counts()


def half_no(sec, i, j, h):
    return i * (2 * len(RING[sec][0])) + (HALVES[sec] + 2 * j + h)


def used(sec, i, j, h=1):
    return half_no(sec, i, j, h) + 3


CREDITED = [f"ring_free{s}" for s in range(R)] + ["tk_step", "sk_evac", "sk_dots", "sp_kt", "sp_qk"] + \
    ["at_pair", "at_s", "at_ot", "at_q", "at_qall"] + \
    ["w_used", "up_c3", "up_acv", "up_afree", "up_bfree"] * 2 + [f"dn{l}_free" for l in range(DEPTH)] * 4

STORES = [6, 9, 15, 18, 19]


def build(nc, I, O):
    with ExitStack() as ctx:
        def sb(name, shape, dt=F32):
            return ctx.enter_context(nc.sbuf_tensor(name, shape, dt))[tuple(slice(0, n) for n in shape)]

        sems = {}

        def S(name):
            if name not in sems:
                sems[name] = ctx.enter_context(nc.semaphore(name))
            return sems[name]

        ps = ctx.enter_context(nc.psum_tensor("ps", [P, 8, 512], F32))

        def pair(p, rows=P, lo=0):
            return ps[lo:lo + rows, 2 * p:2 * p + 2, 0:HT]

        const = sb("const", [P, K_N])
        ident = const[:, K_ID:K_ID + P]
        swap = const[:, K_ROT:K_ROT + P]
        diag16 = const[:, K_D16:K_D16 + NS]
        diag8 = const[0:64, K_D8:K_D8 + NS]
        ones = sb("ones", [P, P])
        zeros = sb("zeros", [P, P])
        epsc = sb("epsc", [P, 1])
        colmask8 = sb("colmask8", [64, NS, 64])
        table = sb("table", [NPG, NS], I32)
        tablef = sb("tablef", [NPG, NS])
        idx = sb("idx", [P, NS], I32)
        ring = sb("ring", [P, R, KC * PC])
        xT = sb("xT", [P, KC, TOK])
        hH = sb("hH", [P, KC, TOK], F32R)
        hL = sb("hL", [P, KC, TOK], F32R)
        wH = sb("wH", [P, 2, HK, PC], F32R)
        wL = sb("wL", [P, 2, HK, PC], F32R)
        c2 = sb("c2", [P, KC, CP], F32R)
        cT = sb("cT", [P, KC, CC])
        vT = sb("vT", [P, 40])
        badaT = sb("badaT", [P, DEPTH * NADA])
        cwT = sb("cwT", [P, FC, 40])
        cs0 = sb("cs0", [P, DEPTH, FC, NS])
        ada = sb("ada", [P, DEPTH * NADA, CC])
        modA = sb("modA", [P, KC, CC])
        sq = sb("sq", [P, 2, TOK])
        rt = sb("rt", [P, TOK])
        bfb = sb("bfb", [P, NH])
        small = sb("small", [P, 64])
        tmp8 = sb("tmp8", [P, NS])
        scrap = sb("scrap", [1, 2])
        scrap2 = sb("scrap2", [1, 1])

        A_N = 19900
        arena = sb("arena", [P, A_N])
        at = [0]

        def part(n, reset=None):
            if reset is not None:
                at[0] = reset
            a = arena[:, at[0]:at[0] + n]
            at[0] += n
            assert at[0] <= A_N, at[0]
            return a

        hT = arena[:, A_N - KC * TOK:A_N].rearrange("p (k t) -> p k t", k=KC)
        xload = part(QT * D, 0).rearrange("p (t d) -> p t d", t=QT)
        xsload = part(D)
        cload = part(D)
        vrow = part(P)
        vrow2 = part(P)
        crow = part(FF)
        qst = part(GR * TOK, 0).rearrange("p (h t) -> p h t", h=GR)
        kaug = part(NKV * TOK).rearrange("p (g t) -> p g t", g=NKV)
        Vt = part(QT * PC).rearrange("p (t c) -> p t c", t=QT)
        OT = part(KC * TOK).rearrange("p (k t) -> p k t", k=KC)
        maskP = part(QT * SEQ).rearrange("p (t c) -> p t c", t=QT)
        knT = part(2 * NS).rearrange("p (a b) -> p a b", a=2)
        vnew = part(PC)
        knew = part(PC)
        Qall = part(2 * P).rearrange("p (a c) -> p a c", a=2)
        qz = part(4 * P).rearrange("p (r a c) -> p r a c", r=2, a=2)
        cq = part(QT * NH).rearrange("p (t h) -> p t h", t=QT)
        lf = part(5 * NH).rearrange("p (t h) -> p t h", t=5)
        scs = part(PAST + 1)
        biasS, maskS = scs[:, 0:PAST], scs[:, PAST:PAST + 1]
        work0 = at[0]
        raw = part(3 * TOK, work0).rearrange("p (b t) -> p b t", b=3)
        fm = part(3 * TOK).rearrange("p (b t) -> p b t", b=3)
        ktok = part(QT * PC).rearrange("p (t c) -> p t c", t=QT)
        ikw = part(QT * 72).rearrange("p (t c) -> p t c", t=QT)
        ikws = part(72)
        iqT = OT
        ikT = part(TOK)
        sc = raw.rearrange("p b t -> p (b t)")
        sc = sc[:, 0:3 * SEQ].rearrange("p (t c) -> p t c", t=3)
        relu = fm.rearrange("p b t -> p (b t)")[:, 0:3 * SEQ].rearrange("p (b c) -> p b c", b=3)
        ikb = ktok.rearrange("p t c -> p (t c)")
        iqall = part(P)
        iqz = part(2 * P).rearrange("p (r c) -> p r c", r=2)
        iwx = part(64)
        iwbd = part(NS)
        Rsb = fm.rearrange("p b t -> p (b t)")[0:64, 0:PAST + 1]
        raw2 = part(2 * TOK, work0).rearrange("p (b t) -> p b t", b=2)
        Sm = part(2 * SEQ).rearrange("p (b c) -> p b c", b=2)
        Pr = part(2 * SEQ).rearrange("p (b c) -> p b c", b=2)
        PT = part(2 * SEQ).rearrange("p (b c) -> p b c", b=2)
        On = part(2 * PC).rearrange("p (b c) -> p b c", b=2)
        mx = part(16)
        nm = part(16)
        lsum = part(16)
        rl = part(16)
        KT = part(4 * 512, work0).rearrange("p (r c) -> p r c", r=4)
        Pb = part(PAST)
        PTs = part(NPG * P).rearrange("p (j c) -> p j c", j=NPG)
        pnT = part(P)
        pnx = part(NS)
        ovs = part(PC)
        Pz = KT.rearrange("p r c -> p (r c)").rearrange("p (r n c) -> p r n c", r=2, n=NPG)
        ssm = part(16)
        colmask = part(NS * P).rearrange("p (b c) -> p b c", b=NS)
        lfT = part(PAST + 1, work0)
        cs = part(PAST + 1)
        lgx = part(P)
        zf = part(5 * NH)
        zg = part(5 * NH)
        gT = part(FC * TOK, 0).rearrange("p (k t) -> p k t", k=FC)
        aS = part(2 * (TOK + 2)).rearrange("p (b t) -> p b t", b=2)
        cvA = part(2 * TOK).rearrange("p (b t) -> p b t", b=2)
        acv = part(FC * 10).rearrange("p (k t) -> p k t", k=FC)
        cvrow = part(FF)
        ytok = part(2 * D, 0).rearrange("p (b d) -> p b d", b=2)
        ysam = part(D)

        def v520(a):
            return a.rearrange("p (a t) -> p a t", a=2)

        block = ctx.enter_context(nc.Block())

        def panel_ready(pe, sec, i, j):
            s, _, full = fill(sec, i, j)
            pe.wait_ge(S(full_name(sec, s)), full)
            return s

        def panel_used(ins, s):
            ins.then_inc(S(f"ring_free{s}"), 1)

        def slot_free(sp, sec, i, j):
            s, before, _ = fill(sec, i, j)
            sp.wait_ge(S(f"ring_free{s}"), before)
            return s

        def panel_view(s, cols=PC):
            return ring[:, s, :].rearrange("p (k c) -> p k c", c=PC)[:, :, 0:cols]

        def by_token(a):
            return a[:, 0:PAST].rearrange("p (k n) -> p n k", n=NPG)

        def pages_view(s, cols):
            return ring[:, s, 0:NPG * cols].rearrange("p (j c) -> p j c", c=cols)

        class Chain:
            n = 0

            def __init__(self, eng):
                self.eng = eng

            def link(self, ins):
                Chain.n += 1
                ins.then_inc(S("dve_step"), 1)
                self.eng.wait_ge(S("dve_step"), Chain.n)

        pool_n = [0]

        def in_turn(pool, ins):
            pool_n[0] += 1
            ins.then_inc(S("pool_step"), 1)
            pool.wait_ge(S("pool_step"), pool_n[0])

        ENG = ("pe", "act", "dve", "pool")
        phase_n = {e: 0 for e in ENG}

        def phase_end(eng, me):
            phase_n[me] += 1
            eng.drain().then_inc(S(f"phase_{me}"), 1)
            for e in ENG:
                if e != me:
                    eng.wait_ge(S(f"phase_{e}"), phase_n[me])

        def settle(dve, n=0):
            dve.memset(scrap[0:1, n:n + 1], 0.0)

        def load_panel(sp, sec, i, j, w, k0, nk, c0, cols=PC):
            s = slot_free(sp, sec, i, j)
            src = w.rearrange("(k p) c -> p k c", p=P)[:, k0:k0 + nk, ds(c0, cols)]
            sp.dma_start(panel_view(s, cols)[:, 0:nk, :], src).then_inc(S(f"ring_full{s}"), 16)

        def gather(pool, sec, i, j, cache, b, cols):
            s = slot_free(pool, sec, i, j)
            gather_rows(pool, ring[:, s, 0:NPG * cols], cache, b).then_inc(S(full_name(sec, s)), 16)

        def gather_rows(pool, out, cache, b):
            rows = cache.rearrange("g (u n) c -> (g u) (n c)", n=NPG)
            return pool.indirect_dma_start(out=out, out_offset=None, in_=rows,
                                           in_offset=bass.IndirectOffsetOnAxis(ap=idx[:, b:b + 1], axis=0))

        def gather_logf(pool, b):
            s = fill("logf", 0, 0)[0]
            gather_rows(pool, ring[:, s, b * P:b * P + P], I["cache_logf_b"], b).then_inc(S(full_name("logf", s)), 16)

        @block.sync
        def _(sp):
            sp.dma_start(cload[0:1, :], I["c_prompt"]).then_inc(S("in_vec"), 16)
            sp.dma_start(cload[1:CC, :], I["c_sample"]).then_inc(S("in_vec"), 16)
            sp.dma_start(vrow[0:DEPTH * NADA, :], I["b_ada"].rearrange("l (m p) -> (l m) p", p=P)).then_inc(S("in_vec"), 16)
            for n, g in enumerate(("g_mix", "g_ffn")):
                sp.dma_start(vrow2[16 * n:16 * n + 16, :], I[g].rearrange("l (m p) -> (l m) p", p=P)).then_inc(S("in_vec"), 16)
            sp.dma_start(vrow2[32:40, :], I["g_final"].rearrange("(m p) -> m p", p=P)).then_inc(S("in_vec"), 16)
            sp.dma_start(const[:, :], I["const"]).then_inc(S("in_const"), 16)
            with sp.Fori(0, 2) as i:
                for j in range(4):
                    load_panel(sp, "ada0a", i, j, I["w_ada"][0], 0, KC, (i * 4 + j) * PC)
            wa = I["w_in_a"][0]
            IQ0, IK0 = QKV, QKV + NIH * HD
            for j, (c0, cols) in enumerate(((NH * HD, PC), (NH * HD + PC, PC), (IK0, 72), (IQ0, PC), (IQ0 + PC, PC))):
                load_panel(sp, "head0", 0, j, wa, 0, KC, c0, cols)
            with sp.Fori(0, 4) as i:
                for j in range(4):
                    load_panel(sp, "ada0b", i, j, I["w_ada"][0], 0, KC, (i * 4 + j) * PC + 2 * D)
            for l in range(DEPTH):
                w_in = wa if l == 0 else I["w_in_b"][0]
                if l == 1:
                    with sp.Fori(0, 6) as i:
                        for j in range(4):
                            load_panel(sp, "ada1", i, j, I["w_ada"][1], 0, KC, (i * 4 + j) * PC)
                    for j, (c0, cols) in enumerate(((NH * HD, PC), (NH * HD + PC, PC), (QKV, NH))):
                        load_panel(sp, "head1", 0, j, w_in, 0, KC, c0, cols)
                with sp.Fori(0, NKV) as i:
                    load_panel(sp, f"q{l}", i, 0, w_in, 0, KC, i * PC)
                for j in range(4):
                    load_panel(sp, f"o{l}", 0, j, I[f"w_o_{'ab'[l]}"][0], 0, KC, j * PC)
                for j in range(2):
                    load_panel(sp, f"up{l}h", 0, j, I["w_up"][l], 0, KC, j * FF)
                with sp.Fori(0, 5) as i:
                    for j in range(4):
                        load_panel(sp, f"up{l}", i, j, I["w_up"][l], 0, KC, (i * 2 + (1 + j // 2)) * PC + (j % 2) * FF)
                with sp.Fori(0, 2) as i:
                    for j in range(6):
                        load_panel(sp, f"dn{l}", i, j, I["w_down"][l], *GROUPS[j // 2], (i * 2 + j % 2) * PC)

        def split_high(act, sec, i, j, h, nk=HK, cols=PC):
            s, _, full = fill(sec, i, j)
            if h == 0:
                act.wait_ge(S(full_name(sec, s)), full)
            act.wait_ge(S("w_used"), half_no(sec, i, j, h) + 1)
            act.activation(wH[:, h, 0:nk, 0:cols], panel_view(s)[:, HK * h:HK * h + nk, 0:cols], ACT.Copy).then_inc(S("w_hi"), 1)

        def split_low(eng, sec, i, j, h, nk=HK, cols=PC, sem="w_lo"):
            s, _, _ = fill(sec, i, j)
            eng.wait_ge(S("w_hi"), half_no(sec, i, j, h) + 1)
            eng.tensor_tensor(wL[:, h, 0:nk, 0:cols], panel_view(s)[:, HK * h:HK * h + nk, 0:cols],
                              wH[:, h, 0:nk, 0:cols].bitcast(F32), ALU.subtract).then_inc(S(sem), 1)

        def half_ready(pe, sec, i, j, h):
            s, _, _ = fill(sec, i, j)
            if sec == "ada0b" and h == 1:
                pe.wait_ge(S("w_lo_odd"), i * 4 + (j + 1))
                pe.sem_inc(S("w_lo"), 1)
            else:
                pe.wait_ge(S("w_lo"), half_no(sec, i, j, h) + 1)
            if h == 1:
                pe.sem_inc(S(f"ring_free{s}"), 1)

        def mm_half(pe, h, pairs, k0, nk, first, last, wait=None):
            for t, p in enumerate(pairs):
                for kc in range(nk):
                    if wait is not None and t == 0:
                        wait(k0 + kc)
                    for n, (w, mov) in enumerate(((wH, hH), (wH, hL), (wL, hH))):
                        for half in range(2):
                            ins = pe.matmul(ps[:, 2 * p + half, 0:HT], w[:, h, kc, t * P:t * P + P],
                                            mov[:, k0 + kc, half * HT:half * HT + HT],
                                            start=(first and kc == 0 and n == 0), stop=(last and kc == nk - 1 and n == 2))
            ins.then_inc(S("w_used"), 1)

        def mm_panel(pe, sec, i, j, pairs, wait=None):
            for h in range(2):
                half_ready(pe, sec, i, j, h)
                mm_half(pe, h, pairs, HK * h, HK, h == 0, h == 1, wait)

        def ada_turn(pe, j, t0):
            pe.wait_ge(S("ad_row"), t0 + 1)
            for m in range(2):
                ins = pe.matmul(ps[:, 4 + j, CC * m:CC * m + CC], sq[0:CP, j % 2, m * P:m * P + P], const[0:CP, K_SUM:K_SUM + CC],
                                start=True, stop=True)
            ins.then_inc(S("ad_turn"), 1)

        def pe_ada(pe, sec, turns, n0):
            with pe.Fori(0, turns) as i:
                for j in range(5):
                    if j < 4:
                        for h in range(2):
                            half_ready(pe, sec, i, j, h)
                            for kc in range(HK):
                                pe.matmul(ps[0:CP, j, 0:PC], c2[:, HK * h + kc, :], wH[:, h, kc, :], start=(h + kc == 0), stop=False)
                                ins = pe.matmul(ps[0:CP, j, 0:PC], c2[:, HK * h + kc, :], wL[:, h, kc, :], start=False,
                                                stop=(h == 1 and kc == HK - 1))
                            ins.then_inc(S("w_used"), 1)
                    if j >= 1:
                        ada_turn(pe, j - 1, i * 4 + (n0 + j - 1))

        def act_ada(act, sec, turns, m0, n0):
            def result(j, i):
                act.wait_ge(S("ad_turn"), i * 4 + (n0 + j + 1))
                for m in range(2):
                    mt = (i * 4 + j) * 2 + (m0 + m)
                    act.activation(ada[:, ds(mt, 1), :].rearrange("p o c -> p (o c)"), ps[:, 4 + j, CC * m:CC * m + CC],
                                   ACT.Identity, bias=badaT[:, ds(mt, 1)])

            def ahead(i, j, h):
                split_high(act, sec, i + (j + 1) // 4, (j + 1) % 4, h)

            if sec == "ada0b":
                for h in range(2):
                    split_high(act, sec, 0, 0, h)
            with act.Fori(0, turns) as i:
                for j in range(4):
                    ahead(i, j, 0)
                    ahead(i, j, 1)
                    act.wait_ge(S("w_used"), used(sec, i, j))
                    if j >= 2:
                        act.wait_ge(S("ad_turn"), i * 4 + (n0 + j - 1))
                    act.activation(sq[0:CP, j % 2, 0:PC], ps[0:CP, j, 0:PC], ACT.Copy).then_inc(S("ad_row"), 1)
                    if j >= 1:
                        result(j - 1, i)
                result(3, i)

        def low_ada(dve, sec, turns):
            with dve.Fori(0, turns) as i:
                for j in range(4):
                    for h in range(2):
                        split_low(dve, sec, i + (j + 1) // 4, (j + 1) % 4, h)

        def low_even(pool, sec, turns):
            with pool.Fori(0, turns) as i:
                for j in range(4):
                    split_low(pool, sec, i, j, 0)
            for h in range(2):
                split_low(pool, sec, turns, 0, h)

        def low_odd(dve, sec, p):
            split_low(dve, sec, p // 4, p % 4, 1, sem="w_lo_odd")

        NEXT = {0: "ada0a", 1: "up0h", 2: "ada1", 3: "up1h"}

        def x_done(eng, n, kc):
            if n % 2 == 1:
                eng.wait_ge(S(f"o{n // 2}_res"), kc + 1)
            elif n:
                eng.wait_ge(S(f"dn{n // 2 - 1}_free"), 4 + kc + 1)

        def pe_rms(pe, n, tiles=range(KC)):
            x_done(pe, n, 4)
            for kc in tiles:
                pe.wait_ge(S("rms_sq"), n * KC + kc + 1)
                for half in range(2):
                    ins = pe.matmul(ps[:, half, 0:HT], ones[:, :], sq[:, kc % 2, half * HT:half * HT + HT],
                                    start=(kc == 0), stop=(kc == KC - 1))
                ins.then_inc(S("rms_sum"), 1)

        def act_rms(act, n):
            for kc in range(KC):
                if n in NEXT and kc in (2, 6):
                    split_high(act, NEXT[n], 0, 0, kc // 4)
                if kc >= 2:
                    act.wait_ge(S("rms_sum"), n * KC + kc - 1)
                x_done(act, n, kc)
                act.activation(sq[:, kc % 2, :], xT[:, kc, :], ACT.Square).then_inc(S("rms_sq"), 1)
            act.activation(scrap2[0:1, :], epsc[0:1, :], ACT.Sqrt)
            act.wait_ge(S("rms_sum"), n * KC + KC)
            act.activation(v520(rt[:, :]), pair(0), ACT.Sqrt, bias=epsc[:, 0:1], scale=1.0 / D).then_inc(S("rms_rt"), 1)

        def dve_rms(dve, n):
            if n in NEXT:
                for h in range(2):
                    split_low(dve, NEXT[n], 0, 0, h)
            dve.wait_ge(S("rms_rt"), n + 1)
            dve.reciprocal(rt[:, :], rt[:, :]).then_inc(S("rms_ri"), 1)
            dve.wait_ge(S("rms_ri"), n + 1)

        def normed(eng, kc):
            eng.tensor_tensor(hT[:, kc, :], xT[:, kc, :], rt[:, :], ALU.mult).then_inc(S("rms_t"), 1)

        def pool_normed(pool, n):
            pool.wait_ge(S("rms_ri"), n + 1)
            for kc in range(KC):
                normed(pool, kc)

        def act_mod(act, n, shift):
            for kc in range(KC + 1):
                if kc < KC:
                    act.wait_ge(S("rms_t"), n * KC + kc + 1)
                    if kc == 0:
                        act.wait_ge(S("rms_mod"), n + 1)
                    act.activation(hT[:, kc, 0:SEQ], hT[:, kc, 0:SEQ], ACT.Identity, bias=shift[:, kc, 0:1], scale=modA[:, kc, 0:1])\
                        .then_inc(S("rms_v"), 1)
                if kc >= 1:
                    act.wait_ge(S("rms_v"), n * KC + kc)
                    act.wait_ge(S("rms_s"), n * KC + kc)
                    act.activation(hH[:, kc - 1, :], hT[:, kc - 1, :], ACT.Copy).then_inc(S("rms_hi"), 1)

        def pool_mod(pool, n, shift):
            pool.wait_ge(S("rms_mod"), n + 1)
            for kc in range(KC):
                hs = hT[:, kc, SEQ:TOK]
                pool.wait_ge(S("rms_t"), n * KC + kc + 1)
                in_turn(pool, pool.tensor_tensor(hs, hs, modA[:, kc, 1:CC], ALU.mult))
                pool.tensor_tensor(hs, hs, shift[:, kc, 1:CC], ALU.add).then_inc(S("rms_s"), 1)

        def dve_gain(dve, scale, gain):
            dve.scalar_tensor_tensor(out=modA[:, :, :], in0=scale, scalar=1.0, in1=gain.unsqueeze(2).to_broadcast([P, KC, CC]),
                                     op0=ALU.add, op1=ALU.mult).then_inc(S("rms_mod"), 1)

        def dve_mod(dve, n):
            for kc in range(KC + 2):
                if n % 2 == 1 and kc < KC:
                    normed(dve, kc)
                if kc >= 2:
                    dve.wait_ge(S("rms_hi"), n * KC + kc - 1)
                    dve.tensor_tensor(hL[:, kc - 2, :], hT[:, kc - 2, :], hH[:, kc - 2, :].bitcast(F32), ALU.subtract)\
                        .then_inc(S("rms_lo"), 1)

        def split_input(pe, n):
            return lambda kc: pe.wait_ge(S("rms_lo"), n * KC + kc + 1)

        TILES = [[(0, 0, P, "k"), (0, P, P, "k"), (1, 0, P, "v"), (1, P, P, "v"), (2, 0, 72, "ikw"),
                  (3, 0, P, "iq"), (3, P, P, "iq"), (4, 0, P, "iq"), (4, P, P, "iq")],
                 [(0, 0, P, "k"), (0, P, P, "k"), (1, 0, P, "v"), (1, P, P, "v"), (2, 0, NH, "fg")]]

        def tiles_in(l, pn):
            return sum(1 for tile in TILES[l] if tile[0] == pn)

        def last_in(l, t):
            return t + 1 == len(TILES[l]) or TILES[l][t + 1][1] == 0

        def head_cols(l, pn):
            return {2: 72 if l == 0 else NH}.get(pn, PC)

        def rotates(l, t):
            return l == 0 and TILES[l][t][3] != "v"

        def turned(l, t):
            return TILES[l][t][3] != "iq"

        def copied(l, t):
            return TILES[l][t][3] in ("k", "ikw", "iq")

        def upto(test, l, t):
            return sum(1 for u in range(t + 1) if test(l, u))

        def src_of(l, t):
            return (fm if rotates(l, t) else raw)[:, t % 3, :]

        def pe_head(pe, l):
            tag, sec = f"hd{l}", f"head{l}"
            T = TILES[l]
            for t in range(len(T) + 2):
                if t < len(T) and T[t][1] == 0:
                    if t:
                        pe.wait_ge(S(f"{tag}_raw"), t)
                    mm_panel(pe, sec, 0, T[t][0], [u % 2 for u in range(t, t + tiles_in(l, T[t][0]))],
                             split_input(pe, 2 * l) if t == 0 else None)
                u = t - 1
                if 0 <= u < len(T) and rotates(l, u):
                    pe.wait_ge(S(f"{tag}_raw"), u + 1)
                    if upto(rotates, l, u) >= 2:
                        pe.wait_ge(S(f"{tag}_fm"), upto(rotates, l, u) - 1)
                    rows = min(T[u][2], P) if T[u][3] != "ikw" else HD
                    for half in range(2):
                        ins = pe.matmul(ps[0:rows, 4 + half, 0:HT], swap[0:rows, 0:rows],
                                        raw[0:rows, u % 3, half * HT:half * HT + HT], start=True, stop=True)
                    ins.then_inc(S(f"{tag}_rot"), 1)
                u = t - 2
                if 0 <= u < len(T) and turned(l, u):
                    rows = T[u][2]
                    if rotates(l, u):
                        pe.wait_ge(S(f"{tag}_fm"), upto(rotates, l, u))
                    if upto(turned, l, u) >= 2:
                        pe.wait_ge(S(f"{tag}_tok"), upto(turned, l, u) - 1)
                    src = src_of(l, u)
                    for q in range(QT):
                        pe.transpose(ps[:, 6, q * P:q * P + rows], src[0:rows, q * P:q * P + P], ident[0:rows, 0:rows])
                    pe.transpose(ps[0:NS, 7, 0:rows], src[0:rows, SEQ:TOK], ident[0:rows, 0:rows]).then_inc(S(f"{tag}_tr"), 1)

        def act_head(act, l):
            tag = f"hd{l}"
            T = TILES[l]

            def tok_major(t):
                rows, kind = T[t][2], T[t][3]
                act.wait_ge(S(f"{tag}_tr"), upto(turned, l, t))
                src = ps[:, 6, :].rearrange("p (q c) -> p q c", q=QT)[:, :, 0:rows]
                big, new, c0 = {"k": (ktok, knew, P * (t % 2)), "v": (Vt, vnew, P * (t % 2)),
                                "ikw": (ikw, ikws, 0), "fg": (lf, None, 0)}[kind]
                act.activation(big[:, 0:QT, c0:c0 + rows], src, ACT.Copy)
                dst = lf[0:NS, QT, :] if kind == "fg" else new[0:NS, c0:c0 + rows]
                act.activation(dst, ps[0:NS, 7, 0:rows], ACT.Copy).then_inc(S(f"{tag}_tok"), 1)

            sec = f"head{l}"
            for t in range(len(T) + 2):
                if t < len(T):
                    pn, m0, rows, _ = T[t]
                    ahead = pn + 1 <= T[-1][0]
                    if m0 == 0 and ahead:
                        split_high(act, sec, 0, pn + 1, 0, HK, head_cols(l, pn + 1))
                    act.wait_ge(S("w_used"), used(sec, 0, pn))
                    if t >= 3:
                        u = t - 3
                        if upto(rotates, l, u):
                            act.wait_ge(S(f"{tag}_fm"), upto(rotates, l, u))
                            act.wait_ge(S(f"{tag}_rot"), upto(rotates, l, u))
                        if upto(turned, l, u):
                            act.wait_ge(S(f"{tag}_tr"), upto(turned, l, u))
                        if upto(copied, l, u):
                            act.wait_ge(S(f"{tag}_cp"), upto(copied, l, u))
                    act.activation(v520(raw[0:rows, t % 3, :]), pair(t % 2, rows), ACT.Copy).then_inc(S(f"{tag}_raw"), 1)
                    if last_in(l, t) and ahead:
                        split_high(act, sec, 0, pn + 1, 1, HK, head_cols(l, pn + 1))
                if t >= 2 and turned(l, t - 2):
                    tok_major(t - 2)
            act.wait_ge(S(f"{tag}_tok"), upto(turned, l, len(T) - 1))
            x = "ab"[l]
            for src, new, name in ((ktok, knew, "k"), (Vt, vnew, "v")):
                act.dma_start(O[f"{name}_{x}_p"].rearrange("(t p) c -> p t c", p=P), src).then_inc(S("stores"), 16)
                act.dma_start(O[f"{name}_{x}_s"], new[0:NS, :]).then_inc(S("stores"), 16)
            if l == 0:
                act.dma_start(O["kidx_p"].rearrange("(t p) c -> p t c", p=P), ikw[:, :, 0:HD]).then_inc(S("stores"), 16)
                act.dma_start(O["kidx_s"], ikws[0:NS, 0:HD]).then_inc(S("stores"), 16)

        def dve_head(dve, l):
            tag = f"hd{l}"
            T = TILES[l]
            ch = Chain(dve)
            for t in range(len(T)):
                pn = T[t][0]
                if T[t][1] == 0 and pn + 1 <= T[-1][0]:
                    for h in range(2):
                        split_low(dve, f"head{l}", 0, pn + 1, h, HK, head_cols(l, pn + 1))
                if not rotates(l, t):
                    continue
                rows = HD if T[t][3] == "ikw" else P
                dve.wait_ge(S(f"{tag}_raw"), t + 1)
                if upto(rotates, l, t) >= 2:
                    dve.wait_ge(S(f"{tag}_fm"), upto(rotates, l, t) - 1)
                dve.tensor_tensor(sq[0:rows, 0, :], raw[0:rows, t % 3, :], const[0:rows, K_COS:K_COS + TOK], ALU.mult)
                dve.wait_ge(S(f"{tag}_rot"), upto(rotates, l, t))
                ch.link(dve.tensor_tensor(v520(sq[0:rows, 1, :]), pair(2, rows), v520(const[0:rows, K_SIN:K_SIN + TOK]), ALU.mult))
                if t >= 3:
                    if upto(turned, l, t - 3):
                        dve.wait_ge(S(f"{tag}_tr"), upto(turned, l, t - 3))
                    dve.wait_ge(S(f"{tag}_cp"), upto(copied, l, t - 3))
                if T[t][3] == "ikw":
                    dve.tensor_copy(fm[HD:72, t % 3, :], raw[HD:72, t % 3, :])
                dve.tensor_tensor(fm[0:rows, t % 3, :], sq[0:rows, 0, :], sq[0:rows, 1, :], ALU.add).then_inc(S(f"{tag}_fm"), 1)

        def pool_head(pool, l):
            tag = f"hd{l}"
            T = TILES[l]
            for t in range(len(T)):
                if not copied(l, t):
                    continue
                if rotates(l, t):
                    pool.wait_ge(S(f"{tag}_fm"), upto(rotates, l, t))
                else:
                    pool.wait_ge(S(f"{tag}_raw"), t + 1)
                src, kind = src_of(l, t), T[t][3]
                if kind == "k":
                    in_turn(pool, pool.tensor_copy(kaug[0:HD, 2 * t, :], src[0:HD, :]))
                    in_turn(pool, pool.tensor_copy(kaug[0:HD, 2 * t + 1, :], src[HD:P, :]))
                    ins = pool.tensor_copy(knT[:, t, :], src[:, SEQ:TOK])
                elif kind == "ikw":
                    ins = pool.tensor_copy(ikT[0:HD, :], src[0:HD, :])
                else:
                    h = 2 * (t - 5)
                    in_turn(pool, pool.tensor_copy(iqT[0:HD, h, :], src[0:HD, :]))
                    ins = pool.tensor_copy(iqT[0:HD, h + 1, :], src[HD:P, :])
                ins.then_inc(S(f"{tag}_cp"), 1)
                pool.wait_ge(S(f"{tag}_cp"), upto(copied, l, t))

        def pe_score(pe):
            def turn(b):
                s = panel_ready(pe, "kidx", b // 2, b % 2)
                pe.wait_ge(S("sk_evac"), 1 + b * 2)
                for n in range(NPG // 2):
                    ins = pe.transpose(ps[:, 4, n * P:n * P + P], ring[:, s, 2 * n * HD:2 * n * HD + P], ident)
                panel_used(ins, s)

            def dots(b):
                pe.wait_ge(S("sk_qz"), b + 1)
                pe.wait_ge(S("sk_evac"), 1 + b * 2 + 2)
                for c in range(2):
                    ins = pe.matmul(ps[:, 6 + c, :], iqz[0:HD, b % 2, :], ikb[0:HD, c * 512:c * 512 + 512], start=False, stop=False)
                ins.then_inc(S("sk_dots"), 1)

            for c in range(2):
                pe.matmul(ps[:, 6 + c, :], zeros[0:HD, :], const[0:HD, 0:512], start=True, stop=False)
            for u in range(3 * NIH):
                qt, h = u // NIH + 1, u % NIH
                if u >= 4:
                    pe.wait_ge(S("sc_relu"), u - 3)
                pe.matmul(ps[:, u % 4, 0:(qt + 1) * P], iqT[0:HD, h, qt * P:qt * P + P], ikT[0:HD, 0:(qt + 1) * P],
                          start=True, stop=True).then_inc(S("sc_dot"), 1)
                if u % 3 == 1:
                    turn(u // 3)
                if u % 3 == 2 and u >= 3:
                    dots(u // 3 - 1)
            dots(NS - 1)
            for c in range(2):
                pe.matmul(ps[:, 6 + c, :], zeros[0:HD, :], const[0:HD, 0:512], start=False, stop=True)
            pe.wait_ge(S("sc_relu"), 3 * NIH)
            pe.matmul(ps[0:64, 3, 0:NS], iqall[0:HD, 0:64], ikT[0:HD, SEQ:TOK], start=True, stop=True).then_inc(S("sk_all"), 1)
            pe.wait_ge(S("sk_iwx"), 1)
            pe.transpose(ps[0:64, 2, 0:NS], iwx[0:NS, :], ident[0:NS, 0:NS]).then_inc(S("sk_iwt"), 1)
            pe.wait_ge(S("sk_rs"), 3)
            pe.wait_ge(S("sk_iwbd"), 1)
            for c in range(2):
                pe.matmul(ps[0:NS, c, :], iwbd[0:64, :], Rsb[:, c * 512:c * 512 + 512], start=True, stop=True)
            pe.matmul(ps[0:NS, 2, 16:17], iwbd[0:64, :], Rsb[:, PAST:PAST + 1], start=True, stop=True).then_inc(S("sk_score"), 1)

        def act_score(act):
            def keys(b):
                if b == 0:
                    act.wait_ge(S("stores"), 16 * STORES[0])
                s, before, _ = fill("kidx", b // 2, b % 2)
                act.wait_ge(S(f"ring_free{s}"), before + 1)
                act.wait_ge(S("sk_dots"), 1 + b)
                for c in range(2):
                    act.activation(ikb[0:HD, :].rearrange("p (n e t) -> p n e t", e=2, t=P)[:, :, c, :],
                                   ps[64 * c:64 * c + 64, 4, :].rearrange("p (n t) -> p n t", t=P), ACT.Copy).then_inc(S("sk_evac"), 1)

            for u in range(3 * NIH):
                w = (u // NIH + 2) * P
                act.wait_ge(S("sc_dot"), u + 1)
                if u >= 3:
                    act.wait_ge(S("sc_acc"), u - 2)
                act.activation(relu[:, u % 3, 0:w], ps[:, u % 4, 0:w], ACT.Relu).then_inc(S("sc_relu"), 1)
                if u % 3 == 2:
                    keys(u // 3)
            act.wait_ge(S("sk_all"), 1)
            act.wait_ge(S("sc_acc"), 3 * NIH)
            for c in range(2):
                act.activation(by_token(Rsb)[:, 4 * c:4 * c + 4, :], ps[0:64, 6 + c, :].rearrange("p (n k) -> p n k", n=4), ACT.Relu)\
                    .then_inc(S("sk_rs"), 1)
            act.wait_ge(S("sk_new"), 1)
            act.activation(Rsb[:, PAST:PAST + 1], small[0:64, 0:1], ACT.Relu).then_inc(S("sk_rs"), 1)

        def pool_score(pool):
            in_turn(pool, pool.memset(iqz[0:HD, :, 64:P], 0.0))
            pool.tensor_copy(iqall[0:HD, 0:64].rearrange("p (b h) -> p h b", h=NIH), iqT[0:HD, :, SEQ:TOK]).then_inc(S("pl_iq"), 1)
            pool.wait_ge(S("pl_iq"), 1)
            for i in range(4):
                for j in range(2):
                    gather(pool, "kidx", i, j, I["cache_kidx_a"], i * 2 + j, HD)
                for j in range(2):
                    pool.wait_ge(S("sk_dots"), 1 + (i * 2))
                    pool.tensor_tensor(iqz[0:HD, j, 0:64], iqall[0:HD, 0:64], colmask8[:, ds(i * 2 + j, 1), :].rearrange("p o c -> p (o c)"),
                                       ALU.mult).then_inc(S("sk_qz"), 1)

        def dve_score(dve):
            ch = Chain(dve)
            dve.tensor_tensor(iwx[0:NS, :].rearrange("p (b h) -> p b h", h=NIH), const[0:NS, K_E8:K_E8 + 64].rearrange("p (b h) -> p b h", h=NIH),
                              ikws[0:NS, HD:72].unsqueeze(1).to_broadcast([NS, NS, NIH]), ALU.mult).then_inc(S("sk_iwx"), 1)
            for u in range(3 * NIH):
                qt, h = u // NIH + 1, u % NIH
                w = (qt + 1) * P
                dve.wait_ge(S("sc_relu"), u + 1)
                iw = ikw[:, qt, HD + h:HD + h + 1]
                if h == 0:
                    ins = dve.tensor_scalar(sc[:, qt - 1, 0:w], relu[:, u % 3, 0:w], iw, None, ALU.mult)
                else:
                    ins = dve.scalar_tensor_tensor(out=sc[:, qt - 1, 0:w], in0=relu[:, u % 3, 0:w], scalar=iw,
                                                   in1=sc[:, qt - 1, 0:w], op0=ALU.mult, op1=ALU.add)
                ins.then_inc(S("sc_acc"), 1)
                dve.wait_ge(S("sc_acc"), u + 1)
                if h == NIH - 1:
                    ch.link(dve.tensor_tensor(sc[:, qt - 1, 0:w], sc[:, qt - 1, 0:w], const[:, K_CAU + SEQ - w:K_CAU + SEQ], ALU.add))
            dve.wait_ge(S("sk_iwt"), 1)
            dve.tensor_copy(iwbd[0:64, :], ps[0:64, 2, 0:NS]).then_inc(S("sk_iwbd"), 1)
            dve.wait_ge(S("sk_all"), 1)
            dve.tensor_tensor_reduce(small[0:64, 8:16], ps[0:64, 3, 0:NS], diag8, 1.0, 0.0, ALU.mult, ALU.add, small[0:64, 0:1])\
                .then_inc(S("sk_new"), 1)
            dve.wait_ge(S("sk_score"), 1)
            dve.tensor_copy(scs[0:NS, 0:PAST].rearrange("p (a c) -> p a c", a=2), ps[0:NS, 0:2, :])
            ch.link(dve.tensor_copy(scs[0:NS, PAST:PAST + 1], ps[0:NS, 2, 16:17]))

        def dve_topk(dve):
            ch = Chain(dve)
            dve.tensor_copy(maskP[:, 0, 0:P], const[:, K_CAU + SEQ - P:K_CAU + SEQ])
            for qt in range(1, QT):
                w = (qt + 1) * P
                scores, m8 = sc[:, qt - 1, 0:w], small[:, 0:8]
                for n in range(NSEL_P // 8):
                    ch.link(dve.max(m8, scores))
                    ch.link(dve.match_replace(scores, m8, scores, TAKEN))
                    step = (qt - 1) * (NSEL_P // 8) + n
                    if step % 3 == 1:
                        low_odd(dve, "ada0b", step // 3)
                dve.tensor_scalar(maskP[:, qt, 0:w], sc[:, qt - 1, 0:w], 0.5 * TAKEN, NEG, ALU.is_gt, ALU.mult)

        def act_logf(act):
            z, e = zf.rearrange("p (t h) -> p t h", t=5), zg.rearrange("p (t h) -> p t h", t=5)
            act.wait_ge(S("lf_z"), 1)
            act.activation(e, z, ACT.Abs).then_inc(S("lf_act"), 1)
            act.wait_ge(S("lf_act"), 1)
            act.activation(e, e, ACT.Exp, scale=-1.0).then_inc(S("lf_act"), 1)
            act.wait_ge(S("lf_act"), 2)
            act.activation(e, e, ACT.Ln, bias=ones[:, 0:1]).then_inc(S("lf_act"), 1)
            act.wait_ge(S("lf_done"), 1)
            act.dma_start(O["logf_p"].rearrange("(t p) c -> p t c", p=P), lf[:, 0:QT, :]).then_inc(S("stores"), 16)
            act.dma_start(O["logf_s"], lf[0:NS, QT, :]).then_inc(S("stores"), 16)
            act.wait_ge(S("lf_ck"), 1)
            act.activation(kaug[64:68, :, 0:SEQ], ps[64:68, 0:NKV, :], ACT.Copy, scale=-1.0 / SCALE)
            act.wait_ge(S("lf_turn"), 1)
            for c in range(2):
                ins = act.activation(by_token(lfT)[:, 4 * c:4 * c + 4, :], ps[:, 4 + c, :].rearrange("p (n k) -> p n k", n=4), ACT.Copy)
            ins.then_inc(S("lf_past"), 1)
            act.wait_ge(S("stores"), 16 * STORES[2])

        def dve_logf(dve):
            ch = Chain(dve)
            z, e = zf.rearrange("p (t h) -> p t h", t=5), zg.rearrange("p (t h) -> p t h", t=5)
            s = panel_ready(dve, "logf", 0, 0)
            panel_used(dve.tensor_copy(cs[:, 0:PAST].rearrange("p (n b h) -> p b n h", n=NPG, b=NS),
                                       ring[:, s, 0:PAST].rearrange("p (b n h) -> p b n h", b=NS, n=NPG)), s)
            dve.tensor_tensor(z, lf, bfb[:, :].unsqueeze(1).to_broadcast([P, 5, NH]), ALU.add).then_inc(S("lf_z"), 1)
            dve.wait_ge(S("lf_act"), 3)
            dve.scalar_tensor_tensor(out=lf, in0=z, scalar=0.0, in1=e, op0=ALU.min, op1=ALU.subtract).then_inc(S("lf_done"), 1)
            dve.wait_ge(S("lf_done"), 1)
            dve.tensor_tensor(lgx[0:NS, :].rearrange("p (b h) -> p b h", h=NH), const[0:NS, K_E16:K_E16 + P].rearrange("p (b h) -> p b h", h=NH),
                              lf[0:NS, QT, :].unsqueeze(1).to_broadcast([NS, NS, NH]), ALU.mult).then_inc(S("lf_x"), 1)
            dve.wait_ge(S("lf_cq"), 1)
            dve.tensor_copy(cq, ps[:, 6, 0:QT * NH].rearrange("p (t h) -> p t h", t=QT))
            dve.wait_ge(S("lf_xt"), 1)
            dve.tensor_reduce(lfT[:, PAST:PAST + 1], ps[:, 7, 0:NS], AX.X, ALU.add).then_inc(S("lf_past"), 1)
            dve.wait_ge(S("lf_past"), 2)
            ch.link(dve.tensor_tensor_scan(cs, lfT, lfT, 0.0, ALU.add, ALU.bypass))
            dve.tensor_scalar(biasS, cs[:, 0:PAST], cs[:, PAST:PAST + 1], -1.0 / SCALE, ALU.subtract, ALU.mult)

        def pe_logf(pe):
            tri = const[:, K_TRI:K_TRI + 896]
            slot, before, _ = fill("logf", 0, 0)
            pe.wait_ge(S(f"ring_free{slot}"), before + 1)
            for n in range(NPG):
                ins = pe.transpose(ps[:, 4 + n // 4, (n % 4) * P:(n % 4) * P + P], cs[:, n * P:n * P + P], ident)
            ins.then_inc(S("lf_turn"), 1)
            pe.wait_ge(S("lf_done"), 1)
            for qt in range(QT):
                for kb in range(qt + 1):
                    x = P * (qt - kb) + 384
                    ins = pe.matmul(ps[:, 6, qt * NH:qt * NH + NH], tri[:, x:x + P], lf[:, kb, :], start=(kb == 0), stop=(kb == qt))
            ins.then_inc(S("lf_cq"), 1)
            for g in range(NKV):
                for kb in range(QT):
                    ins = pe.matmul(ps[64:68, g, kb * P:SEQ], lf[:, kb, GR * g:GR * g + GR], tri[:, 384:384 + SEQ - kb * P],
                                    start=(kb == 0), stop=(kb == QT - 1))
            ins.then_inc(S("lf_ck"), 1)
            pe.wait_ge(S("lf_x"), 1)
            pe.transpose(ps[:, 7, 0:NS], lgx[0:NS, :], ident[0:NS, 0:NS]).then_inc(S("lf_xt"), 1)

        NU = QT * GR
        QPARTS = {3: (0, 1), 4: (2, 3), 5: (4, 5), 6: (6, 7), 9: (8,), 10: (9,), 11: (10, 11), 12: (12,), 13: (13,), 14: (14, 15)}
        QPAIR = 3

        def pe_qpart(pe, sec, i, n, part):
            t, h, kc = part // 8, part // HK % 2, part % HK
            if h + kc == 0:
                pe.wait_ge(S("at_pair"), n * 2 + (t + 1))
            if t == 0 and kc == 0:
                half_ready(pe, sec, i, 0, h)
            for m, (w, mov) in enumerate(((wH, hH), (wH, hL), (wL, hH))):
                for half in range(2):
                    ins = pe.matmul(ps[:, 2 * QPAIR + half, 0:HT], w[:, h, kc, t * P:t * P + P],
                                    mov[:, HK * h + kc, half * HT:half * HT + HT],
                                    start=(h + kc + m == 0), stop=(h == 1 and kc == HK - 1 and m == 2))
            if kc == HK - 1:
                if t == 1:
                    ins.then_inc(S("w_used"), 1)
                elif h == 1:
                    ins.then_inc(S("at_mm"), 1)

        def pe_qrot(pe, n, t):
            pe.wait_ge(S("at_raw"), n * 2 + (t + 1))
            for half in range(2):
                ins = pe.matmul(ps[:, 2 * QPAIR + half, 0:HT], swap, raw2[:, t, half * HT:half * HT + HT], start=True, stop=True)
            ins.then_inc(S("at_rot"), 1)

        def pe_units(pe, l, g, n, nxt):
            K = HD + GR
            pe.wait_ge(S("at_q"), n * 2 + 3)
            for u in range(NU + 5):
                if u < NU:
                    qt, hh = u // GR, u % GR
                    w = (qt + 1) * P
                    if u >= 2:
                        pe.wait_ge(S("at_sm"), n * NU + (u - 1))
                    pe.matmul(ps[:, u % 2, 0:w], qst[0:K, hh, qt * P:qt * P + P],
                              kaug[0:K, ds(g, 1), 0:w].rearrange("p o t -> p (o t)"), start=True, stop=True).then_inc(S("at_s"), 1)
                v = u - 2
                if 0 <= v < NU:
                    qt = v // GR
                    pe.wait_ge(S("at_p"), n * NU + (v + 1))
                    if v >= 2:
                        pe.wait_ge(S("at_pt"), n * NU + (v - 1))
                    for kb in range(qt + 1):
                        ins = pe.transpose(ps[:, 2 + v % 2, kb * P:kb * P + P], Pr[:, v % 2, kb * P:kb * P + P], ident)
                    ins.then_inc(S("at_tr"), 1)
                v = u - 3
                if 0 <= v < NU:
                    qt, hh = v // GR, v % GR
                    pe.wait_ge(S("at_pt"), n * NU + (v + 1))
                    if hh == 0 and qt >= 1:
                        pe.wait_ge(S("at_on"), n * QT + qt)
                    for kb in range(qt + 1):
                        ins = pe.matmul(ps[:, 4, hh * HD:hh * HD + HD], PT[:, v % 2, kb * P:kb * P + P],
                                        Vt[:, kb, ds(g * HD, HD)], start=(kb == 0), stop=(kb == qt))
                    ins.then_inc(S("at_o"), 1)
                v = u - 5
                if 0 <= v < NU and v % GR == GR - 1:
                    qt = v // GR
                    pe.wait_ge(S("at_on"), n * QT + (qt + 1))
                    pe.wait_ge(S("at_ot"), n * QT + (qt + 1))
                    for t in range(2):
                        ins = pe.transpose(ps[:, 5, t * P:t * P + P], On[:, qt % 2, t * P:t * P + P], ident)
                    ins.then_inc(S("at_otr"), 1)
                if nxt is not None:
                    for part in QPARTS.get(u, ()):
                        pe_qpart(pe, f"q{l}", nxt, n + 1, part)
                    if l == 0 and u in (8, 16):
                        pe_qrot(pe, n + 1, u // 16)

        def pe_attn(pe, l):
            n0 = l * NKV
            for t in range(2):
                for part in range(8):
                    pe_qpart(pe, f"q{l}", 0, n0, 8 * t + part)
                if l == 0:
                    pe_qrot(pe, n0, t)
            with pe.Fori(0, NKV - 1) as g:
                pe_units(pe, l, g, g + n0, g + 1)
            pe_units(pe, l, NKV - 1, n0 + NKV - 1, None)

        def act_raw(act, l, i, n, t):
            if t == 0:
                act.wait_ge(S("at_mm"), n + 1)
            else:
                act.wait_ge(S("w_used"), used(f"q{l}", i, 0))
            act.wait_ge(S("at_q"), n * 2 + 1)
            act.activation(v520(raw2[:, t, :]), pair(QPAIR), ACT.Copy).then_inc(S("at_raw"), 1)
            if l == 1:
                act.wait_ge(S("at_raw"), n * 2 + (t + 1))
                act.sem_inc(S("at_pair"), 1)

        def to_qst(eng, copy, n, t):
            eng.wait_ge(S("at_s"), n * NU + 1)
            eng.wait_ge(S("at_qall"), n + 1)
            copy(qst[0:HD, 2 * t, :], raw2[0:HD, t, :])
            copy(qst[0:HD, 2 * t + 1, :], raw2[HD:P, t, :]).then_inc(S("at_q"), 1)

        def act_attn(act, l):
            n0 = l * NKV

            def to_place(n):
                if l == 0:
                    act.wait_ge(S("at_rope"), n * 2 + 1)
                else:
                    act.wait_ge(S("at_raw"), n * 2 + 1)
                to_qst(act, lambda out, x: act.activation(out, x, ACT.Copy), n, 0)

            def units(n, nxt):
                for u in range(NU + 2):
                    if u < NU:
                        w = (u // GR + 1) * P
                        act.wait_ge(S("at_nm"), n * NU + (u + 1))
                        if u >= 2:
                            act.wait_ge(S("at_tr"), n * NU + (u - 1))
                        act.activation(Pr[:, u % 2, 0:w], Sm[:, u % 2, 0:w], ACT.Exp, bias=nm[:, u:u + 1],
                                       accum_out=lsum[:, u:u + 1]).then_inc(S("at_p"), 1)
                    v = u - 2
                    if 0 <= v:
                        w = (v // GR + 1) * P
                        act.wait_ge(S("at_tr"), n * NU + (v + 1))
                        if v >= 2:
                            act.wait_ge(S("at_o"), n * NU + (v - 1))
                        act.activation(PT[:, v % 2, 0:w], ps[:, 2 + v % 2, 0:w], ACT.Copy).then_inc(S("at_pt"), 1)
                    if nxt is not None:
                        if u < 2:
                            split_high(act, f"q{l}", nxt, 0, u)
                        if u in (7, 15):
                            act_raw(act, l, nxt, n + 1, u // 15)
                if nxt is not None:
                    to_place(n + 1)

            if l == 1:
                for h in range(2):
                    split_high(act, "q1", 0, 0, h)
            for t in range(2):
                act_raw(act, l, 0, n0, t)
            to_place(n0)
            with act.Fori(0, NKV - 1) as g:
                units(g + n0, g + 1)
            units(n0 + NKV - 1, None)

        def dve_attn(dve, l):
            n0 = l * NKV

            def rope(n, t):
                dve.wait_ge(S("at_raw"), n * 2 + (t + 1))
                dve.tensor_tensor(sq[:, 0, :], raw2[:, t, :], const[:, K_COS:K_COS + TOK], ALU.mult).then_inc(S("at_rp"), 1)
                dve.wait_ge(S("at_rot"), n * 2 + (t + 1))
                dve.tensor_tensor(v520(sq[:, 1, :]), pair(QPAIR), v520(const[:, K_SIN:K_SIN + TOK]), ALU.mult).then_inc(S("at_pair"), 1)
                dve.wait_ge(S("at_rp"), n * 2 + (t + 1))
                dve.wait_ge(S("at_pair"), n * 2 + (t + 2))
                dve.tensor_tensor(raw2[:, t, :], sq[:, 0, :], sq[:, 1, :], ALU.add).then_inc(S("at_rope"), 1)
                dve.wait_ge(S("at_rope"), n * 2 + (t + 1))

            def to_place(n):
                if l == 1:
                    dve.wait_ge(S("at_raw"), n * 2 + 2)
                to_qst(dve, dve.tensor_copy, n, 1)

            def outputs(n, qt):
                dve.wait_ge(S("at_o"), n * NU + (qt * GR + GR))
                dve.reciprocal(rl[:, qt * GR:qt * GR + GR], lsum[:, qt * GR:qt * GR + GR]).then_inc(S("at_rl"), 1)
                dve.wait_ge(S("at_rl"), n * QT + (qt + 1))
                dve.tensor_tensor(On[:, qt % 2, :].rearrange("p (h d) -> p h d", h=GR),
                                  ps[:, 4, 0:PC].rearrange("p (h d) -> p h d", h=GR),
                                  rl[:, qt * GR:qt * GR + GR].unsqueeze(2).to_broadcast([P, GR, HD]), ALU.mult)\
                    .then_inc(S("at_on"), 1)

            def turned_outputs(g, n, qt):
                dve.wait_ge(S("at_otr"), n * QT + (qt + 1))
                dve.tensor_copy(OT[:, ds(g * 2, 2), qt * P:qt * P + P], ps[:, 5, 0:PC].rearrange("p (t c) -> p t c", t=2))\
                    .then_inc(S("at_ot"), 1)

            def units(g, n, nxt):
                for u in range(NU + 4):
                    if u >= GR + 3 and (u - 4) % GR == GR - 1:
                        qt = (u - 4) // GR
                        outputs(n, qt)
                    if u < NU:
                        qt, hh = u // GR, u % GR
                        w = (qt + 1) * P
                        mask = maskP[:, qt, 0:w] if l == 0 else const[:, K_CAU + SEQ - w:K_CAU + SEQ]
                        dve.wait_ge(S("at_s"), n * NU + (u + 2))
                        if u >= 2:
                            dve.wait_ge(S("at_p"), n * NU + (u - 1))
                        settle(dve)
                        dve.tensor_tensor_reduce(Sm[:, u % 2, 0:w], ps[:, u % 2, 0:w], mask, SCALE, -3e38, ALU.add, ALU.max, mx[:, u:u + 1])\
                            .then_inc(S("at_sm"), 1)
                        dve.wait_ge(S("at_sm"), n * NU + (u + 1))
                        if l == 0:
                            dve.tensor_scalar(nm[:, u:u + 1], mx[:, u:u + 1], -1.0, None, ALU.mult).then_inc(S("at_nm"), 1)
                        else:
                            c = cq[:, qt, ds(g * GR + hh, 1)]
                            dve.tensor_tensor(mx[:, u:u + 1], mx[:, u:u + 1], c, ALU.add).then_inc(S("at_mc"), 1)
                            dve.wait_ge(S("at_mc"), g * NU + (u + 1))
                            dve.tensor_tensor(nm[:, u:u + 1], c, mx[:, u:u + 1], ALU.subtract).then_inc(S("at_nm"), 1)
                    if l == 0 and u < NU:
                        dve.wait_ge(S("tk_step"), n * NU + (u + 1))
                        settle(dve, 1)
                        if u % 2 == 0:
                            dve.max(small[0:NS, 0:8], scs[0:NS, :]).then_inc(S("tk_step"), 1)
                        else:
                            dve.match_replace(scs[0:NS, :], small[0:NS, 0:8], scs[0:NS, :], TAKEN).then_inc(S("tk_step"), 1)
                    if u >= 2 * GR + 3 and (u - 4) % GR == GR - 1:
                        turned_outputs(g, n, (u - 4) // GR - 1)
                    if nxt is not None:
                        if l == 0 and u in (9, 17):
                            rope(n + 1, u // 17)
                        if u == 17:
                            to_place(n + 1)
                turned_outputs(g, n, QT - 1)

            if l == 1:
                for h in range(2):
                    split_low(dve, "q1", 0, 0, h)
            for t in range(2):
                if l == 0:
                    rope(n0, t)
            to_place(n0)
            with dve.Fori(0, NKV - 1) as g:
                units(g, g + n0, g + 1)
            units(NKV - 1, n0 + NKV - 1, None)
            if l == 0:
                assert 4 * NU == 2 * NSEL_S // 8
                dve.wait_ge(S("tk_step"), 1 + 4 * NU)
                dve.tensor_scalar(scs[0:NS, :], scs[0:NS, :], 0.5 * TAKEN, NEG, ALU.is_gt, ALU.mult)

        def pool_attn(pool, l):
            for j in range(2):
                gather(pool, f"K{l}", 0, j, I[f"cache_k_{'ab'[l]}"], j, PC)
            for g in range(NKV):
                n, half = g + l * NKV, 64 * (g % 2)
                pool.wait_ge(S("at_q"), n * 2 + 2 + 1)
                dst = Qall[half:half + 64, g // 2, :].rearrange("p (b h) -> p b h", h=NH)
                for hh in range(GR):
                    ins = pool.tensor_copy(dst[:, :, g * GR + hh], qst[0:HD, hh, SEQ:TOK])
                ins.then_inc(S("at_qall"), 1)
                pool.wait_ge(S("at_qall"), n + 2)
                if g + 1 < NKV:
                    for h in range(2):
                        split_low(pool, f"q{l}", g + 1, 0, h)

        def pe_samp(pe, l):
            for c in range(2):
                if l == 0:
                    pe.matmul(ps[:, 4 + c, :], const[0:NS, K_E16:K_E16 + P], by_token(biasS)[0:NS, 4 * c:4 * c + 4, :], start=True, stop=False)
                else:
                    pe.matmul(ps[:, 4 + c, :], ident, by_token(biasS)[:, 4 * c:4 * c + 4, :], start=True, stop=False)
            with pe.Fori(0, 4) as i:
                for j in range(2):
                    b = i * 2 + j
                    s = panel_ready(pe, f"K{l}", i, j)
                    for c in range(4):
                        pe.wait_ge(S("sp_kt"), 1 + b * 4 + 32 * l)
                        for n in range(4):
                            pg = 4 * (c % 2) + n
                            ins = pe.transpose(ps[:, c, n * P:n * P + P], pages_view(s, PC)[:, pg, (c // 2) * P:(c // 2) * P + P], ident)
                        if c < 3:
                            ins.then_inc(S("sp_ktr"), 1)
                    panel_used(ins, s)
                    pe.wait_ge(S("sp_qz"), b + 1 + 8 * l)
                    for c in range(4):
                        pe.wait_ge(S("sp_kt"), 1 + b * 4 + c + 1 + 32 * l)
                        ins = pe.matmul(ps[:, 4 + c % 2, :], qz[:, j, c // 2, :], KT[:, c, 0:512], start=False, stop=False)
                    ins.then_inc(S("sp_qk"), 1)
            for c in range(2):
                pe.matmul(ps[:, 4 + c, :], zeros, const[:, 0:512], start=False, stop=True)
            for half in range(2):
                ins = pe.matmul(ps[:, 6, 0:NS], Qall[:, half, :], knT[:, half, :], start=(half == 0), stop=(half == 1))
            if l == 0:
                ins = pe.matmul(ps[:, 6, 16:17], const[0:NS, K_E16:K_E16 + P], maskS[0:NS, :], start=True, stop=True)
            ins.then_inc(S("sp_logits"), 1)
            pe.wait_ge(S("sp_pb"), 1 + l)
            for n in range(NPG):
                ins = pe.transpose(ps[:, n // 4, (n % 4) * P:(n % 4) * P + P], Pb[:, n * P:n * P + P], ident)
            pe.transpose(ps[0:NS, 2, 0:P], pnx, ident).then_inc(S("sp_ptr"), 1)
            pe.wait_ge(S("sp_pts"), 2 + 2 * l)
            pe.matmul(ps[:, 7, 0:PC], pnT[0:NS, :], vnew[0:NS, :], start=True, stop=False)
            with pe.Fori(0, 2) as i:
                for j in range(4):
                    s = panel_ready(pe, f"V{l}", i, j)
                    pe.wait_ge(S("sp_pz"), i * 4 + j + 1 + 8 * l)
                    for n in range(NPG):
                        ins = pe.matmul(ps[:, 7, 0:PC], Pz[:, j % 2, n, :], pages_view(s, PC)[:, n, :], start=False, stop=False)
                    ins.then_inc(S("sp_vb"), 1)
                    pe.wait_ge(S("sp_vb"), i * 4 + j + 1 + 8 * l)
                    pe.sem_inc(S(f"ring_free{s}"), 1)
            pe.matmul(ps[:, 7, 0:PC], zeros, const[:, 0:PC], start=False, stop=True).then_inc(S("sp_ov"), 1)
            pe.wait_ge(S("sp_ovs"), 1 + l)
            for half in range(2):
                ins = pe.transpose(ps[:, 6, half * P:half * P + P], ovs[:, half * P:half * P + P], ident)
            ins.then_inc(S("sp_ot"), 1)

        def act_samp(act, l):
            with act.Fori(0, 4) as i:
                for j in range(2):
                    b = i * 2 + j
                    slot, before, _ = fill(f"K{l}", i, j)
                    act.wait_ge(S("sp_qk"), 1 + b + 8 * l)
                    for c in range(4):
                        if c < 3:
                            act.wait_ge(S("sp_ktr"), b * 3 + c + 1 + 24 * l)
                        else:
                            act.wait_ge(S(f"ring_free{slot}"), before + 1)
                        act.activation(KT[:, c, 0:512], ps[:, c, :], ACT.Copy).then_inc(S("sp_kt"), 1)
            act.wait_ge(S("sp_nm"), 1 + l)
            act.activation(Pb.rearrange("p (a c) -> p a c", a=2), ps[:, 4:6, :], ACT.Exp, bias=ssm[:, 2:3], scale=SCALE,
                           accum_out=ssm[:, 3:4]).then_inc(S("sp_e"), 1)
            act.activation(ssm[:, 4:5], ssm[:, 0:1], ACT.Exp, bias=ssm[:, 2:3], scale=SCALE).then_inc(S("sp_e"), 1)
            act.wait_ge(S("sp_ptr"), 1 + l)
            act.activation(PTs.rearrange("p (a j) c -> p a (j c)", a=2), ps[:, 0:2, :], ACT.Copy).then_inc(S("sp_pts"), 1)
            act.activation(pnT[0:NS, :], ps[0:NS, 2, 0:P], ACT.Copy).then_inc(S("sp_pts"), 1)
            for h in range(2):
                act.activation(hH[:, HK * h:HK * h + HK, 0:SEQ], OT[:, HK * h:HK * h + HK, 0:SEQ], ACT.Copy).then_inc(S("o_hi"), 1)

        def pool_samp(pool, l):
            K, V = (I[f"cache_{x}_{'ab'[l]}"] for x in "kv")
            in_turn(pool, pool.memset(colmask[:, :, :], 0.0))
            for b in range(NS):
                ins = pool.memset(colmask[:, b, b * NH:b * NH + NH], 1.0)
            in_turn(pool, ins)

            def zeroed(i):
                for j in range(2):
                    pool.wait_ge(S("sp_qk"), 1 + i * 2 + 8 * l)
                    for half in range(2):
                        ins = pool.tensor_tensor(qz[:, j, half, :], Qall[:, half, :],
                                                 colmask[:, ds(i * 2 + j, 1), :].rearrange("p o c -> p (o c)"), ALU.mult)
                    ins.then_inc(S("sp_qz"), 1)

            for j in range(2):
                gather(pool, f"V{l}", 0, j, V, j, PC)
            for i in range(3):
                zeroed(i)
                for j in range(2):
                    gather(pool, f"K{l}", i + 1, j, K, (i + 1) * 2 + j, PC)
            zeroed(3)
            for b in range(2, NS):
                gather(pool, f"V{l}", b // 4, b % 4, V, b, PC)

        def o_low(dve, l, n, cols):
            k = slice(0, KC) if n == 2 else slice(HK * n, HK * n + HK)
            dve.wait_ge(S("o_hi"), 3 * l + n + 1)
            dve.tensor_tensor(hL[:, k, cols], OT[:, k, cols], hH[:, k, cols].bitcast(F32), ALU.subtract).then_inc(S("o_lo"), 1)

        def dve_samp(dve, l):
            ch = Chain(dve)
            dve.wait_ge(S("sp_logits"), 1 + l)
            ch.link(dve.tensor_tensor_reduce(ssm[:, 8:16], ps[:, 6, 0:NS], diag16, 1.0, 0.0, ALU.mult, ALU.add, ssm[:, 0:1]))
            if l == 0:
                ch.link(dve.tensor_tensor(ssm[:, 0:1], ssm[:, 0:1], ps[:, 6, 16:17], ALU.add))
            ch.link(dve.tensor_reduce(ssm[:, 1:2], ps[:, 4:6, :], AX.XY, ALU.max))
            ch.link(dve.tensor_tensor(ssm[:, 1:2], ssm[:, 1:2], ssm[:, 0:1], ALU.max))
            dve.tensor_scalar(ssm[:, 2:3], ssm[:, 1:2], -SCALE, None, ALU.mult).then_inc(S("sp_nm"), 1)
            dve.wait_ge(S("sp_e"), 2 + 2 * l)
            ch.link(dve.tensor_tensor(ssm[:, 3:4], ssm[:, 3:4], ssm[:, 4:5], ALU.add))
            ch.link(dve.reciprocal(ssm[:, 5:6], ssm[:, 3:4]))
            ch.link(dve.tensor_tensor(ssm[:, 4:5], ssm[:, 4:5], ssm[:, 5:6], ALU.mult))
            dve.tensor_scalar(pnx, diag16, ssm[:, 4:5], None, ALU.mult)
            dve.tensor_scalar(Pb, Pb, ssm[:, 5:6], None, ALU.mult).then_inc(S("sp_pb"), 1)
            dve.wait_ge(S("sp_pts"), 2 + 2 * l)
            for b in range(NS):
                if b >= 2:
                    dve.wait_ge(S("sp_vb"), b - 1 + 8 * l)
                dve.tensor_tensor(Pz[:, b % 2, :, :], PTs, colmask[:, b:b + 1, :].to_broadcast([P, NPG, P]), ALU.mult)\
                    .then_inc(S("sp_pz"), 1)
                if b in (3, 5):
                    o_low(dve, l, (b - 3) // 2, slice(0, SEQ))
            dve.wait_ge(S("sp_ov"), 1 + l)
            dve.tensor_copy(ovs, ps[:, 7, 0:PC]).then_inc(S("sp_ovs"), 1)
            dve.wait_ge(S("sp_ot"), 1 + l)
            o = ps[:, 6, 0:2 * P].rearrange("p (a b h) -> p a h b", a=2, h=NH)
            for half in range(2):
                for lo in range(2):
                    for odd in range(2):
                        h0 = 8 * half + 4 * lo + odd
                        dve.tensor_copy(OT[64 * odd:64 * odd + 64, 4 * half + 2 * lo:4 * half + 2 * lo + 2, SEQ:TOK],
                                        o[64 * lo:64 * lo + 64, half, h0:h0 + 3:2, :])

        def residual(dve, ch, l, chunk, m, p):
            row, x = ada[:, l * NADA + chunk * KC + m, :], xT[:, m, :]
            dve.scalar_tensor_tensor(out=x[:, 0:HT], in0=ps[:, 2 * p, 0:HT], scalar=row[:, 0:1], in1=x[:, 0:HT], op0=ALU.mult, op1=ALU.add)
            dve.scalar_tensor_tensor(out=x[:, HT:SEQ], in0=ps[:, 2 * p + 1, 0:SEQ - HT], scalar=row[:, 0:1], in1=x[:, HT:SEQ],
                                     op0=ALU.mult, op1=ALU.add)
            ch(dve.tensor_tensor(tmp8[:, :], ps[:, 2 * p + 1, SEQ - HT:HT], row[:, 1:CC], ALU.mult))
            return dve.tensor_tensor(x[:, SEQ:TOK], x[:, SEQ:TOK], tmp8[:, :], ALU.add)

        def pe_out(pe, l):
            for j in range(4):
                for h in range(2):
                    half_ready(pe, f"o{l}", 0, j, h)
                    if j == 0:
                        pe.wait_ge(S("o_lo"), 3 * l + 3)
                    if j >= 2 and h == 0:
                        pe.wait_ge(S(f"o{l}_res"), 2 * j - 2)
                    if j == 3 and h == 1:
                        pe_rms(pe, 2 * l + 1, range(HK))
                    mm_half(pe, h, (2 * j % 4, 2 * j % 4 + 1), HK * h, HK, h == 0, h == 1)

        def act_out(act, l):
            act.activation(hH[:, :, SEQ:TOK], OT[:, :, SEQ:TOK], ACT.Copy).then_inc(S("o_hi"), 1)
            for j in range(4):
                for h in range(2):
                    split_high(act, f"o{l}", 0, j, h)

        def dve_out(dve, l):
            ch = Chain(dve)
            o_low(dve, l, 2, slice(SEQ, TOK))
            for j in range(5):
                if j < 4:
                    for h in range(2):
                        split_low(dve, f"o{l}", 0, j, h)
                if j >= 1:
                    dve.wait_ge(S("w_used"), used(f"o{l}", 0, j - 1))
                    for m in (2 * j - 2, 2 * j - 1):
                        residual(dve, ch.link, l, 2, m, m % 4).then_inc(S(f"o{l}_res"), 1)
                        dve.wait_ge(S(f"o{l}_res"), m + 1)

        def pe_up(pe, l):
            tag = f"up{l}"

            def two(sec, i, q, k, wait=None):
                pe.wait_ge(S("up_afree"), k * 2 + (l * FC + 2))
                mm_panel(pe, sec, i, 2 * q, (0, 2), wait)
                pe.wait_ge(S("up_bfree"), k * 2 + (l * FC + 2))
                mm_panel(pe, sec, i, 2 * q + 1, (1, 3))

            two(f"{tag}h", 0, 0, 0, split_input(pe, 2 * l + 1))
            with pe.Fori(0, 5) as i:
                for q in range(2):
                    two(tag, i, q, i * 2 + (1 + q))
            pe.wait_ge(S("up_acv"), 2 + l * FC + FC)
            pe.wait_ge(S("up_bfree"), l * FC + FC + 2)
            pe.wait_ge(S("up_afree"), l * FC + FC + 2)
            for q in range(NCV):
                if q >= 2:
                    pe.wait_ge(S("up_cvo"), l * NCV + q - 1)
                for n in range(min(4, FC - 4 * q)):
                    ins = pe.transpose(ps[0:10, 6 + q % 2, n * P:n * P + P], acv[:, 4 * q + n, :], ident)
                ins.then_inc(S("up_cvt"), 1)

        def act_up(act, l):
            tag = f"up{l}"

            def out(f, t):
                fr = ds(f, 1)
                act.wait_ge(S("up_c3"), f + (1 + l * FC))
                act.wait_ge(S("up_acv"), f + (1 + l * FC))
                act.wait_ge(S("up_bfree"), f + (l * FC + 1))
                act.activation(v520(aS[:, t, 2:2 + TOK]), pair(2 * t), ACT.Copy).then_inc(S("up_afree"), 1)
                act.wait_ge(S("up_afree"), f + (l * FC + 3))
                cw = cwT[:, fr, :].rearrange("p o c -> p (o c)")
                act.activation(cvA[:, t, 0:SEQ], aS[:, t, 0:SEQ], ACT.Identity, scale=cw[:, 20 * l + 16:20 * l + 17],
                               bias=cw[:, 20 * l + 19:20 * l + 20]).then_inc(S("up_c1"), 1)

            def silu(f, t):
                act.wait_ge(S("up_c3"), f + (3 + l * FC))
                act.activation(cvA[:, t, :], cvA[:, t, :], ACT.Silu).then_inc(S("up_silu"), 1)

            def two(sec, i, q, k, nxt):
                for h in range(2):
                    split_high(act, sec, i, 2 * q + 1, h)
                act.wait_ge(S("w_used"), used(sec, i, 2 * q))
                for t in range(2):
                    out(k * 2 + t, t)
                split_high(act, *nxt, 0)
                for t in range(2):
                    silu(k * 2 + t, t)
                split_high(act, *nxt, 1)

            two(f"{tag}h", 0, 0, 0, (tag, 0, 0))
            with act.Fori(0, 5) as i:
                two(tag, i, 0, i * 2 + 1, (tag, i, 2))
                two(tag, i, 1, i * 2 + 2, (tag, i + 1, 0))
            act_group(act, l, 0, 0, 0)
            for q in range(NCV):
                n = min(4, FC - 4 * q)
                act.wait_ge(S("up_cvt"), l * NCV + q + 1)
                act.activation(cvrow[0:10, 4 * q * P:(4 * q + n) * P], ps[0:10, 6 + q % 2, 0:n * P], ACT.Copy).then_inc(S("up_cvo"), 1)
            act.wait_ge(S("up_cvo"), l * NCV + NCV)
            act.dma_start(O["conv_p"][l], cvrow[0:2, :]).then_inc(S("stores"), 16)
            act.dma_start(O["conv_s"][l, :, 1, :], cvrow[2:10, :]).then_inc(S("stores"), 16)
            act.dma_start(O["conv_s"][l, :, 0, :], I["state_conv"][l, :, 1, :]).then_inc(S("stores"), 16)

        def dve_up(dve, l):
            tag = f"up{l}"

            def conv(f, t):
                fr = ds(f, 1)
                cw = cwT[:, fr, :].rearrange("p o c -> p (o c)")
                w1, w2 = cw[:, 20 * l + 17:20 * l + 18], cw[:, 20 * l + 18:20 * l + 19]
                dve.wait_ge(S("up_c1"), l * FC + f + 1)
                dve.scalar_tensor_tensor(out=cvA[:, t, 0:SEQ], in0=aS[:, t, 1:SEQ + 1], scalar=w1, in1=cvA[:, t, 0:SEQ],
                                         op0=ALU.mult, op1=ALU.add).then_inc(S("up_c2"), 1)
                dve.scalar_tensor_tensor(out=cvA[:, t, SEQ:TOK], in0=aS[:, t, SEQ + 2:TOK + 2], scalar=w2,
                                         in1=cs0[:, l, fr, :].rearrange("p o c -> p (o c)"), op0=ALU.mult, op1=ALU.add)
                dve.wait_ge(S("up_c2"), l * FC + f + 1)
                dve.scalar_tensor_tensor(out=cvA[:, t, 0:SEQ], in0=aS[:, t, 2:SEQ + 2], scalar=w2, in1=cvA[:, t, 0:SEQ],
                                         op0=ALU.mult, op1=ALU.add).then_inc(S("up_c3"), 1)

            def gates(done, k):
                dve.wait_ge(S("w_used"), done)
                for t in range(2):
                    f = k * 2 + t
                    dve.wait_ge(S("up_silu"), l * FC + f + 1)
                    dve.tensor_tensor(v520(gT[:, ds(f, 1), :].rearrange("p o t -> p (o t)")), pair(2 * t + 1), v520(cvA[:, t, :]), ALU.mult)\
                        .then_inc(S("up_bfree"), 1)

            def lows(sec, i, j):
                for h in range(2):
                    split_low(dve, sec, i, j, h)

            def two(sec, i, q, k, nxt):
                lows(sec, i, 2 * q + 1)
                for t in range(2):
                    conv(k * 2 + t, t)
                lows(*nxt)
                gates(used(sec, i, 2 * q + 1), k)

            two(f"{tag}h", 0, 0, 0, (tag, 0, 0))
            with dve.Fori(0, 5) as i:
                two(tag, i, 0, i * 2 + 1, (tag, i, 2))
                two(tag, i, 1, i * 2 + 2, (tag, i + 1, 0))

        def pool_up(pool, l):
            tag = f"up{l}"

            def tile(f, t):
                pool.wait_ge(S("up_c1"), l * FC + f + 1)
                pool.tensor_copy(acv[:, ds(f, 1), :].rearrange("p o c -> p (o c)"), aS[:, t, SEQ:SEQ + 10]).then_inc(S("up_acv"), 1)

            with pool.Fori(0, 5) as i:
                for q in range(4):
                    tile(i * 4 + q, q % 2)
            for q in range(2):
                tile(20 + q, q)

        def halves_of(n):
            return [(h, min(HK, GROUPS[n][1] - HK * h)) for h in range(2)]

        def pe_down(pe, l):
            tag = f"dn{l}"
            for i in range(2):
                for n in range(len(GROUPS)):
                    for q in range(2):
                        if n == 0:
                            pe.wait_ge(S(f"{tag}_free"), i * 4 + (2 * q + 2))
                        if n == 0 and q == 1:
                            pe.wait_ge(S("up_cvo"), (l + 1) * NCV)
                        for h, nk in halves_of(n):
                            half_ready(pe, tag, i, 2 * n + q, h)
                            if q == 0:
                                pe.wait_ge(S("g_lo"), i * 6 + (12 * l + 2 * n + h + 1))
                            if (i, n, q, h) == (1, 2, 1, 1):
                                pe_rms(pe, 2 * l + 2, range(HK))
                            mm_half(pe, h, (2 * q, 2 * q + 1), HK * h, nk, n == 0 and h == 0, n == 2 and h == 1)

        def act_group(act, l, i, n, h):
            g0, nk = GROUPS[n][0] + HK * h, halves_of(n)[h][1]
            if i == 0:
                act.wait_ge(S("up_bfree"), l * FC + 2 + g0 + nk)
            act.activation(hH[:, HK * h:HK * h + nk, :], gT[:, g0:g0 + nk, :], ACT.Copy).then_inc(S("g_hi"), 1)

        def dve_group(dve, l, i, n, h):
            g0, nk = GROUPS[n][0] + HK * h, halves_of(n)[h][1]
            dve.wait_ge(S("g_hi"), (2 * l + i) * 6 + 2 * n + h + 1)
            dve.tensor_tensor(hL[:, HK * h:HK * h + nk, :], gT[:, g0:g0 + nk, :], hH[:, HK * h:HK * h + nk, :].bitcast(F32), ALU.subtract)\
                .then_inc(S("g_lo"), 1)

        def act_down(act, l):
            tag = f"dn{l}"
            for i in range(2):
                for n in range(len(GROUPS)):
                    for q in range(2):
                        for h, nk in halves_of(n):
                            if (i, n, q) > (0, 0, 0):
                                split_high(act, tag, i, 2 * n + q, h, nk)
                            if q == 0 and (i, n, h) > (0, 0, 0):
                                act_group(act, l, i, n, h)

        def dve_down(dve, l):
            tag = f"dn{l}"
            dve_group(dve, l, 0, 0, 0)

            def sums(i, q):
                dve.wait_ge(S("w_used"), used(tag, i, 4 + q))
                for t in range(2):
                    m = i * 4 + q * 2 + t

                    def link(ins, m=m):
                        ins.then_inc(S(f"{tag}_dve"), 1)
                        dve.wait_ge(S(f"{tag}_dve"), m + 1)
                    residual(dve, link, l, 5, m, 2 * q + t).then_inc(S(f"{tag}_free"), 1)
                    dve.wait_ge(S(f"{tag}_free"), m + 5)

            for i in range(2):
                for n in range(len(GROUPS)):
                    for q in range(2):
                        for h, nk in halves_of(n):
                            if (i, n, q) > (0, 0, 0):
                                split_low(dve, tag, i, 2 * n + q, h, nk)
                            if q == 0 and (i, n, h) > (0, 0, 0):
                                dve_group(dve, l, i, n, h)
                            if i == 1 and n == q == h == 0:
                                sums(0, 1)
                sums(i, 0)
            sums(1, 1)

        FIN_GROUPS = 2 * QT + 2

        @block.tensor
        def _(pe):
            pe.wait_ge(S("in_const"), 16)
            pe.wait_ge(S("in_vec"), 96)
            for kc in range(KC):
                pe.transpose(ps[:, 0, kc * CC:kc * CC + CC], cload[0:CC, kc * P:kc * P + P], ident[0:CC, 0:CC])
            pe.transpose(ps[:, 1, 0:96], vrow[0:96, :], ident[0:96, 0:96])
            pe.transpose(ps[:, 1, 96:136], vrow2[0:40, :], ident[0:40, 0:40]).then_inc(S("pr_vec"), 1)
            pe.wait_ge(S("in_x"), 32)
            for kc in range(KC):
                if kc >= 2:
                    pe.wait_ge(S("pr_xe"), 2 * (kc - 1))
                b = 2 + 2 * (kc % 2)
                for t in range(QT):
                    pe.transpose(ps[:, b, t * P:t * P + P], xload[:, t, kc * P:kc * P + P], ident)
                pe.transpose(ps[:, b + 1, 0:NS], xsload[0:NS, kc * P:kc * P + P], ident[0:NS, 0:NS]).then_inc(S("pr_x"), 1)
            pe.wait_ge(S("in_conv"), 96)
            for f in range(FC):
                ins = pe.transpose(ps[:, 6 + f // 11, (f % 11) * 40:(f % 11) * 40 + 40], crow[0:40, f * P:f * P + P], ident[0:40, 0:40])
            ins.then_inc(S("pr_cw"), 1)
            pe.wait_ge(S("pr_tab"), 1)
            pe.matmul(ps[:, 1, 256:256 + NS], const[0:NPG, K_E16:K_E16 + P], tablef[:, :], start=True, stop=True).then_inc(S("pr_pages"), 1)
            phase_end(pe, "pe")
            pe_rms(pe, 0)
            pe.wait_ge(S("rms_rt"), 1)
            pe_ada(pe, "ada0a", 2, 0)
            phase_end(pe, "pe")
            for l in range(DEPTH):
                if l == 1:
                    pe.wait_ge(S("rms_rt"), 3)
                    pe.wait_ge(S("dn0_free"), 4 + KC)
                    pe_ada(pe, "ada1", 6, 24)
                    phase_end(pe, "pe")
                pe_head(pe, l)
                phase_end(pe, "pe")
                if l == 0:
                    pe_score(pe)
                    phase_end(pe, "pe")
                    pe_ada(pe, "ada0b", 4, 8)
                else:
                    pe_logf(pe)
                phase_end(pe, "pe")
                pe_attn(pe, l)
                phase_end(pe, "pe")
                pe_samp(pe, l)
                phase_end(pe, "pe")
                pe_out(pe, l)
                pe_rms(pe, 2 * l + 1, range(HK, KC))
                pe_up(pe, l)
                pe_down(pe, l)
                pe_rms(pe, 2 * l + 2, range(HK, KC))
            phase_end(pe, "pe")
            for n in range(FIN_GROUPS):
                t, half = n // 2, n % 2
                if n >= 4:
                    pe.wait_ge(S("fi_y"), n - 3)
                for k in range(4):
                    if t < QT:
                        ins = pe.transpose(ps[:, n % 4, k * P:k * P + P], hT[:, 4 * half + k, t * P:t * P + P], ident)
                    else:
                        ins = pe.transpose(ps[0:NS, n % 4, k * P:k * P + P], hT[:, 4 * half + k, SEQ:TOK], ident)
                ins.then_inc(S("fi_t"), 1)
            phase_end(pe, "pe")

        @block.scalar
        def _(act):
            act.dma_start(xload, I["x_prompt"][0].rearrange("(t p) d -> p t d", p=P)).then_inc(S("in_x"), 16)
            act.dma_start(xsload[0:NS, :], I["x_sample"].rearrange("b o d -> (b o) d")).then_inc(S("in_x"), 16)
            for l in range(DEPTH):
                act.dma_start(crow[20 * l:20 * l + 16, :], I["state_conv"][l].rearrange("b w f -> (b w) f")).then_inc(S("in_conv"), 16)
                act.dma_start(crow[20 * l + 16:20 * l + 19, :], I["conv_w"][l]).then_inc(S("in_conv"), 16)
                act.dma_start(crow[20 * l + 19:20 * l + 20, :], I["conv_b"][l:l + 1, :]).then_inc(S("in_conv"), 16)
            act.dma_start(table[:, :], I["page_table"].rearrange("b j -> j b"), allow_slow_non_contiguous=True).then_inc(S("in_table"), 16)
            act.dma_start(bfb[:, :], I["b_f"].partition_broadcast(P)).then_inc(S("in_bf"), 16)
            act.wait_ge(S("pr_vec"), 1)
            act.activation(cT[:, :, :], ps[:, 0, 0:KC * CC].rearrange("p (k c) -> p k c", k=KC), ACT.Silu).then_inc(S("pr_silu"), 1)
            act.activation(badaT[:, :], ps[:, 1, 0:96], ACT.Copy)
            act.wait_ge(S("pr_c2z"), 1)
            act.wait_ge(S("pr_silu"), 1)
            act.activation(c2[:, :, 0:CC], cT[:, :, :], ACT.Copy).then_inc(S("pr_chi"), 1)
            act.activation(vT[:, :], ps[:, 1, 96:136], ACT.Copy)
            for kc in range(KC):
                act.wait_ge(S("pr_x"), kc + 1)
                act.activation(xT[:, kc, 0:SEQ], ps[:, 2 + 2 * (kc % 2), :], ACT.Copy).then_inc(S("pr_xe"), 1)
                act.activation(xT[:, kc, SEQ:TOK], ps[:, 3 + 2 * (kc % 2), 0:NS], ACT.Copy).then_inc(S("pr_xe"), 1)
            act.wait_ge(S("pr_cw"), 1)
            for h in range(2):
                act.activation(cwT[:, 11 * h:11 * h + 11, :], ps[:, 6 + h, 0:440].rearrange("p (k c) -> p k c", k=11), ACT.Copy)\
                    .then_inc(S("pr_cwe"), 1)
            phase_end(act, "act")
            act_rms(act, 0)
            act_ada(act, "ada0a", 2, 0, 0)
            phase_end(act, "act")
            for l in range(DEPTH):
                base = l * NADA
                if l == 1:
                    act_ada(act, "ada1", 6, NADA, 24)
                    phase_end(act, "act")
                act_mod(act, 2 * l, ada[:, base:base + KC, :])
                act_head(act, l)
                phase_end(act, "act")
                if l == 0:
                    act_score(act)
                    phase_end(act, "act")
                    act_ada(act, "ada0b", 4, 2 * KC, 8)
                else:
                    act_logf(act)
                phase_end(act, "act")
                act_attn(act, l)
                phase_end(act, "act")
                act_samp(act, l)
                phase_end(act, "act")
                act_out(act, l)
                act_rms(act, 2 * l + 1)
                act_mod(act, 2 * l + 1, ada[:, base + 3 * KC:base + 4 * KC, :])
                act_up(act, l)
                act_down(act, l)
                act.wait_ge(S("stores"), 16 * STORES[2 * l + 1])
                act_rms(act, 2 * l + 2)
            for kc in range(KC):
                act.wait_ge(S("rms_t"), 4 * KC + kc + 1)
                act.activation(hT[:, kc, :], hT[:, kc, :], ACT.Identity, scale=vT[:, 32 + kc:33 + kc])
            phase_end(act, "act")
            for n in range(FIN_GROUPS):
                t, half = n // 2, n % 2
                act.wait_ge(S("fi_t"), n + 1)
                if t < QT:
                    if t >= 2 and half == 0:
                        act.wait_ge(S(f"fi_out{t % 2}"), 16 * (t // 2))
                    act.activation(ytok[:, t % 2, half * 512:half * 512 + 512], ps[:, n % 4, :], ACT.Copy).then_inc(S("fi_y"), 1)
                    if half == 1:
                        act.wait_ge(S("fi_y"), n + 1)
                        act.dma_start(O["y_p"][t * P:t * P + P, :], ytok[:, t % 2, :]).then_inc(S(f"fi_out{t % 2}"), 16)
                else:
                    act.activation(ysam[0:NS, half * 512:half * 512 + 512], ps[0:NS, n % 4, :], ACT.Copy).then_inc(S("fi_y"), 1)
            act.wait_ge(S("fi_y"), FIN_GROUPS)
            act.dma_start(O["y_s"], ysam[0:NS, :]).then_inc(S("stores"), 16)
            act.wait_ge(S("fi_out0"), 32)
            act.wait_ge(S("fi_out1"), 32)
            act.wait_ge(S("stores"), 16 * STORES[4])
            phase_end(act, "act")

        @block.vector
        def _(dve):
            ch = Chain(dve)
            dve.memset(epsc[:, :], EPS)
            dve.memset(ones[:, :], 1.0)
            ch.link(dve.memset(zeros[:, :], 0.0))
            for n in range(2):
                ins = dve.tensor_copy(c2[:, :, n * (CC + 1):n * (CC + 1) + CC + 1], zeros[:, 0:KC * (CC + 1)].rearrange("p (k c) -> p k c", k=KC))
            ins.then_inc(S("pr_c2z"), 1)
            dve.wait_ge(S("in_table"), 16)
            dve.tensor_copy(tablef[:, :], table[:, :]).then_inc(S("pr_tab"), 1)
            dve.wait_ge(S("pr_pages"), 1)
            dve.tensor_scalar(idx[:, :], ps[:, 1, 256:256 + NS], 16.0, const[:, K_B16:K_B16 + 1], ALU.mult, ALU.add)
            dve.wait_ge(S("pr_chi"), 1)
            dve.tensor_tensor(c2[:, :, CC + 1:CC + 1 + CC], cT[:, :, :], c2[:, :, 0:CC].bitcast(F32), ALU.subtract)
            dve.wait_ge(S("pr_cwe"), 2)
            for l in range(DEPTH):
                c = cwT[:, :, 20 * l:20 * l + 20]
                st0, st1 = c[:, :, 0:16:2], c[:, :, 1:16:2]

                def tap(n, c=c):
                    return c[:, :, n:n + 1].to_broadcast([P, FC, NS])
                u = sq[:, 0, 0:FC * NS].rearrange("p (k c) -> p k c", k=FC)
                ch.link(dve.tensor_tensor(cs0[:, l, :, :], st0, tap(16), ALU.mult))
                ch.link(dve.tensor_tensor(u, st1, tap(17), ALU.mult))
                ch.link(dve.tensor_tensor(cs0[:, l, :, :], cs0[:, l, :, :], u, ALU.add))
                ch.link(dve.tensor_tensor(cs0[:, l, :, :], cs0[:, l, :, :], tap(19), ALU.add))
            phase_end(dve, "dve")
            dve_rms(dve, 0)
            low_ada(dve, "ada0a", 2)
            phase_end(dve, "dve")
            for l in range(DEPTH):
                base = l * NADA
                if l == 1:
                    low_ada(dve, "ada1", 6)
                    phase_end(dve, "dve")
                dve_gain(dve, ada[:, base + KC:base + 2 * KC, :], vT[:, 8 * l:8 * l + 8])
                dve_mod(dve, 2 * l)
                if l == 1:
                    dve.wait_ge(S("in_bf"), 16)
                dve_head(dve, l)
                phase_end(dve, "dve")
                if l == 0:
                    dve_score(dve)
                    phase_end(dve, "dve")
                    dve_topk(dve)
                else:
                    dve_logf(dve)
                phase_end(dve, "dve")
                dve_attn(dve, l)
                phase_end(dve, "dve")
                dve_samp(dve, l)
                phase_end(dve, "dve")
                dve_out(dve, l)
                dve_gain(dve, ada[:, base + 4 * KC:base + 5 * KC, :], vT[:, 16 + 8 * l:24 + 8 * l])
                dve_rms(dve, 2 * l + 1)
                dve_mod(dve, 2 * l + 1)
                dve_up(dve, l)
                dve_down(dve, l)
                dve_rms(dve, 2 * l + 2)
            for kc in range(KC):
                normed(dve, kc)
            phase_end(dve, "dve")
            phase_end(dve, "dve")

        @block.gpsimd
        def _(pool):
            for name in CREDITED:
                pool.sem_inc(S(name), 1)
            pool.memset(colmask8[:, :, :], 0.0).then_inc(S("pl_z"), 1)
            pool.wait_ge(S("pl_z"), 1)
            for b in range(NS):
                pool.memset(colmask8[:, b, b * NIH:b * NIH + NIH], 1.0)
            phase_end(pool, "pool")
            pool_normed(pool, 0)
            phase_end(pool, "pool")
            for l in range(DEPTH):
                base = l * NADA
                if l == 1:
                    pool_normed(pool, 2)
                    phase_end(pool, "pool")
                in_turn(pool, pool.memset(Qall[:, :, :], 0.0))
                if l == 1:
                    in_turn(pool, pool.memset(lf[:, :, :], 0.0))
                else:
                    in_turn(pool, pool.memset(kaug[64:68, :, 0:SEQ], 0.0))
                pool.dma_start(qst[HD:HD + GR, :, 0:SEQ], I["hsel"]).then_inc(S("in_hsel"), 16)
                pool.wait_ge(S("in_hsel"), 16 * (l + 1))
                pool_mod(pool, 2 * l, ada[:, base:base + KC, :])
                pool_head(pool, l)
                if l == 1:
                    slot_free(pool, "logf", 0, 0)
                    for b in range(NS):
                        gather_logf(pool, b)
                phase_end(pool, "pool")
                if l == 0:
                    pool_score(pool)
                    phase_end(pool, "pool")
                    low_even(pool, "ada0b", 4)
                phase_end(pool, "pool")
                pool_attn(pool, l)
                phase_end(pool, "pool")
                pool_samp(pool, l)
                phase_end(pool, "pool")
                for t in range(2):
                    pool.memset(aS[:, t, 0:2], 0.0)
                pool_mod(pool, 2 * l + 1, ada[:, base + 3 * KC:base + 4 * KC, :])
                pool_up(pool, l)
            phase_end(pool, "pool")
            phase_end(pool, "pool")


def _constants():
    f = np.float32
    c = np.zeros((P, K_N), f)
    c[:, K_ID:K_ID + P] = np.eye(P, dtype=f)
    half = HD // 4 // 2
    pos = np.concatenate([np.arange(SEQ), np.full(NS, PAST)]).astype(f)
    inv = (f(500000.0) ** (-np.arange(half, dtype=f) / f(half))).astype(f)
    ang = (pos[None, :] * inv[:, None]).astype(f)
    c[:, K_COS:K_COS + TOK] = 1.0
    for p in range(P):
        d = p % HD
        if d < 2 * half:
            c[p, K_ROT + (p ^ half)] = 1.0
            c[p, K_COS:K_COS + TOK] = np.cos(ang[d % half])
            c[p, K_SIN:K_SIN + TOK] = np.sin(ang[d % half]) * (-1.0 if d < half else 1.0)
    p = np.arange(P)[:, None]
    c[:, K_TRI:K_TRI + 896] = p <= np.arange(896)[None, :] - 384
    c[:, K_CAU:K_CAU + 512] = np.where(np.arange(512)[None, :] - 384 <= p, 0.0, NEG)
    c[:, K_D16:K_D16 + 8] = p // 16 == np.arange(8)[None, :]
    c[:, K_D8:K_D8 + 8] = p // 8 == np.arange(8)[None, :]
    c[:, K_E16:K_E16 + 128] = p == np.arange(128)[None, :] // 16
    c[:, K_E8:K_E8 + 64] = p == np.arange(64)[None, :] // 8
    c[:, K_B16] = np.arange(P) % 16
    c[0:CP, K_SUM:K_SUM + CC] = np.arange(CP)[:, None] % (CC + 1) == np.arange(CC)[None, :]
    hsel = np.zeros((GR, GR, SEQ), f)
    hsel[np.arange(GR), np.arange(GR), :] = 1.0
    return c, hsel


_POOL_PAGES = None
_INS = ["x_prompt", "x_sample", "cache_k_a", "cache_v_a", "cache_kidx_a", "cache_k_b", "cache_v_b", "cache_logf_b",
        "state_conv", "page_table", "c_prompt", "c_sample", "w_ada", "b_ada", "g_mix", "g_ffn", "w_in_a", "w_o_a",
        "w_in_b", "b_f", "w_o_b", "w_up", "conv_w", "conv_b", "w_down", "g_final"]
_OUTS = [("y_p", (SEQ, D), (1, SEQ, D)), ("y_s", (NS, D), (NS, 1, D)),
         ("k_a_p", (SEQ, PC), (1, 1, SEQ, NKV, HD)), ("v_a_p", (SEQ, PC), (1, 1, SEQ, NKV, HD)),
         ("kidx_p", (SEQ, HD), (1, 1, SEQ, HD)),
         ("k_b_p", (SEQ, PC), (1, 1, SEQ, NKV, HD)), ("v_b_p", (SEQ, PC), (1, 1, SEQ, NKV, HD)),
         ("logf_p", (SEQ, NH), (1, 1, SEQ, NH)), ("conv_p", (DEPTH, CW - 1, FF), (DEPTH, 1, CW - 1, FF)),
         ("k_a_s", (NS, PC), (1, NS, 1, NKV, HD)), ("v_a_s", (NS, PC), (1, NS, 1, NKV, HD)),
         ("kidx_s", (NS, HD), (1, NS, 1, HD)),
         ("k_b_s", (NS, PC), (1, NS, 1, NKV, HD)), ("v_b_s", (NS, PC), (1, NS, 1, NKV, HD)),
         ("logf_s", (NS, NH), (1, NS, 1, NH)), ("conv_s", (DEPTH, NS, CW - 1, FF), (DEPTH, NS, CW - 1, FF))]


def kernel(**inputs):
    import concourse.bacc as _bacc
    from concourse.bass_utils import run_bass_kernel_spmd as _run

    nc = _bacc.Bacc("TRN2", target_bir_lowering=False, num_devices=1)
    arrays, I, O = {}, {}, {}

    def give(name, a):
        a = np.ascontiguousarray(a)
        arrays[f"in_{name}"] = a
        I[name] = nc.dram_tensor(f"in_{name}", a.shape, mybir.dt.from_np(a.dtype), kind="ExternalInput").ap()

    for name in _INS:
        a = np.asarray(inputs[name])
        if name.startswith("cache"):
            a = a.reshape(a.shape[1], PAGE, -1)
        give(name, a)
    const, hsel = _constants()
    give("const", const)
    give("hsel", hsel)
    for name, shape, _ in _OUTS:
        O[name] = nc.dram_tensor(f"out_{name}", shape, F32, kind="ExternalOutput").ap()
    build(nc, I, O)
    r = _run(nc, [arrays], core_ids=[0])
    return tuple(r.results[0][f"out_{name}"].reshape(full) for name, _, full in _OUTS)
```
